# Optimizing a Trainium2 kernel written in Bass

```python
import numpy as np
import jax
import jax.numpy as jnp
from jax import lax

D_MODEL = 1024
BATCH = 1
SEQ = 512
DEPTH = 2
DEC_BATCH = 8
DEC_SEQ = 4
PAST_LEN = 4096
PAGE_SIZE = 128

HEAD_DIM = 64
GROUP_W = D_MODEL // 4
N_GH = GROUP_W // HEAD_DIM
D_MIX = 4 * GROUP_W
N_MEM = 256
XA_HEADS = 4
XA_HEAD_DIM = D_MODEL // XA_HEADS
D_FF = 4 * D_MODEL
CONV_W = 4
RGLRU_C = 8.0
RW_DECAY_RANK = D_MODEL // 16
RW_A_RANK = D_MODEL // 16
RW_GATE_RANK = D_MODEL // 8
RWKV_W = 3 * GROUP_W + RW_DECAY_RANK + RW_A_RANK + RW_GATE_RANK
MLSTM_W = 4 * GROUP_W + 2 * N_GH
RET_W = 4 * GROUP_W
RGLRU_W = 2 * GROUP_W
N_IN = MLSTM_W + RET_W + RGLRU_W + RWKV_W
CHUNK = 64
ROPE_BASE = 10000.0
ALPHA = (2.0 * DEPTH) ** 0.25
BETA = (8.0 * DEPTH) ** -0.25
LN_EPS = 1e-5
HEAD_EPS = 1e-6
RWKV_GN_EPS = 64e-5

kernel_name = 'hymba_mlstm_retnet_rglru_rwkv7_decoder_step'

F32 = jnp.float32

def _layer_norm(x, g, b):
    xf = x.astype(F32)
    mu = jnp.mean(xf, -1, keepdims=True)
    var = jnp.mean(jnp.square(xf - mu), -1, keepdims=True)
    return ((xf - mu) * lax.rsqrt(var + LN_EPS) * g + b).astype(x.dtype)

def _head_norm(x, eps):
    xf = x.astype(F32)
    mu = jnp.mean(xf, -1, keepdims=True)
    var = jnp.mean(jnp.square(xf - mu), -1, keepdims=True)
    y = (xf - mu) * lax.rsqrt(var + eps)
    return y.reshape(x.shape[0], x.shape[1], -1)

def _chunk_len(T):
    return CHUNK if T % CHUNK == 0 else T

def _to_chunks(a, L):
    B, T = a.shape[:2]
    return jnp.moveaxis(a.reshape((B, T // L, L) + a.shape[2:]), 1, 0)

def _from_chunks(a):
    n, B, L = a.shape[:3]
    return jnp.moveaxis(a, 0, 1).reshape((B, n * L) + a.shape[3:])

def _rotary(x, pos):
    half = x.shape[-1] // 2
    inv = ROPE_BASE ** (-jnp.arange(half, dtype=F32) / half)
    ang = pos.astype(F32)[:, None] * inv[None, :]
    cos = jnp.cos(ang)[None, :, None, :]
    sin = jnp.sin(ang)[None, :, None, :]
    x1 = x[..., :half].astype(F32)
    x2 = x[..., half:].astype(F32)
    return jnp.concatenate([x1 * cos - x2 * sin, x2 * cos + x1 * sin], axis=-1)

def _mlstm(q, k, v, ig, fg, C0, n0, m0):
    B, T, H, dh = q.shape
    L = _chunk_len(T)
    q = q.astype(F32)
    k = k.astype(F32) * dh ** -0.5
    v = v.astype(F32)
    ig = ig.astype(F32)
    logf = jax.nn.log_sigmoid(fg.astype(F32))
    causal = jnp.tril(jnp.ones((L, L), dtype=bool))[None, :, :, None]

    def step(carry, xs):
        C, n, m = carry
        qc, kc, vc, ic, lf = xs
        b = jnp.cumsum(lf, axis=1)
        d_log = jnp.where(causal, b[:, :, None, :] - b[:, None, :, :] + ic[:, None, :, :], -jnp.inf)
        inter = b + m[:, None, :]
        m_t = jnp.maximum(inter, jnp.max(d_log, axis=2))
        s = jnp.einsum('bthd,bjhd->btjh', qc, kc) * jnp.exp(d_log - m_t[:, :, None, :])
        w_inter = jnp.exp(inter - m_t)
        num = jnp.einsum('btjh,bjhd->bthd', s, vc) + w_inter[..., None] * jnp.einsum('bthk,bhkv->bthv', qc, C)
        den = jnp.sum(s, axis=2) + w_inter * jnp.einsum('bthk,bhk->bth', qc, n)
        h = num / jnp.maximum(jnp.abs(den), jnp.exp(-m_t))[..., None]
        b_end = b[:, -1]
        w_log = b_end[:, None, :] - b + ic
        m_new = jnp.maximum(b_end + m, jnp.max(w_log, axis=1))
        w_j = jnp.exp(w_log - m_new[:, None, :])
        carry_w = jnp.exp(b_end + m - m_new)
        C_new = carry_w[..., None, None] * C + jnp.einsum('bjh,bjhk,bjhv->bhkv', w_j, kc, vc)
        n_new = carry_w[..., None] * n + jnp.einsum('bjh,bjhk->bhk', w_j, kc)
        return (C_new, n_new, m_new), h

    xs = tuple(_to_chunks(a, L) for a in (q, k, v, ig, logf))
    (C1, n1, m1), h = lax.scan(step, (C0.astype(F32), n0.astype(F32), m0.astype(F32)), xs)
    return _from_chunks(h), C1, n1, m1

def _retention(q, k, v, R0):
    B, T, H, dk = q.shape
    L = _chunk_len(T)
    k = k * dk ** -0.5
    v = v.astype(F32)
    log_g = jnp.log(1.0 - 2.0 ** (-5.0 - jnp.arange(H, dtype=F32)))
    idx = jnp.arange(L, dtype=F32)
    diff = idx[:, None] - idx[None, :]
    d_mask = jnp.where(diff[..., None] >= 0, jnp.exp(jnp.maximum(diff, 0.0)[..., None] * log_g), 0.0)
    xi = jnp.exp((idx + 1.0)[:, None] * log_g)
    zeta = jnp.exp((L - 1.0 - idx)[:, None] * log_g)
    g_chunk = jnp.exp(L * log_g)

    def step(R, xs):
        qc, kc, vc = xs
        s = jnp.einsum('bthd,bjhd->btjh', qc, kc) * d_mask
        o = jnp.einsum('btjh,bjhv->bthv', s, vc) + xi[None, :, :, None] * jnp.einsum('bthk,bhkv->bthv', qc, R)
        R_new = g_chunk[None, :, None, None] * R + jnp.einsum('jh,bjhk,bjhv->bhkv', zeta, kc, vc)
        return R_new, o

    R1, o = lax.scan(step, R0.astype(F32), tuple(_to_chunks(a, L) for a in (q, k, v)))
    return _from_chunks(o), R1

def _lin_combine(left, right):
    a1, b1 = left
    a2, b2 = right
    return a1 * a2, a2 * b1 + b2

def _rglru(xb, conv0, h0, conv_w, conv_b, w_a, b_a, w_x, b_x, lam):
    B, T, W = xb.shape
    xp = jnp.concatenate([conv0.astype(F32), xb.astype(F32)], axis=1)
    xc = conv_b + sum(xp[:, i:i + T] * conv_w[i] for i in range(CONV_W))
    new_buf = xp[:, T:]
    xh = xc.reshape(B, T, N_GH, HEAD_DIM)
    r = jax.nn.sigmoid(jnp.einsum('btni,nij->btnj', xh, w_a).reshape(B, T, W) + b_a)
    i = jax.nn.sigmoid(jnp.einsum('btni,nij->btnj', xh, w_x).reshape(B, T, W) + b_x)
    log_a = -RGLRU_C * r * jax.nn.softplus(-lam)
    a = jnp.exp(log_a)
    b = jnp.sqrt(-jnp.expm1(2.0 * log_a)) * (i * xc)
    b = b.at[:, 0].add(a[:, 0] * h0.astype(F32))
    _, h = lax.associative_scan(_lin_combine, (a, b), axis=1)
    return h, h[:, -1], new_buf

def _rwkv7(z, shift0, S0, mu, w0, w2, a0, a2, g2, k_k, k_a, r_k, lnx_g, lnx_b):
    B, T, _ = z.shape
    GW = GROUP_W
    z = z.astype(F32)
    zprev = jnp.concatenate([shift0.astype(F32)[:, None], z[:, :-1]], axis=1)
    zs = z + (zprev - z) * mu
    r, k, v, zw, za, zg = jnp.split(zs, [GW, 2 * GW, 3 * GW, 3 * GW + RW_DECAY_RANK,
                                         3 * GW + RW_DECAY_RANK + RW_A_RANK], axis=-1)
    logw = -jax.nn.softplus(-(w0 + jnp.tanh(zw) @ w2)) - 0.5
    decay = jnp.exp(-jnp.exp(logw))
    a = jax.nn.sigmoid(a0 + za @ a2)
    g = jax.nn.sigmoid(zg) @ g2
    hd = lambda t: t.reshape(B, T, N_GH, HEAD_DIM)
    kk = hd(k * k_k)
    kk = kk / jnp.maximum(jnp.sqrt(jnp.sum(kk * kk, -1, keepdims=True)), 1e-12)
    k = k * (1.0 + (a - 1.0) * k_a)
    r_h, k_h, v_h, w_h, a_h = hd(r), hd(k), hd(v), hd(decay), hd(a)
    tm = lambda t: jnp.moveaxis(t, 1, 0)

    def step(S, inp):
        r_t, k_t, v_t, w_t, kk_t, a_t = inp
        s_kk = jnp.einsum('bhvk,bhk->bhv', S, kk_t)
        S = (S * w_t[:, :, None, :] - s_kk[..., None] * (kk_t * a_t)[:, :, None, :]
             + v_t[..., None] * k_t[:, :, None, :])
        return S, jnp.einsum('bhvk,bhk->bhv', S, r_t)

    S1, o = lax.scan(step, S0.astype(F32), (tm(r_h), tm(k_h), tm(v_h), tm(w_h), tm(kk), tm(a_h)))
    o = jnp.moveaxis(o, 0, 1)
    y = _head_norm(o, RWKV_GN_EPS) * lnx_g + lnx_b
    bonus = jnp.sum(r_h * k_h * r_k, -1, keepdims=True) * v_h
    y = (y + bonus.reshape(B, T, GW)) * g
    return y, S1, z[:, -1]

def _cross_attn(x, mem_k, mem_v, wq, wo):
    B, T, _ = x.shape
    q = (x @ wq).reshape(B, T, XA_HEADS, XA_HEAD_DIM)
    s = jnp.einsum('bthd,bnhd->bhtn', q, mem_k).astype(F32) * XA_HEAD_DIM ** -0.5
    p = jax.nn.softmax(s, axis=-1).astype(x.dtype)
    o = jnp.einsum('bhtn,bnhd->bthd', p, mem_v).reshape(B, T, -1)
    return o @ wo

def _layer(x, pos, mem_k, mem_v, state, P):
    B, T, _ = x.shape
    C0, n0, m0, R0, h0, conv0, S0, shift0 = state
    GW = GROUP_W
    z = x @ P['w_in']
    widths = (GW, GW, GW, GW, N_GH, N_GH, GW, GW, GW, GW, GW, GW, RWKV_W)
    splits = np.cumsum(widths)[:-1].tolist()
    mq, mk, mv, mo, mi, mf, rq, rk, rv, rg, gx, gg, wz = jnp.split(z, splits, axis=-1)
    hd = lambda t: t.reshape(B, T, N_GH, HEAD_DIM)
    hm, C1, n1, m1 = _mlstm(hd(mq), hd(mk), hd(mv), mi + P['mlstm_b_i'], mf + P['mlstm_b_f'], C0, n0, m0)
    y_m = jax.nn.sigmoid(mo.astype(F32)) * (_head_norm(hm, HEAD_EPS) * P['mlstm_g'])
    ro, R1 = _retention(_rotary(hd(rq), pos), _rotary(hd(rk), pos), hd(rv), R0)
    y_r = jax.nn.silu(rg.astype(F32)) * (_head_norm(ro, HEAD_EPS) * P['ret_g'])
    hg, h1, conv1 = _rglru(gx, conv0, h0, P['conv_w'], P['conv_b'], P['rg_w_a'], P['rg_b_a'],
                           P['rg_w_x'], P['rg_b_x'], P['rg_lam'])
    y_g = hg * jax.nn.gelu(gg.astype(F32))
    y_w, S1, shift1 = _rwkv7(wz, shift0, S0, P['rwkv_mu'], P['rwkv_w0'], P['rwkv_w2'], P['rwkv_a0'],
                             P['rwkv_a2'], P['rwkv_g2'], P['rwkv_k_k'], P['rwkv_k_a'], P['rwkv_r_k'],
                             P['rwkv_lnx_g'], P['rwkv_lnx_b'])
    mix = jnp.concatenate([y_m, y_r, y_g, y_w], axis=-1).astype(x.dtype) @ P['w_out']
    x = _layer_norm(ALPHA * x + mix, P['ln1_g'], P['ln1_b'])
    x = _layer_norm(ALPHA * x + _cross_attn(x, mem_k, mem_v, P['xa_wq'], P['xa_wo']), P['ln2_g'], P['ln2_b'])
    ff = jnp.square(jax.nn.relu(x @ P['w_up'])) @ P['w_down']
    x = _layer_norm(ALPHA * x + ff, P['ln3_g'], P['ln3_b'])
    dt = x.dtype
    new = (C1.astype(dt), n1.astype(dt), m1.astype(dt), R1.astype(dt), h1.astype(dt),
           conv1.astype(dt), S1.astype(dt), shift1.astype(dt))
    return x, new

def setup_inputs(seed: int = 0) -> dict:
    key = jax.random.key(seed)
    keys = iter(jax.random.split(key, 64))

    def nrm(shape, scale):
        return jax.random.normal(next(keys), shape, F32) * scale

    def gain(shape):
        return 1.0 + nrm(shape, 0.01)

    L, H, dh, GW, D = DEPTH, N_GH, HEAD_DIM, GROUP_W, D_MODEL
    xav = lambda fi, fo: BETA * (2.0 / (fi + fo)) ** 0.5
    u_lru = jax.random.uniform(next(keys), (L, GW), F32, 0.9, 0.999)
    a_base = u_lru ** (1.0 / RGLRU_C)
    rg_lam = jnp.log(a_base) - jnp.log1p(-a_base)
    return {
        'x_prompt': nrm((BATCH, SEQ, D), 1.0),
        'x_sample': nrm((DEC_BATCH, DEC_SEQ, D), 1.0),
        'state_mlstm_C': nrm((L, DEC_BATCH, H, dh, dh), 0.05),
        'state_mlstm_n': nrm((L, DEC_BATCH, H, dh), 0.05),
        'state_mlstm_m': nrm((L, DEC_BATCH, H), 1.0),
        'state_ret': nrm((L, DEC_BATCH, H, dh, dh), 0.1),
        'state_rglru_h': nrm((L, DEC_BATCH, GW), 0.5),
        'state_rglru_conv': nrm((L, DEC_BATCH, CONV_W - 1, GW), 1.0),
        'state_rwkv_S': nrm((L, DEC_BATCH, H, dh, dh), 0.1),
        'state_rwkv_shift': nrm((L, DEC_BATCH, RWKV_W), 1.0),
        'cache_mem_k': nrm((L, DEC_BATCH, N_MEM, XA_HEADS, XA_HEAD_DIM), 1.0),
        'cache_mem_v': nrm((L, DEC_BATCH, N_MEM, XA_HEADS, XA_HEAD_DIM), 0.5),
        'mem_prompt': nrm((BATCH, N_MEM, D), 1.0),
        'ln_in_g': gain((D,)),
        'ln_in_b': nrm((D,), 0.01),
        'w_in': nrm((L, D, N_IN), D ** -0.5),
        'mlstm_b_i': nrm((L, H), 0.1) - 1.0,
        'mlstm_b_f': jnp.linspace(3.0, 6.0, H, dtype=F32) + nrm((L, H), 0.1),
        'mlstm_g': gain((L, GW)),
        'ret_g': gain((L, GW)),
        'conv_w': nrm((L, CONV_W, GW), CONV_W ** -0.5),
        'conv_b': nrm((L, GW), 0.01),
        'rg_w_a': nrm((L, H, dh, dh), dh ** -0.5),
        'rg_b_a': nrm((L, GW), 0.01),
        'rg_w_x': nrm((L, H, dh, dh), dh ** -0.5),
        'rg_b_x': nrm((L, GW), 0.01),
        'rg_lam': rg_lam,
        'rwkv_mu': jax.random.uniform(next(keys), (L, RWKV_W), F32),
        'rwkv_w0': jnp.linspace(-5.0, 1.0, GW, dtype=F32) + nrm((L, GW), 0.1),
        'rwkv_w2': nrm((L, RW_DECAY_RANK, GW), 0.1),
        'rwkv_a0': nrm((L, GW), 0.1),
        'rwkv_a2': nrm((L, RW_A_RANK, GW), 0.1),
        'rwkv_g2': nrm((L, RW_GATE_RANK, GW), RW_GATE_RANK ** -0.5),
        'rwkv_k_k': 0.85 + nrm((L, GW), 0.02),
        'rwkv_k_a': 1.0 + nrm((L, GW), 0.02),
        'rwkv_r_k': nrm((L, H, dh), 0.1),
        'rwkv_lnx_g': gain((L, GW)),
        'rwkv_lnx_b': nrm((L, GW), 0.01),
        'w_out': nrm((L, D_MIX, D), xav(D_MIX, D)),
        'ln1_g': gain((L, D)),
        'ln1_b': nrm((L, D), 0.01),
        'xa_wq': nrm((L, D, D), D ** -0.5),
        'xa_wk': nrm((L, D, D), D ** -0.5),
        'xa_wv': nrm((L, D, D), xav(D, D)),
        'xa_wo': nrm((L, D, D), xav(D, D)),
        'ln2_g': gain((L, D)),
        'ln2_b': nrm((L, D), 0.01),
        'w_up': nrm((L, D, D_FF), xav(D, D_FF)),
        'w_down': nrm((L, D_FF, D), xav(D_FF, D)),
        'ln3_g': gain((L, D)),
        'ln3_b': nrm((L, D), 0.01),
    }

def reference(x_prompt, x_sample, state_mlstm_C, state_mlstm_n, state_mlstm_m, state_ret,
              state_rglru_h, state_rglru_conv, state_rwkv_S, state_rwkv_shift, cache_mem_k,
              cache_mem_v, mem_prompt, ln_in_g, ln_in_b, w_in, mlstm_b_i, mlstm_b_f, mlstm_g,
              ret_g, conv_w, conv_b, rg_w_a, rg_b_a, rg_w_x, rg_b_x, rg_lam, rwkv_mu, rwkv_w0,
              rwkv_w2, rwkv_a0, rwkv_a2, rwkv_g2, rwkv_k_k, rwkv_k_a, rwkv_r_k, rwkv_lnx_g,
              rwkv_lnx_b, w_out, ln1_g, ln1_b, xa_wq, xa_wk, xa_wv, xa_wo, ln2_g, ln2_b, w_up,
              w_down, ln3_g, ln3_b):
    Bp, Tp, _ = x_prompt.shape
    Ts = x_sample.shape[1]
    pos_p = jnp.arange(Tp, dtype=jnp.int32)
    pos_s = PAST_LEN + jnp.arange(Ts, dtype=jnp.int32)
    dt = x_prompt.dtype
    zero_state = (jnp.zeros((Bp, N_GH, HEAD_DIM, HEAD_DIM), dt), jnp.zeros((Bp, N_GH, HEAD_DIM), dt),
                  jnp.zeros((Bp, N_GH), dt), jnp.zeros((Bp, N_GH, HEAD_DIM, HEAD_DIM), dt),
                  jnp.zeros((Bp, GROUP_W), dt), jnp.zeros((Bp, CONV_W - 1, GROUP_W), dt),
                  jnp.zeros((Bp, N_GH, HEAD_DIM, HEAD_DIM), dt), jnp.zeros((Bp, RWKV_W), dt))
    xp = _layer_norm(x_prompt, ln_in_g, ln_in_b)
    xs = _layer_norm(x_sample, ln_in_g, ln_in_b)
    new_p, new_s, mk_p, mv_p = [], [], [], []
    for l in range(DEPTH):
        P = {'w_in': w_in[l], 'mlstm_b_i': mlstm_b_i[l], 'mlstm_b_f': mlstm_b_f[l], 'mlstm_g': mlstm_g[l],
             'ret_g': ret_g[l], 'conv_w': conv_w[l], 'conv_b': conv_b[l], 'rg_w_a': rg_w_a[l],
             'rg_b_a': rg_b_a[l], 'rg_w_x': rg_w_x[l], 'rg_b_x': rg_b_x[l], 'rg_lam': rg_lam[l],
             'rwkv_mu': rwkv_mu[l], 'rwkv_w0': rwkv_w0[l], 'rwkv_w2': rwkv_w2[l], 'rwkv_a0': rwkv_a0[l],
             'rwkv_a2': rwkv_a2[l], 'rwkv_g2': rwkv_g2[l], 'rwkv_k_k': rwkv_k_k[l], 'rwkv_k_a': rwkv_k_a[l],
             'rwkv_r_k': rwkv_r_k[l], 'rwkv_lnx_g': rwkv_lnx_g[l], 'rwkv_lnx_b': rwkv_lnx_b[l],
             'w_out': w_out[l], 'ln1_g': ln1_g[l], 'ln1_b': ln1_b[l], 'xa_wq': xa_wq[l], 'xa_wo': xa_wo[l],
             'ln2_g': ln2_g[l], 'ln2_b': ln2_b[l], 'w_up': w_up[l], 'w_down': w_down[l],
             'ln3_g': ln3_g[l], 'ln3_b': ln3_b[l]}
        kp = (mem_prompt @ xa_wk[l]).reshape(Bp, -1, XA_HEADS, XA_HEAD_DIM)
        vp = (mem_prompt @ xa_wv[l]).reshape(Bp, -1, XA_HEADS, XA_HEAD_DIM)
        xp, st_p = _layer(xp, pos_p, kp, vp, zero_state, P)
        st_in = (state_mlstm_C[l], state_mlstm_n[l], state_mlstm_m[l], state_ret[l], state_rglru_h[l],
                 state_rglru_conv[l], state_rwkv_S[l], state_rwkv_shift[l])
        xs, st_s = _layer(xs, pos_s, cache_mem_k[l], cache_mem_v[l], st_in, P)
        new_p.append(st_p)
        new_s.append(st_s)
        mk_p.append(kp)
        mv_p.append(vp)
    p_C, p_n, p_m, p_R, p_h, p_conv, p_S, p_shift = [jnp.stack(s) for s in zip(*new_p)]
    s_C, s_n, s_m, s_R, s_h, s_conv, s_S, s_shift = [jnp.stack(s) for s in zip(*new_s)]
    p_mem_k = jnp.stack(mk_p)
    p_mem_v = jnp.stack(mv_p)
    return (xp, xs, p_C, p_n, p_m, p_R, p_h, p_conv, p_S, p_shift, p_mem_k, p_mem_v,
            s_C, s_n, s_m, s_R, s_h, s_conv, s_S, s_shift)


_drawn_inputs = setup_inputs


def setup_inputs(seed=0):
    import zlib

    import numpy as np

    out = dict(_drawn_inputs(seed))
    spreads = {}
    factors = {'cache_mem_k': 2.76,
     'ln_in_g': 3.039,
     'mlstm_g': 183.614,
     'ret_g': 27.841,
     'rg_b_a': 33.138,
     'rg_b_x': 25.631,
     'rwkv_k_k': 40.449,
     'rwkv_lnx_g': 191.521,
     'rwkv_lnx_b': 190.609,
     'ln1_g': 3.862,
     'ln2_g': 3.765,
     'ln3_g': 3.671,
     'ln_in_b': 3.437,
     'mlstm_b_i': 4.753,
     'conv_b': 3.458,
     'ln1_b': 5.594,
     'ln2_b': 6.299,
     'ln3_b': 4.637}
    for name, (base, spread) in spreads.items():
        noise = np.random.default_rng([zlib.crc32(name.encode()), seed]).standard_normal(out[name].shape)
        drawn = base * np.exp(spread * noise) if base else spread * noise
        out[name] = jnp.asarray(drawn.astype(out[name].dtype))
    for name, factor in factors.items():
        out[name] = (out[name] * factor).astype(out[name].dtype)
    return out
```

```python
from contextlib import ExitStack

import concourse.bass as bass
from concourse import mybir

F32 = mybir.dt.float32
ALU = mybir.AluOpType
ACT = mybir.ActivationFunctionType
AX = mybir.AxisListType

P = 128
D = 1024
KC = D // P
DEPTH = 2
SEQ = 512
NB = 8
TS = 4
NS = NB * TS
NT = SEQ + NS
H = 4
HD = 64
FF = 4 * D
FC = FF // P
NMEM = 256
W512 = 512
N_IN = 3592
ALPHA = (2.0 * DEPTH) ** 0.25
LN_EPS = 1e-5
HEAD_EPS = 1e-6
RW_EPS = 64e-5
QSCALE = HD ** -0.5
XSCALE = 256 ** -0.5
RW_C = 0.6065306597126334
NEG = -1.0e30
TMP = 11712
TILES = [(0, 128), (128, 128), (256, 128), (384, 128), (SEQ, NS)]

ZQ_A, ZK_A, ZV_A, ZO_A = 0, 2, 4, 6
ZQ_B, ZK_B, ZV_B, ZG_B = 8, 10, 12, 14
ZX_C, ZG_C = 16, 18
ZR_D, ZK_D, ZV_D, ZWA_D, ZG_D = 20, 22, 24, 26, 27
SLABS_IN = [(2056, 16), (2568, 20), (3080, 24), (0, 0), (512, 4), (1032, 8), (1544, 12)]
GATE_COL = 1024

ROWS = {}
for _n, _k in (("mlstm_g", 2), ("ret_g", 2), ("conv_w", 8), ("conv_b", 2), ("rg_b_a", 2), ("rg_b_x", 2),
               ("rg_lam", 2), ("rwkv_mu", 8), ("rwkv_w0", 2), ("rwkv_a0", 2), ("rwkv_k_k", 2), ("rwkv_k_a", 2),
               ("rwkv_r_k", 2), ("rwkv_lnx_g", 2), ("rwkv_lnx_b", 2), ("state_rglru_h", 16),
               ("state_rwkv_shift", 64)):
    ROWS[_n] = (sum(k for _, k in ROWS.values()), _k)
N_ROWS = sum(k for _, k in ROWS.values())


def constants():
    import numpy as np
    p = np.arange(P)
    c = {}
    c["ident"] = np.eye(P)
    same64 = (p[:, None] // 64 == p[None, :] // 64)
    c["sum64"] = same64
    c["mean64"] = same64 / 64.0
    swap = np.zeros((P, P))
    for m in range(P):
        d = m % 64
        swap[m + 32 if d < 32 else m - 32, m] = -1.0 if d < 32 else 1.0
    c["swap"] = swap
    inv = (10000.0 ** (-np.arange(32, dtype=np.float32) / 32)).astype(np.float32)
    pos = np.concatenate([np.arange(SEQ), 4096 + np.tile(np.arange(TS), NB)]).astype(np.float32)
    ang = (pos[None, :] * inv[p % 32][:, None]).astype(np.float32)
    c["cos"] = np.cos(ang)
    c["sin"] = np.sin(ang)
    j, t = p[:, None], p[None, :]
    js, ts = j[:NS], t[:, :NS]
    seq_same = (js // TS == ts // TS)
    c["causal"] = np.where(j <= t, 0.0, NEG)
    cs = np.full((P, NS), NEG)
    cs[:NS] = np.where(seq_same & (js <= ts), 0.0, NEG)
    c["causal_s"] = cs
    lg = np.log(1.0 - 2.0 ** (-5.0 - np.arange(H, dtype=np.float32))).astype(np.float64)
    dm = np.where((j <= t)[:, None, :], np.exp(np.maximum(t - j, 0)[:, None, :] * lg[None, :, None]), 0.0)
    c["decay"] = dm.reshape(P, H * P)
    ds = np.zeros((P, H, NS))
    ds[:NS] = np.where((seq_same & (js <= ts))[:, None, :],
                       np.exp(np.maximum(ts - js, 0)[:, None, :] * lg[None, :, None]), 0.0)
    c["decay_s"] = ds.reshape(P, H * NS)
    idx = np.concatenate([np.arange(SEQ) % P, np.tile(np.arange(TS), NB)])
    hp = 2 * np.arange(2)[None, :] + (p // 64)[:, None]
    c["xi"] = np.exp((idx + 1.0)[None, None, :] * lg[hp][:, :, None])[:, :, :P]
    c["xi_s"] = np.exp((idx + 1.0)[None, None, :] * lg[hp][:, :, None])[:, :, SEQ:]
    c["zeta"] = np.exp((P - 1.0 - p)[:, None] * lg[None, :])
    c["zeta_s"] = np.exp((TS - 1.0 - p % TS)[:, None] * lg[None, :])
    c["g_chunk"] = np.exp(P * lg[hp])
    c["g_chunk_s"] = np.exp(TS * lg[hp])
    same = (j // 64 == t // 64)
    c["delta"] = np.stack([same & (j < t), same & (j <= t)], 1)
    dsm = np.zeros((P, 2, NS))
    dsm[:NS] = np.stack([seq_same & (js < ts), seq_same & (js <= ts)], 1)
    c["delta_s"] = dsm
    for m in (1, 2, 4, 8, 16, 32):
        c[f"level{m}"] = (j // (2 * m) == t // (2 * m)) & (j % (2 * m) < m) & (t % (2 * m) >= m)
    c["own"] = (p[:, None] // TS == np.arange(NB)[None, :])
    sp = np.zeros((P, 2, P))
    sg = np.zeros((P, H, P))
    for h in range(H):
        for pr in range(2):
            sp[h, pr] = (h == 2 * pr + p // 64)
        sg[h, h] = 1.0
    c["sel_pair"] = sp
    c["sel_head"] = sg
    r128 = np.ones(NT)
    r128[0:SEQ:P] = 0
    r128[SEQ::TS] = 0
    c["keep_a"] = np.tile(r128, (P, 1))
    md = np.zeros(NT)
    md[SEQ::TS] = NEG
    c["drop_a"] = np.tile(md, (P, 1))
    r64 = np.ones(NT)
    r64[0:SEQ:64] = 0
    r64[SEQ::TS] = 0
    c["keep_d"] = np.tile(r64, (P, 1))
    c["ones"] = np.ones((P, 64))
    c["eps"] = np.tile(np.array([HEAD_EPS, RW_EPS, 10.0 * np.log(2.0), LN_EPS]), (P, 1))
    table, at, n = [], {}, 0
    for k, a in c.items():
        a = np.asarray(a, np.float32).reshape(P, -1)
        at[k] = (n, a.shape[1])
        table.append(a)
        n += a.shape[1]
    return np.ascontiguousarray(np.concatenate(table, 1)), at


class Signals:

    def __init__(self, nc, ctx, prefix):
        self.nc, self.ctx, self.prefix = nc, ctx, prefix
        self.sems, self.count = {}, {}

    def __getitem__(self, name):
        if name not in self.sems:
            self.sems[name] = self.ctx.enter_context(self.nc.semaphore(self.prefix + name))
            self.count[name] = 0
        return self.sems[name]

    def up(self, ins, name, by=1):
        ins.then_inc(self[name], by)
        self.count[name] += by
        return self.count[name]

    def numbers(self):
        n = [s.num for s in self.sems.values()]
        return range(min(n), max(n) + 1)


class Banks:

    def __init__(self, sig, psum):
        self.sig, self.psum = sig, psum
        self.uses = [0] * 8
        self.turn = {}
        for b in range(8):
            sig[f"full{b}"], sig[f"free{b}"]

    def begin(self, pe, key, b):
        assert key not in self.turn, key
        if self.uses[b]:
            pe.wait_ge(self.sig[f"free{b}"], self.uses[b])
        self.uses[b] += 1
        self.turn[key] = (b, self.uses[b])
        return self.psum[:, b, :]

    def filled(self, ins, key):
        ins.then_inc(self.sig[f"full{self.turn[key][0]}"], 1)

    def take(self, eng, key):
        b, n = self.turn[key]
        eng.wait_ge(self.sig[f"full{b}"], n)
        return self.psum[:, b, :]

    def give(self, ins, key):
        ins.then_inc(self.sig[f"free{self.turn[key][0]}"], 1)

    def given(self, eng, key):
        b, n = self.turn[key]
        eng.wait_ge(self.sig[f"free{b}"], n)


def build(nc, A, O, table, where):
    with ExitStack() as ctx:
        def sb(name, cols):
            return ctx.enter_context(nc.sbuf_tensor(name, [P, cols], F32))

        con = sb("con", table.shape[1])
        big = sb("big", 32 * NT)
        xT = sb("xT", KC * NT)
        xtok = sb("xtok", 5 * D)
        ring = sb("ring", 2 * KC * W512)
        tmp = sb("tmp", TMP)
        sm = sb("sm", 96)
        psum = ctx.enter_context(nc.psum_tensor("psum", [P, 8, 512], F32))

        def const(name, *shape):
            a, n = where[name]
            v = con[:, a:a + n]
            if len(shape) == 2:
                v = v.rearrange("p (a b) -> p a b", a=shape[0])
            return v

        def cols(t, at, *shape):
            n = 1
            for s in shape:
                n *= s
            v = t[:, at:at + n]
            if len(shape) == 2:
                v = v.rearrange("p (a b) -> p a b", a=shape[0])
            if len(shape) == 3:
                v = v.rearrange("p (a b c) -> p a b c", a=shape[0], b=shape[1])
            if len(shape) == 4:
                v = v.rearrange("p (a b c d) -> p a b c d", a=shape[0], b=shape[1], c=shape[2])
            return v

        def z(f, n=1):
            v = big[:, f * NT:(f + n) * NT]
            return v if n == 1 else v.rearrange("p (n t) -> p n t", n=n)

        def bc(ap, shape):
            return ap.broadcast_to(shape)

        xTv = cols(xT, 0, KC, NT)
        xk = cols(xtok, 0, 5, D)
        wring = cols(ring, 0, 2, KC, W512)
        stats = cols(sm, 0, 5, 2, 6)
        mv = cols(sm, 60, 5, 2)
        rstd = cols(sm, 70, 5)
        ident = const("ident")
        lnp = cols(tmp, 0, 2, D)
        yp = O["y_prompt"].rearrange("a (t p) d -> p (a t) d", p=P)
        ys = O["y_sample"].rearrange("b t d -> (b t) d")

        def ln_vector(v, sig, i, T):
            n = TILES[T][1]
            x = xk[:n, T, :]
            for half in range(2):
                ins = v.bn_stats(stats[:n, T, half, :], x[:, half * 512:half * 512 + 512])
            v.wait_ge(sig["v"], sig.up(ins, "v"))
            sig.up(v.bn_aggr(mv[:n, T, :], stats[:n, T, :, :].rearrange("p a b -> p (a b)")), "ln_var")
            v.wait_ge(sig["ln_rstd"], 5 * i + T + 1)
            sig.up(v.tensor_scalar(x, x, mv[:n, T, 0:1], rstd[:n, T:T + 1], ALU.subtract, ALU.mult), "ln_norm")

        def ln_scalar(s, sig, i, T):
            n = TILES[T][1]
            s.wait_ge(sig["ln_var"], 5 * i + T + 1)
            r = rstd[:n, T:T + 1]
            s.wait_ge(sig["s"], sig.up(s.activation(r, mv[:n, T, 1:2], ACT.Ln, bias=const("eps")[:n, 3:4]), "s"))
            sig.up(s.activation(r, r, ACT.Exp, scale=-0.5), "ln_rstd")

        def ln_pool(g, sig, i, T):
            n = TILES[T][1]
            x = xk[:n, T, :]
            if T == 0:
                g.wait_ge(sig["ln_param"], 32 * (i + 1))
            g.wait_ge(sig["ln_norm"], 5 * i + T + 1)
            g.wait_ge(sig["g"], sig.up(g.tensor_tensor(x, x, lnp[:n, 0, :], ALU.mult), "g"))
            sig.up(g.tensor_tensor(x, x, lnp[:n, 1, :], ALU.add), "ln_done")

        def turn_x_tensor(pe, bk, sig, i, T, banks):
            t0, n = TILES[T]
            pe.wait_ge(sig["ln_done"], 5 * i + T + 1)
            for g in range(2):
                ps = bk.begin(pe, ("xT", i, T, g), banks[g]).rearrange("p (c t) -> p c t", c=4)
                for c in range(4):
                    ins = pe.transpose(ps[:, c, :n], xk[:n, T, (4 * g + c) * P:(4 * g + c + 1) * P], ident[:n, :n])
                bk.filled(ins, ("xT", i, T, g))

        def turn_x_scalar(s, bk, sig, i, T):
            t0, n = TILES[T]
            for g in range(2):
                ps = bk.take(s, ("xT", i, T, g)).rearrange("p (c t) -> p c t", c=4)
                bk.give(s.activation(xTv[:, 4 * g:4 * g + 4, t0:t0 + n], ps[:, :, :n], ACT.Copy), ("xT", i, T, g))

        def ln_params(sp, sig, g, b):
            sig.up(sp.dma_start(lnp[:, 0, :], g.partition_broadcast(P)), "ln_param", 16)
            sig.up(sp.dma_start(lnp[:, 1, :], b.partition_broadcast(P)), "ln_param", 16)

        s0 = Signals(nc, ctx, "in_")
        b0 = Banks(s0, psum)
        with nc.Block() as block:
            @block.tensor
            def _(pe):
                pe.wait_ge(s0["con"], 16)
                for T in range(5):
                    turn_x_tensor(pe, b0, s0, 0, T, (2 * (T % 2), 2 * (T % 2) + 1))

            @block.scalar
            def _(s):
                s.wait_ge(s0["con"], 16)
                for T in range(5):
                    ln_scalar(s, s0, 0, T)
                for T in range(5):
                    turn_x_scalar(s, b0, s0, 0, T)

            @block.vector
            def _(v):
                v.wait_ge(s0["x"], 32)
                for T in range(5):
                    ln_vector(v, s0, 0, T)

            @block.gpsimd
            def _(g):
                for T in range(5):
                    ln_pool(g, s0, 0, T)

            @block.sync
            def _(sp):
                sp.dma_start(con[:, :], table).then_inc(s0["con"], 16)
                sp.dma_start(xk[:, 0:4, :], A["x_prompt"].rearrange("a (t p) d -> p (a t) d", p=P)).then_inc(s0["x"], 16)
                sp.dma_start(xk[:NS, 4, :], A["x_sample"].rearrange("b t d -> (b t) d")).then_inc(s0["x"], 16)
                ln_params(sp, s0, A["ln_in_g"], A["ln_in_b"])
                sp.wait_ge(s0["ln_done"], 5)
                sp.dma_start(yp, xk[:, 0:4, :]).then_inc(s0["y"], 16)
                sp.dma_start(ys, xk[:NS, 4, :]).then_inc(s0["y"], 16)
                sp.wait_ge(s0["y"], 32)

        engines = list(nc.engines.keys())
        nc.multi_engine_barrier(engines, sems_to_clear=s0.numbers())

        sig = Signals(nc, ctx, "")
        bk = Banks(sig, psum)
        with nc.Fori(0, DEPTH) as l:
            N_ROW_DMAS = len(ROWS) + 2
            N_SMALL_W = 11
            N_OUT1 = []
            def slab_read(sp, n):
                if n < 7:
                    bk.take(sp, ("z", SLABS_IN[n][1] + 3, 1))
                elif n < 9:
                    bk.take(sp, ("wout", 4, n - 7))
                elif n < 13:
                    bk.take(sp, ("kv", n - 9, 1))
                elif n < 15:
                    bk.take(sp, ("q", 4 * (n - 13) + 3, 1))
                elif n < 17:
                    bk.take(sp, ("wo", 4, n - 15))
                elif n < 25:
                    bk.take(sp, ("up", 4 * (n - 17) + 3, 1))
                elif (n - 25) % 4 == 3:
                    bk.take(sp, ("down", (n - 25) // 4, 4))
                else:
                    sp.wait_ge(sig["downread"], n - 25 + 1 - (n - 25) // 4)


            def out_slab(sp, n):
                if n < 9:
                    name, r, c = "w_out", 0, n - 7
                elif n < 13:
                    name, r, c = ("xa_wk", "xa_wv")[(n - 9) // 2], 0, (n - 9) % 2
                elif n < 15:
                    name, r, c = "xa_wq", 0, n - 13
                elif n < 17:
                    name, r, c = "xa_wo", 0, n - 15
                elif n < 25:
                    name, r, c = "w_up", 0, n - 17
                else:
                    name, r, c = "w_down", (n - 25) % 4, (n - 25) // 4
                slab_read(sp, n - 2)
                sp.dma_start(wring[:, n % 2], A[name][bass.ds(l, 1), r * D:(r + 1) * D, c * W512:(c + 1) * W512]
                             .rearrange("a (c p) n -> p (a c) n", p=P)).then_inc(sig[f"slab{n % 2}"], 16)



            row = {k: slice(a, a + n) for k, (a, n) in ROWS.items()}
            at = 0

            def region(t, n):
                nonlocal_at[t] += n
                return nonlocal_at[t] - n

            nonlocal_at = {"tmp": 0, "xtok": 0}
            prow = cols(tmp, region("tmp", 128), 128)
            prow2 = cols(tmp, region("tmp", 128), 128)
            pc = cols(tmp, region("tmp", N_ROWS), N_ROWS)
            pc2 = cols(tmp, region("tmp", 64), 64)
            oc1 = cols(tmp, region("tmp", 126), 126)
            oc2 = cols(tmp, region("tmp", 36), 36)
            orow1, orow2 = prow, prow2
            graw = cols(tmp, region("tmp", NT), NT)
            wgate = cols(tmp, region("tmp", 512), KC, 64)
            wax = cols(tmp, region("tmp", 512), 2, 2, P)
            wwa = cols(tmp, region("tmp", 512), 4, P)
            wg2 = cols(tmp, region("tmp", 256), 2, P)
            bif = cols(tmp, region("tmp", 2), 2)
            m0 = cols(tmp, region("tmp", 8), NB)
            lamc = cols(tmp, region("tmp", 6), 3, 2)
            omka = cols(tmp, region("tmp", 2), 2)
            mcar = cols(tmp, region("tmp", 4), 4)
            carry = cols(tmp, region("tmp", 24), 2, 12)
            epc = cols(tmp, region("tmp", 32), 2, 16)
            SsT = cols(tmp, region("tmp", 1024), 2, NB, HD)
            X1 = cols(tmp, region("tmp", 2 * NT), 2, NT)
            X2 = cols(tmp, region("tmp", 2 * NT), 2, NT)
            X4 = cols(tmp, region("tmp", 2 * NT), 2, NT)
            X5 = cols(tmp, region("tmp", 2 * NT), 2, NT)
            dbase = region("tmp", 3072)
            Xm = cols(tmp, dbase, H, P)
            Dm = cols(tmp, dbase + 512, H, P)
            DmT = cols(tmp, dbase + 1024, H, P)
            WKT = cols(tmp, dbase + 1536, 2, P)
            CV = cols(tmp, dbase + 1792, H, HD)
            UV = cols(tmp, dbase + 2048, H, HD)
            SAn = cols(tmp, dbase + 2304, H, HD)
            ST = cols(tmp, dbase + 2560, 2, P)
            STe = cols(tmp, dbase + 2816, 2, P)
            assert nonlocal_at["tmp"] <= TMP, nonlocal_at
            dpad = cols(xtok, 0, 2, 2, 2, P)
            BM = cols(xtok, 1024, 2, 2, 2, P)
            KM = cols(xtok, 2048, 2, 2, 2, P)
            Dtok = cols(xtok, 3072, 4, 2, P)
            OmT = cols(xtok, 4096, 2, H, P)
            Sraw = cols(xtok, 1024, 4, H, HD)
            rows = [cols(xtok, 544 * i, NT) for i in range(6)]
            qpad = cols(xtok, 3264, 2, 2, P)
            Em = cols(xtok, 3776, H, P)
            Wm = cols(xtok, 4288, H, P)
            kw = cols(tmp, dbase, 2, P)
            vt = cols(tmp, dbase + 256, 2, P)
            Cb = cols(tmp, dbase + 512, 2, P)
            nb_ = cols(tmp, dbase + 768, 2, P)
            Rb = cols(tmp, dbase + 1024, 2, P)
            Cs = cols(tmp, dbase + 1280, 2, NB, HD)
            gcol = cols(tmp, dbase + 2304, 36)
            ncol = cols(tmp, dbase + 2340, 2)
            qspad = cols(tmp, dbase + 2344, 2, 2, NS)
            rden = cols(tmp, dbase + 2480, 2, P)
            qx = cols(tmp, dbase + 2736, 2, P)
            vx2 = cols(xtok, 3776, 2, NB, HD)
            Rs = cols(big, 28 * NT, 2, NB, HD)
            n0x = cols(big, 28 * NT + 1024, 2, NB, HD)
            OM0 = [0, 6, 12, 18, 24]
            T28 = z(28, 2)
            T30 = z(30, 2)


            HALVES = ((0, slice(0, NT // 2)), (1, slice(NT // 2, NT)))


            def segs(v):
                if len(v.shape) == 2:
                    return v[:, SEQ:].rearrange("p (b t) -> p b t", b=NB)
                return v[:, :, SEQ:].rearrange("p n (b t) -> p n b t", b=NB)


            def prm(name, i):
                return pc[:, ROWS[name][0] + i:ROWS[name][0] + i + 1]


            conv0 = pc2[:, 0:48].rearrange("p (b i f) -> p f b i", b=NB, i=3)
            n0c = pc2[:, 48:64].rearrange("p (b q) -> p q b", b=NB)
            h0c = pc[:, row["state_rglru_h"]].rearrange("p (b f) -> p f b", b=NB)
            sh0 = pc[:, row["state_rwkv_shift"]].rearrange("p (b f) -> p f b", b=NB)
            ZPOS = {}
            for _, f0 in SLABS_IN:
                for f in range(f0, f0 + 4):
                    ZPOS[f] = len(ZPOS)


            def z_wait(eng, *fs):
                f = max(fs, key=ZPOS.get)
                bk.given(eng, ("z", f, 0))
                bk.given(eng, ("z", f, 1))


            def slab_pe(pe, n):
                pe.wait_ge(sig[f"slab{n % 2}"], 16 * (n // 2 + 1))
                return wring[:, n % 2, :, :]


            def after(eng, ins, name):
                eng.wait_ge(sig[name], sig.up(ins, name))


            def product(pe, key, bank, rhs, lhsT_list):
                n = len(lhsT_list)
                m = lhsT_list[0].shape[1]
                for part, c in HALVES:
                    b, w = bank + 2 * part, c.stop - c.start
                    ps = bk.begin(pe, key + (part,), b)
                    for k in range(n):
                        ins = pe.matmul(ps[:m, :w], lhsT_list[k], rhs(k)[:, c], start=(k == 0), stop=(k == n - 1))
                    bk.filled(ins, key + (part,))


            def x_product(pe, key, bank, lhsT_list):
                product(pe, key, bank, lambda k: xTv[:, k, :], lhsT_list)


            def drain(eng, key, fn):
                for part, c in HALVES:
                    ps = bk.take(eng, key + (part,))
                    ins = fn(ps[:, :c.stop - c.start], c)
                    bk.give(ins, key + (part,))
                    bk.given(eng, key + (part,))


            SPARE = [(n, SLABS_IN[n][1] + i, half, k) for n in (4, 5, 6) for i in range(4) for half in range(2) for k in range(KC)]
            HALF_DONE = {}
            FILL_WA, FILL_GATES, FILL_BONUS, FILL_RWKV = 16, 16, 16, 0
            FILL_OM, FILL_X, FILL_ST, FILL_SA = 2, 2, 2, 1
            FILL_ROWS, FILL_A, FILL_A2 = 32, 4, 4


            def spare_products(pe, point, count, banks):
                at = HALF_DONE.get("at", 0)
                for n, f, half, k in SPARE[at:at + count]:
                    if k == 0 and half == 0 and f == SLABS_IN[n][1]:
                        slab_pe(pe, n)
                    c = HALVES[half][1]
                    if k == 0:
                        bk.begin(pe, ("z", f, half), banks[half])
                    ps = psum[:, bk.turn[("z", f, half)][0], :c.stop - c.start]
                    i = f - SLABS_IN[n][1]
                    ins = pe.matmul(ps, wring[:, n % 2, k, i * P:(i + 1) * P], xTv[:, k, c], start=(k == 0), stop=(k == KC - 1))
                    if k == KC - 1:
                        bk.filled(ins, ("z", f, half))
                HALF_DONE["at"] = min(at + count, len(SPARE))
                HALF_DONE[point] = HALF_DONE["at"] // KC


            def finish_half(pe, point, banks, upto=0):
                at = HALF_DONE["at"]
                spare_products(pe, point, max(-at % KC, KC * upto - at), banks)


            with nc.Block() as block:

                @block.tensor
                def _(pe):
                    pe.wait_ge(sig["rows"], 16 * N_ROW_DMAS)
                    ps = bk.begin(pe, ("prow",), 4)
                    bk.filled(pe.transpose(ps[:, :N_ROWS], prow[:N_ROWS, :], ident[:N_ROWS, :N_ROWS]), ("prow",))
                    ps = bk.begin(pe, ("prow2",), 5)
                    bk.filled(pe.transpose(ps[:, :64], prow2[:64, :], ident[:64, :64]), ("prow2",))
                    pe.wait_ge(sig["Sraw"], 16 * NB)
                    for pr in range(2):
                        ps = bk.begin(pe, ("SsT", pr), 6 + pr).rearrange("p (b c) -> p b c", b=4)
                        for b4 in range(4):
                            ins = pe.transpose(ps[:, b4, :], Sraw[:, b4, 2 * pr:2 * pr + 2, :].rearrange("p a b -> p (a b)"), ident)
                        bk.filled(ins, ("SsT", pr))

                    def gemm(n):
                        c0, f0 = SLABS_IN[n]
                        w = slab_pe(pe, n)
                        for i in range(4):
                            x_product(pe, ("z", f0 + i), (f0 + i) % 2, [w[:, k, i * P:(i + 1) * P] for k in range(KC)])

                    gemm(0)
                    gemm(1)
                    pe.wait_ge(sig["small_w"], 16 * N_SMALL_W)
                    pe.wait_ge(sig["xc"], 1)
                    for g in range(2):
                        for f in range(2):
                            product(pe, ("rg", g, f), f, lambda k: X1[:, f, :], [wax[:, g, f, :]])
                    gemm(2)
                    gemm(3)
                    spare_products(pe, "wa", FILL_WA, (0, 1))
                    pe.wait_ge(sig["act_d"], 2)
                    for i in range(4):
                        product(pe, ("wa", i), i % 2, lambda k: z(26)[:, :], [wwa[:, i, :]])
                    for i in range(2):
                        product(pe, ("g2", i), i % 2, lambda k: z(27)[:, :], [wg2[:, i, :]])
                    spare_products(pe, "gates", FILL_GATES, (0, 1))
                    finish_half(pe, "gates", (0, 1))
                    x_product(pe, ("gates",), 0, [wgate[:, k, 0:36] for k in range(KC)])
                    pe.wait_ge(sig["kk2"], 1)
                    for i in range(2):
                        product(pe, ("kk", i), i, lambda k: X5[:, i, :], [const("sum64")])
                    spare_products(pe, "bonus", FILL_BONUS, (0, 1))
                    finish_half(pe, "bonus", (0, 1))
                    pe.wait_ge(sig["rk"], 1)
                    for i in range(2):
                        product(pe, ("bonus", i), i, lambda k: X5[:, i, :], [const("sum64")])
                    spare_products(pe, "rwkv", FILL_RWKV, (0, 1))

                    pe.wait_ge(sig["oc1"], 1)
                    ps = bk.begin(pe, ("orow1",), 6)
                    bk.filled(pe.transpose(ps[:126, :P], oc1[:, :], ident), ("orow1",))

                    for T in range(5):
                        t0, n = TILES[T]
                        pe.wait_ge(sig["dfeat"], 1)
                        for i, pair in enumerate(((X2, X4), (z(ZK_D, 2), z(ZV_D, 2)))):
                            ps = bk.begin(pe, ("dtok", T, i), 4 + i).rearrange("p (a c) -> p a c", a=4)
                            for j in range(2):
                                for pr in range(2):
                                    ins = pe.transpose(ps[:n, 2 * j + pr, :], pair[j][:, pr, t0:t0 + n], ident)
                            bk.filled(ins, ("dtok", T, i))
                        spare_products(pe, ("dpad", T), 2, (0, 1))
                        pe.wait_ge(sig["dpad"], 2 * (T + 1))
                        for i, (left, b) in enumerate(((X4, 6), (z(ZK_D, 2), 6))):
                            if i:
                                spare_products(pe, ("dsc", T), 4, (0, 1))
                            for pr in range(2):
                                ps = bk.begin(pe, ("dsc", T, i, pr), b + pr).rearrange("p (a s t) -> p a s t", a=2, s=2)
                                bk.filled(pe.matmul(ps[:n, :, :, :n], left[:, pr, t0:t0 + n], dpad[:, pr, :, :, :n],
                                                    start=True, stop=True), ("dsc", T, i, pr))
                        levels = (1, 2, 4, 8, 16, 32) if T < 4 else (1, 2)
                        for li, m in enumerate(levels):
                            last = m == levels[-1]
                            spare_products(pe, ("om", T, m), FILL_OM, (0, 1))
                            pe.wait_ge(sig["om"], OM0[T] + li + 1)
                            ps = bk.begin(pe, ("X", T, m), 2).rearrange("p (h t) -> p h t", h=H)
                            om = OmT[:, (OM0[T] + li) % 2]
                            if m > 1:
                                bk.given(pe, ("X", T, 1) if m == 2 else ("DT", T, m // 2))
                            for h in range(H):
                                ins = pe.matmul(ps[:n, h, :n], om[:n, h, :n], (ident if m == 1 else Dm[:, h, :])[:n, :n],
                                                start=True, stop=True)
                            bk.filled(ins, ("X", T, m))
                            if m == 1:
                                continue
                            spare_products(pe, ("X", T, m), FILL_X, (0, 1))
                            bk.given(pe, ("X", T, m))
                            if not last:
                                ps = bk.begin(pe, ("D", T, m), 3).rearrange("p (h t) -> p h t", h=H)
                                for h in range(H):
                                    ins = pe.matmul(ps[:n, h, :n], DmT[:n, h, :n], Xm[:n, h, :n], start=True, stop=True)
                                bk.filled(ins, ("D", T, m))
                            ps = bk.begin(pe, ("DT", T, m), 4).rearrange("p (h t) -> p h t", h=H)
                            for h in range(H):
                                ins = pe.matmul(ps[:n, h, :n], Xm[:n, h, :n], DmT[:n, h, :n], start=True, stop=True)
                            bk.filled(ins, ("DT", T, m))
                        bk.given(pe, ("dtok", T, 1))
                        bk.given(pe, ("dsc", T, 1, 1))
                        ps = bk.begin(pe, ("CV", T), 6)[:, 0:256].rearrange("p (h v) -> p h v", h=H)
                        for h in range(H):
                            ins = pe.matmul(ps[:n, h, :], KM[:n, h // 2, h % 2, 0, :n],
                                            Dtok[:n, 3, h // 2, (h % 2) * HD:(h % 2) * HD + HD], start=True, stop=True)
                        bk.filled(ins, ("CV", T))
                        spare_products(pe, ("inv", T), 1, (0, 1))
                        bk.given(pe, ("DT", T, levels[-1]))
                        if T < 4:
                            ps = bk.begin(pe, ("WK", T), 5)[:, 0:256].rearrange("p (q t) -> p q t", q=2)
                            for h in range(H):
                                par = (h % 2) * HD
                                ins = pe.matmul(ps[par:par + HD, h // 2, :], Dtok[:, 0, h // 2, par:par + HD], DmT[:, h, :],
                                                start=True, stop=True)
                            bk.filled(ins, ("WK", T))
                            bk.given(pe, ("CV", T))
                            ps = bk.begin(pe, ("UV", T), 7)[:, 0:256].rearrange("p (h v) -> p h v", h=H)
                            for h in range(H):
                                ins = pe.matmul(ps[:, h, :], DmT[:, h, :], CV[:, h, :], start=True, stop=True)
                            bk.filled(ins, ("UV", T))
                            spare_products(pe, ("UV", T), 1, (0, 1))
                            bk.given(pe, ("WK", T))
                            bk.given(pe, ("UV", T))
                            for cc in range(2):
                                c0 = cc * 64
                                cn = 2 * T + cc
                                if cn:
                                    spare_products(pe, ("state", cn), FILL_ST, (0, 1))
                                    bk.given(pe, ("st", cn - 1))
                                else:
                                    pe.wait_ge(sig["zeroed"], 1)
                                ps = bk.begin(pe, ("SA", cn), 2)[:, 0:256].rearrange("p (q v) -> p q v", q=2)
                                for pr in range(2):
                                    ins = pe.matmul(ps[c0:c0 + 64, pr, :], WKT[:, pr, c0:c0 + 64], ST[:, pr, :],
                                                    start=True, stop=True)
                                bk.filled(ins, ("SA", cn))
                                spare_products(pe, ("SA", cn), FILL_SA, (0, 1))
                                bk.given(pe, ("SA", cn))
                                ps2 = bk.begin(pe, ("o", cn), 3)[:, 0:128].rearrange("p (q t) -> p q t", q=2)
                                for pr in range(2):
                                    pe.matmul(ps2[:, pr, :], ST[:, pr, :], z(ZR_D + pr)[:, t0 + c0:t0 + c0 + 64],
                                              start=True, stop=False, skip_group_check=True)
                                    for a in range(2):
                                        h = 2 * pr + a
                                        o = ps2[a * HD:a * HD + HD, pr, :]
                                        pe.matmul(o, Dtok[:, 3, pr, a * HD:a * HD + HD], KM[:, pr, a, 1, c0:c0 + 64],
                                                  start=False, stop=False, skip_group_check=True)
                                        ins2 = pe.matmul(o, SAn[:, h, :], BM[:, pr, a, 1, c0:c0 + 64],
                                                         start=False, stop=True, skip_group_check=True)
                                bk.filled(ins2, ("o", cn))
                                ps = bk.begin(pe, ("st", cn), 4)[:, 0:256].rearrange("p (q v) -> p q v", q=2)
                                for pr in range(2):
                                    san = SAn[c0:c0 + 64, 2 * pr:2 * pr + 2, :].rearrange("p a b -> p (a b)")
                                    pe.matmul(ps[:, pr, :], Dtok[c0:c0 + 64, 1, pr, :], san, start=True, stop=False)
                                    ins = pe.matmul(ps[:, pr, :], Dtok[c0:c0 + 64, 2, pr, :], Dtok[c0:c0 + 64, 3, pr, :],
                                                    start=False, stop=True)
                                bk.filled(ins, ("st", cn))
                        else:
                            ps = bk.begin(pe, ("KS",), 2)[:, 0:64].rearrange("p (q t) -> p q t", q=2)
                            for pr in range(2):
                                for a in range(2):
                                    for b in range(NB):
                                        ins = pe.matmul(ps[a * HD:a * HD + HD, pr, TS * b:TS * b + TS], SsT[:, pr, b, :],
                                                        dpad[:, pr, a, 0, TS * b:TS * b + TS], start=True, stop=True)
                            bk.filled(ins, ("KS",))
                            spare_products(pe, ("KS",), 2, (0, 1))
                            bk.given(pe, ("KS",))
                            ps = bk.begin(pe, ("KSt",), 3)[:, 0:256].rearrange("p (q v) -> p q v", q=2)
                            for pr in range(2):
                                ins = pe.transpose(ps[:NS, pr, :], Xm[:, 0, pr * NS:pr * NS + NS], ident)
                            bk.filled(ins, ("KSt",))
                            spare_products(pe, ("KSt",), 2, (0, 1))
                            bk.given(pe, ("KSt",))
                            ps = bk.begin(pe, ("SAs",), 7)[:, 0:256].rearrange("p (h v) -> p h v", h=H)
                            for h in range(H):
                                ins = pe.matmul(ps[:n, h, :], DmT[:n, h, :n], CV[:n, h, :], start=True, stop=True)
                            bk.filled(ins, ("SAs",))
                            spare_products(pe, ("SAs",), 2, (0, 1))
                            bk.given(pe, ("SAs",))
                            ps = bk.begin(pe, ("os",), 3)[:, 0:64].rearrange("p (q t) -> p q t", q=2)
                            for pr in range(2):
                                for a in range(2):
                                    o = ps[a * HD:a * HD + HD, pr, :]
                                    pe.matmul(o, Dtok[:NS, 3, pr, a * HD:a * HD + HD], KM[:NS, pr, a, 1, :NS],
                                              start=True, stop=False, skip_group_check=True)
                                    pe.matmul(o, SAn[:NS, 2 * pr + a, :], BM[:NS, pr, a, 1, :NS],
                                              start=False, stop=False, skip_group_check=True)
                                    for b in range(NB):
                                        ins = pe.matmul(o[:, TS * b:TS * b + TS], SsT[:, pr, b, :],
                                                        dpad[:, pr, a, 1, TS * b:TS * b + TS],
                                                        start=False, stop=(b == NB - 1), skip_group_check=True)
                            bk.filled(ins, ("os",))
                            for pr in range(2):
                                ps = bk.begin(pe, ("sts", pr), 4 + pr)
                                for a in range(2):
                                    h = 2 * pr + a
                                    spare_products(pe, ("SX", h), 3, (0, 1))
                                    pe.wait_ge(sig["SX"], h + 1)
                                    pe.matmul(ps[a * HD:a * HD + HD, :], Dtok[:NS, 1, pr, a * HD:a * HD + HD],
                                              OmT[:NS, h % 2].rearrange("p a b -> p (a b)"), start=True, stop=False)
                                    ins = pe.matmul(ps[a * HD:a * HD + HD, :], Dtok[:NS, 2, pr, a * HD:a * HD + HD],
                                                    (Xm, Dm)[h % 2][:NS].rearrange("p a b -> p (a b)"), start=False, stop=True)
                                    if a == 0:
                                        sig.up(ins, "SXread")
                                bk.filled(ins, ("sts", pr))
                            spare_products(pe, ("Sss",), 3, (0, 1))
                            pe.wait_ge(sig["Sss"], 2)
                            for pr in range(2):
                                ps = bk.begin(pe, ("SsB", pr), 6 + pr).rearrange("p (b c) -> p b c", b=4)
                                for b4 in range(4):
                                    ins = pe.transpose(ps[:, b4, :], SsT[:, pr, 2 * b4:2 * b4 + 2, :].rearrange("p a b -> p (a b)"),
                                                       ident)
                                bk.filled(ins, ("SsB", pr))
                            bk.given(pe, ("st", 7))
                            ps = bk.begin(pe, ("STb",), 2)[:, 0:256].rearrange("p (q v) -> p q v", q=2)
                            for pr in range(2):
                                ins = pe.transpose(ps[:, pr, :], ST[:, pr, :], ident)
                            bk.filled(ins, ("STb",))

                    finish_half(pe, "Dnorm", (0, 1), 8)

                    def head_norm(pre, ht, sq):
                        pe.wait_ge(sig[pre + "h"], 1)
                        for i in range(2):
                            product(pe, (pre + "mu", i), i, lambda k: ht[:, i, :], [const("mean64")])
                        pe.wait_ge(sig[pre + "sq"], 1)
                        for i in range(2):
                            product(pe, (pre + "var", i), i, lambda k: sq[:, i, :], [const("mean64")])

                    head_norm("D", X1, T28)

                    for pre, zk, zv in (("A", ZK_A, ZV_A), ("B", ZK_B, ZV_B)):
                        if pre == "A":
                            spare_products(pe, "rowsA", FILL_ROWS, (0, 1))
                            finish_half(pe, "rowsA", (0, 1))
                            pe.wait_ge(sig["rowsA"], 1)
                            for q, r in enumerate((3, 2)):
                                for pr in range(2):
                                    product(pe, ("bcA", q, pr), pr, lambda k: rows[r][:4, :],
                                            [const("sel_pair", 2, P)[:4, pr, :]])
                        else:
                            finish_half(pe, "rotary", (0, 1), 16)
                            z_wait(pe, 11)
                            for i in range(4):
                                f = (ZQ_B, ZK_B)[i // 2] + i % 2
                                product(pe, ("swap", i), i % 2, lambda k: z(f)[:, :], [const("swap")])
                            pe.wait_ge(sig["rot"], 1)
                        for T in range(5):
                            t0, n = TILES[T]
                            if pre == "B" and T == 0:
                                finish_half(pe, "Bv", (2, 3), 24)
                                z_wait(pe, 15)
                            ps = bk.begin(pe, (pre + "tr", T), 4).rearrange("p (a c) -> p a c", a=4)
                            for j, f in enumerate((zk, zk + 1, zv, zv + 1)):
                                ins = pe.transpose(ps[:n, j, :], z(f)[:, t0:t0 + n], ident)
                            bk.filled(ins, (pre + "tr", T))
                            if pre == "A":
                                ps = bk.begin(pe, ("Agc", T), 5)[:, 0:36]
                                bk.filled(pe.transpose(ps[:n, :], rows[5][0:36, t0:t0 + n], ident[:36, :36]), ("Agc", T))
                                if T == 0:
                                    pe.wait_ge(sig["negG"], 1)
                                ps = bk.begin(pe, ("AG", T), 6).rearrange("p (h t) -> p h t", h=H)
                                for h in range(H):
                                    ins = pe.matmul(ps[:n, h, :n], const("sel_head", H, P)[:4, h, :n], rows[1][:4, t0:t0 + n],
                                                    start=True, stop=True)
                                bk.filled(ins, ("AG", T))
                            pe.wait_ge(sig[pre + "pad"], 2 * (T + 1))
                            ps = bk.begin(pe, (pre + "sc", T), 7).rearrange("p (q a t) -> p q a t", q=2, a=2)
                            for pr in range(2):
                                ins = pe.matmul(ps[:n, pr, :, :n], z(zk + pr)[:, t0:t0 + n], qpad[:, pr, :, :n], start=True, stop=True)
                            bk.filled(ins, (pre + "sc", T))
                            if pre == "A" and T < 4:
                                spare_products(pe, ("Asc", T), FILL_A, (2, 3))
                            bk.given(pe, (pre + "sc", T))
                            bk.given(pe, (pre + "tr", T))
                            if T:
                                pe.wait_ge(sig[pre + "state"], T)
                            else:
                                pe.wait_ge(sig["Azero"], 1)
                            if pre == "B" and T < 4:
                                pe.wait_ge(sig["Bqx"], T + 1)
                            if T == 4:
                                pe.wait_ge(sig[pre + "s"], 16 * 2)
                                pe.wait_ge(sig[pre + "qs"], 1 if pre == "A" else 2)
                            nd = bk.begin(pe, (pre + "nd", T), 0).rearrange("p (w q t) -> p w q t", w=2, q=2)
                            for w in range(2 if pre == "A" else 1):
                                for pr in range(2):
                                    o = nd[:, w, pr, :n]
                                    for a in range(2):
                                        left = (vt[:n, pr, a * HD:a * HD + HD], const("ones")[:n, :])[w]
                                        pe.matmul(o[a * HD:a * HD + HD, :], left, Wm[:n, 2 * pr + a, :n],
                                                  start=True, stop=False, skip_group_check=True)
                                    if T < 4:
                                        state = ((Cb, nb_)[w] if pre == "A" else Rb)[:, pr, :]
                                        right = X2[:, pr, t0:t0 + n] if pre == "A" else qx[:, pr, :]
                                        ins = pe.matmul(o, state, right, start=False, stop=True, skip_group_check=True)
                                    else:
                                        for a in range(2):
                                            for b in range(NB):
                                                state = (Cs if pre == "A" else Rs)[:, pr, b, :]
                                                if w:
                                                    state = n0x[:, pr, b, :]
                                                ins = pe.matmul(o[a * HD:a * HD + HD, TS * b:TS * b + TS], state,
                                                                qspad[:, pr, a, TS * b:TS * b + TS],
                                                                start=False, stop=(b == NB - 1), skip_group_check=True)
                            bk.filled(ins, (pre + "nd", T))
                            if T < 4:
                                ps = bk.begin(pe, (pre + "st", T), 1)
                                for pr in range(2):
                                    ins = pe.matmul(ps[:, pr * P:(pr + 1) * P], kw[:, pr, :], vt[:, pr, :], start=True, stop=True)
                                    if pre == "A":
                                        ins = pe.matmul(ps[:, 256 + pr:257 + pr], kw[:, pr, :], const("ones")[:, 0:1],
                                                        start=True, stop=True)
                                bk.filled(ins, (pre + "st", T))
                                if pre == "A":
                                    spare_products(pe, ("Ast", T), FILL_A2, (2, 3))
                                    if T == 3:
                                        finish_half(pe, ("Ast", T), (2, 3))
                            else:
                                for pr in range(2):
                                    ps = bk.begin(pe, (pre + "sts", pr), 1 + pr)
                                    for a in range(2):
                                        h = 2 * pr + a
                                        pe.wait_ge(sig[pre + "vx"], h + 1)
                                        ins = pe.matmul(ps[a * HD:a * HD + HD, :], kw[:NS, pr, a * HD:a * HD + HD],
                                                        vx2[:NS, h % 2, :, :].rearrange("p a b -> p (a b)"), start=True, stop=True)
                                        if a == 0:
                                            sig.up(ins, pre + "vxread")
                                    bk.filled(ins, (pre + "sts", pr))
                                if pre == "A":
                                    ps = bk.begin(pe, ("Ans",), 3)[:, 0:16].rearrange("p (q b) -> p q b", q=2)
                                    for pr in range(2):
                                        ins = pe.matmul(ps[:, pr, :], kw[:NS, pr, :], const("own")[:NS, :], start=True, stop=True)
                                    bk.filled(ins, ("Ans",))

                        head_norm(pre, z((ZQ_A if pre == "A" else ZQ_B), 2), X2 if pre == "A" else X4)

                    pe.wait_ge(sig["oc2"], 1)
                    ps = bk.begin(pe, ("orow2",), 6)
                    bk.filled(pe.transpose(ps[:36, :P], oc2[:, :], ident), ("orow2",))

                @block.vector
                def _(v):
                    def one(ins):
                        after(v, ins, "v")

                    tt, stt, ts = v.tensor_tensor, v.scalar_tensor_tensor, v.tensor_scalar
                    bk.take(v, ("prow",))
                    bk.give(v.tensor_copy(pc[:, :], psum[:, 4, :N_ROWS]), ("prow",))
                    bk.take(v, ("prow2",))
                    bk.give(v.tensor_copy(pc2[:, :], psum[:, 5, :64]), ("prow2",))
                    bk.given(v, ("prow",))
                    bk.given(v, ("prow2",))
                    v.memset(SAn[:, :, :], 0.0)
                    sig.up(v.memset(ST[:, :, :], 0.0), "zeroed")
                    lam = pc[:, row["rg_lam"]]
                    sig.up(stt(lamc[:, 0, :], lam, -1.0, lam, ALU.mult, ALU.max), "lam")
                    one(ts(lamc[:, 1, :], lam, -1.0, 0.0, ALU.mult, ALU.max))
                    v.wait_ge(sig["lamln"], 1)
                    one(tt(lamc[:, 1, :], lamc[:, 1, :], lamc[:, 0, :], ALU.add))
                    ts(lamc[:, 2, :], lamc[:, 1, :], -8.0, None, ALU.mult)
                    sig.up(ts(lamc[:, 1, :], lamc[:, 1, :], 8.0, None, ALU.mult), "lamc")
                    one(ts(omka[:, :], pc[:, row["rwkv_k_a"]], -1.0, 1.0, ALU.mult, ALU.add))

                    z_wait(v, 19)
                    v.tensor_copy(oc1[:, 72:78].rearrange("p (i f) -> p f i", i=3), z(ZX_C, 2)[:, :, SEQ - 3:SEQ])
                    for f in range(2):
                        v.tensor_copy(oc1[:, 78:126].rearrange("p (b i f) -> p f b i", b=NB, i=3)[:, f], segs(z(ZX_C + f))[:, :, 1:4])
                    for f in range(2):
                        ins = ts(X1[:, f, :], z(ZX_C + f), prm("conv_w", 6 + f), prm("conv_b", f), ALU.mult, ALU.add)
                    for i in range(3):
                        sh = 3 - i
                        one(ins)
                        for f in range(2):
                            w = prm("conv_w", 2 * i + f)
                            x, y = z(ZX_C + f), X1[:, f, :]
                            stt(y[:, sh:SEQ], x[:, 0:SEQ - sh], w, y[:, sh:SEQ], ALU.mult, ALU.add)
                            xs, ysg = segs(x), segs(y)
                            stt(ysg[:, :, sh:TS], xs[:, :, 0:TS - sh], w, ysg[:, :, sh:TS], ALU.mult, ALU.add)
                            ins = stt(ysg[:, :, 0:sh], conv0[:, f, :, i:3], w, ysg[:, :, 0:sh], ALU.mult, ALU.add)
                            if i == 2 and f == 1:
                                sig.up(ins, "xc")
                    v.wait_ge(sig["xc"], 1)
                    v.wait_ge(sig["gg2"], 1)
                    one(ts(T28, T28, 0.07135481282, 1.5957691216, ALU.mult, ALU.add))
                    sig.up(tt(T28, T28, z(ZG_C, 2), ALU.mult), "gg3")
                    for g in range(2):
                        for f in range(2):
                            bk.given(v, ("rg", g, f, 1))
                            bk.given(v, ("rg", g, f, 0))
                    one(tt(X4, X4, X1, ALU.mult))
                    v.wait_ge(sig["ga"], 2)
                    one(tt(X1, X5, X5, ALU.mult))
                    one(stt(X1, X1, 1.0, X2, ALU.add, ALU.mult))
                    sig.up(ts(X1, X1, 1.0e-19, None, ALU.max), "t1")
                    v.wait_ge(sig["sq1"], 1)
                    one(tt(X4, X4, X1, ALU.mult))
                    one(tt(carry[:, :, 0:8], segs(X5)[:, :, :, 0], h0c, ALU.mult))
                    one(tt(segs(X4)[:, :, :, 0], segs(X4)[:, :, :, 0], carry[:, :, 0:8], ALU.add))
                    one(v.memset(segs(X5)[:, :, :, 0], 0.0))
                    for f in range(2):
                        v.tensor_tensor_scan(X2[:, f, 0:SEQ], X5[:, f, 0:SEQ], X4[:, f, 0:SEQ], 0.0, ALU.mult, ALU.add)
                        ins = v.tensor_tensor_scan(X2[:, f, SEQ:], X5[:, f, SEQ:], X4[:, f, SEQ:], 0.0, ALU.mult, ALU.add)
                    one(ins)
                    v.wait_ge(sig["gg4"], 1)
                    one(tt(T28, T28, z(ZG_C, 2), ALU.mult))
                    v.tensor_copy(oc2[:, 0:2], X2[:, :, SEQ - 1])
                    v.tensor_copy(oc2[:, 2:18].rearrange("p (b f) -> p f b", b=NB), segs(X2)[:, :, :, 3])
                    sig.up(tt(z(ZG_C, 2), X2, T28, ALU.mult), "yC")

                    z_wait(v, 27)
                    v.tensor_copy(oc1[:, 0:8], z(20, 8)[:, :, SEQ - 1])
                    sig.up(v.tensor_copy(oc1[:, 8:72].rearrange("p (b f) -> p f b", b=NB), segs(z(20, 8))[:, :, :, 3]), "oc1")
                    for g in range(2):
                        v.wait_ge(sig["delta"], g + 1)
                        v.wait_ge(sig["oc1"], 1)
                        for i in range(4):
                            f = 4 * g + i
                            ins = stt(z(20 + f), z(28 + i), prm("rwkv_mu", f), z(20 + f), ALU.mult, ALU.add)
                        sig.up(ins, "zs")
                    v.wait_ge(sig["zs"], 2)
                    for i in range(2):
                        ins = ts(X4[:, i, :], z(ZK_D + i), prm("rwkv_k_k", i), None, ALU.mult)
                    sig.up(ins, "kk1")
                    def graw_rows(ps, c):
                        ts(graw[0:4, c], ps[0:4], bif[0:4, 0:1], None, ALU.add)
                        return ts(graw[32:36, c], ps[32:36], bif[32:36, 1:2], None, ALU.add)
                    bk.given(v, ("wa", 1, 0))
                    bk.given(v, ("wa", 1, 1))
                    for i in range(2):
                        ins = v.tensor_tensor_scan(X1[:, i, :], const("keep_d"), T28[:, i, :], 0.0, ALU.mult, ALU.add)
                    one(ins)
                    sig.up(tt(X2, X1, T28, ALU.subtract), "S")
                    v.wait_ge(sig["small_w"], 16 * N_SMALL_W)
                    drain(v, ("gates",), graw_rows)
                    for i in range(2):
                        drain(v, ("kk", i), lambda ps, c: ts(X5[:, i, c], ps, 1.0e-24, None, ALU.max))
                    sig.up(v.memset(sm[:, 81:82], 0.0), "ss")
                    v.wait_ge(sig["expd"], 3)
                    v.tensor_copy(epc[:, :, 0:8], T28[:, :, 63:SEQ:64])
                    v.tensor_copy(epc[:, :, 8:16], segs(T28)[:, :, :, 3])
                    v.wait_ge(sig["rn"], 1)
                    one(tt(X4, X4, X5, ALU.mult))
                    tt(X2, X4, X2, ALU.mult)
                    bk.given(v, ("wa", 3, 0))
                    bk.given(v, ("wa", 3, 1))
                    one(tt(X4, X4, T30, ALU.mult))
                    tt(X4, X4, X1, ALU.mult)
                    for i in range(2):
                        ins = ts(T30[:, i, :], T30[:, i, :], prm("rwkv_k_a", i), omka[:, i:i + 1], ALU.mult, ALU.add)
                    one(ins)
                    one(tt(z(ZK_D, 2), z(ZK_D, 2), T30, ALU.mult))
                    for i in range(2):
                        ins = stt(X5[:, i, :], z(ZR_D + i), prm("rwkv_r_k", i), z(ZK_D + i), ALU.mult, ALU.mult)
                    sig.up(ins, "rk")
                    v.wait_ge(sig["rk"], 1)
                    tt(z(ZR_D, 2), z(ZR_D, 2), T28, ALU.mult)
                    sig.up(tt(z(ZK_D, 2), z(ZK_D, 2), X1, ALU.mult), "dfeat")
                    for i in range(2):
                        drain(v, ("bonus", i), lambda ps, c: tt(X5[:, i, c], ps, z(ZV_D + i)[:, c], ALU.mult))
                    bk.take(v, ("orow1",))
                    bk.give(v.tensor_copy(orow1[:126, :], psum[:126, 6, :P]), ("orow1",))

                    for T in range(5):
                        t0, n = TILES[T]
                        mask = const("delta", 2, P) if T < 4 else const("delta_s", 2, NS)
                        for i, dst in enumerate((BM, KM)):
                            for pr in range(2):
                                ps = bk.take(v, ("dsc", T, i, pr)).rearrange("p (a s t) -> p a s t", a=2, s=2)
                                bk.give(tt(dst[:n, pr, :, :, :n], ps[:n, :, :, :n],
                                           mask[:n].unsqueeze(1).broadcast_to([n, 2, 2, n]), ALU.mult), ("dsc", T, i, pr))
                                bk.given(v, ("dsc", T, i, pr))
                        levels = (1, 2, 4, 8, 16, 32) if T < 4 else (1, 2)
                        idb = ident[:n, :n].unsqueeze(1).broadcast_to([n, H, n])
                        for li, m in enumerate(levels):
                            if m == 1:
                                v.wait_ge(sig["om"], OM0[T] + 1)
                                tt(DmT[:n, :, :n], idb, OmT[:n, OM0[T] % 2, :, :n], ALU.subtract)
                                ps = bk.take(v, ("X", T, 1)).rearrange("p (h t) -> p h t", h=H)
                                bk.give(tt(Dm[:n, :, :n], idb, ps[:n, :, :n], ALU.subtract), ("X", T, 1))
                                bk.given(v, ("X", T, 1))
                                continue
                            if m != levels[-1]:
                                ps = bk.take(v, ("D", T, m)).rearrange("p (h t) -> p h t", h=H)
                                bk.give(tt(Dm[:n, :, :n], Dm[:n, :, :n], ps[:n, :, :n], ALU.subtract), ("D", T, m))
                            ps = bk.take(v, ("DT", T, m)).rearrange("p (h t) -> p h t", h=H)
                            bk.give(tt(DmT[:n, :, :n], DmT[:n, :, :n], ps[:n, :, :n], ALU.subtract), ("DT", T, m))
                            bk.given(v, ("DT", T, m))
                        ps = bk.take(v, ("CV", T))
                        bk.give(v.tensor_copy(CV[:n].rearrange("p a b -> p (a b)"), ps[:n, 0:256]), ("CV", T))
                        if T < 4:
                            bk.given(v, ("UV", T))
                            for cc in range(2):
                                c0, cn = 64 * cc, 2 * T + cc
                                ps = bk.take(v, ("SA", cn))
                                bk.give(stt(SAn[c0:c0 + 64].rearrange("p a b -> p (a b)"), ps[c0:c0 + 64, 0:256], -1.0,
                                            UV[c0:c0 + 64].rearrange("p a b -> p (a b)"), ALU.mult, ALU.subtract), ("SA", cn))
                                ps = bk.take(v, ("st", cn))[:, 0:256].rearrange("p (q v) -> p q v", q=2)
                                v.wait_ge(sig["STe"], cn + 1)
                                for pr in range(2):
                                    for a in range(2):
                                        r = slice(a * HD, a * HD + HD)
                                        ins = stt(ST[r, pr, r], ps[r, pr, r], epc[r, pr, cn:cn + 1], STe[r, pr, r], ALU.mult, ALU.add)
                                bk.give(ins, ("st", cn))
                        else:
                            bk.given(v, ("CV", T))
                            ps = bk.take(v, ("KSt",))
                            cv = CV[:n].rearrange("p a b -> p (a b)")
                            bk.give(tt(cv, cv, ps[:n, 0:256], ALU.add), ("KSt",))
                            ps = bk.take(v, ("SAs",))
                            bk.give(ts(SAn[:n].rearrange("p a b -> p (a b)"), ps[:n, 0:256], -1.0, None, ALU.mult), ("SAs",))
                            bk.given(v, ("SAs",))
                            own = const("own")[:n].unsqueeze(2).broadcast_to([n, NB, HD])
                            bk.take(v, ("os",))
                            for h in range(H):
                                if h == 2:
                                    v.wait_ge(sig["SXread"], 1)
                                if h == 3:
                                    bk.take(v, ("sts", 0))
                                tt(OmT[:n, h % 2].rearrange("p a b -> p (a b)").rearrange("p (b v) -> p b v", b=NB),
                                   SAn[:n, h, :].unsqueeze(1).broadcast_to([n, NB, HD]), own, ALU.mult)
                                sig.up(tt((Xm, Dm)[h % 2][:n].rearrange("p a b -> p (a b)").rearrange("p (b v) -> p b v", b=NB),
                                          Dtok[:n, 3, h // 2, (h % 2) * HD:(h % 2) * HD + HD].unsqueeze(1).broadcast_to([n, NB, HD]),
                                          own, ALU.mult), "SX")
                            for pr in range(2):
                                ps = bk.take(v, ("sts", pr)).rearrange("p (b v) -> p b v", b=NB)
                                bk.give(tt(SsT[:, pr], ps, SsT[:, pr], ALU.add), ("sts", pr))
                                bk.given(v, ("sts", pr))
                                sig.up(tt(SsT[:, pr], SsT[:, pr], epc[:, pr, 8:16].unsqueeze(2).broadcast_to([P, NB, HD]), ALU.mult), "Sss")

                    def center(pre, ht):
                        for i in range(2):
                            drain(v, (pre + "mu", i), lambda ps, c: tt(ht[:, i, c], ht[:, i, c], ps, ALU.subtract))
                        sig.up(v.memset(sm[:, 82:83], 0.0), pre + "cen")

                    center("D", X1)
                    v.wait_ge(sig["Drs"], 1)
                    one(tt(X1, X1, T28, ALU.mult))
                    for i in range(2):
                        ins = ts(X1[:, i, :], X1[:, i, :], prm("rwkv_lnx_g", i), prm("rwkv_lnx_b", i), ALU.mult, ALU.add)
                    one(ins)
                    one(tt(X1, X1, X5, ALU.add))
                    sig.up(tt(z(ZR_D, 2), X1, z(26, 2), ALU.mult), "yD")

                    v.wait_ge(sig["Sout"], 16 * (NB + 2))
                    bk.given(v, ("SsB", 1))
                    bk.given(v, ("STb",))
                    one(v.memset(rows[5][0:36, :], 0.0))
                    sig.up(stt(rows[2][32:36, :], graw[32:36, :], -1.0, graw[32:36, :], ALU.mult, ALU.max), "absf")
                    v.memset(Cb, 0.0)
                    v.memset(ncol, 0.0)
                    v.memset(nb_, 0.0)
                    v.memset(qspad, 0.0)
                    sig.up(v.memset(Rb, 0.0), "Azero")
                    v.wait_ge(sig["Azero"], 1)
                    v.wait_ge(sig["lnf"], 1)
                    one(stt(rows[3][0:4, :], graw[32:36, :], 0.0, rows[2][32:36, :], ALU.min, ALU.subtract))
                    one(v.tensor_tensor_scan(rows[4][0:4, :], const("keep_a")[0:4], rows[3][0:4, :], 0.0, ALU.mult, ALU.add))
                    one(tt(rows[5][0:4, :], graw[0:4, :], rows[4][0:4, :], ALU.subtract))
                    one(v.tensor_copy(rows[0][0:4, :], rows[5][0:4, :]))
                    v.wait_ge(sig["m0"], 16)
                    one(tt(segs(rows[0])[0:4, :, 0], segs(rows[0])[0:4, :, 0], m0[0:4, :], ALU.max))
                    G, b_, g_ = rows[1][0:4], rows[4][0:4], rows[5][0:4]
                    for T in range(4):
                        c = slice(T * P, T * P + P)
                        one(v.tensor_tensor_scan(G[:, c], const("drop_a")[0:4, c], rows[0][0:4, c],
                                                 mcar[0:4, T - 1:T] if T else 0.0, ALU.add, ALU.max))
                        e = T * P + P - 1
                        one(tt(mcar[0:4, T:T + 1], b_[:, e:e + 1], G[:, e:e + 1], ALU.add))
                        ts(rows[3][0:4, c], G[:, c], -1.0, mcar[0:4, T - 1:T] if T else 0.0, ALU.mult, ALU.add)
                        ts(rows[5][32:36, c], g_[:, c], G[:, e:e + 1], None, ALU.subtract)
                    one(v.tensor_tensor_scan(G[:, SEQ:], const("drop_a")[0:4, SEQ:], rows[0][0:4, SEQ:], 0.0, ALU.add, ALU.max))
                    Gs = segs(G)
                    tt(segs(rows[3][0:4]), m0[0:4, :].unsqueeze(2).broadcast_to([4, NB, TS]), Gs, ALU.subtract)
                    tt(segs(rows[5][32:36]), segs(g_), Gs[:, :, 3:4].broadcast_to([4, NB, TS]), ALU.subtract)
                    one(tt(rows[2][0:4, :], b_, G, ALU.add))
                    sig.up(v.tensor_copy(m0[0:4, :], segs(rows[2][0:4])[:, :, 3]), "mrows")
                    sig.up(ts(G, G, -1.0, None, ALU.mult), "negG")
                    for pr in range(2):
                        v.tensor_copy(n0x[:, pr], n0c[:, pr, :].unsqueeze(2).broadcast_to([P, NB, HD]))
                    for q in range(2):
                        for pr in range(2):
                            bk.given(v, ("bcA", q, pr, 0))
                            bk.given(v, ("bcA", q, pr, 1))
                    v.tensor_copy(carry[:, :, 0:4], X2[:, :, P - 1:SEQ:P])
                    one(v.tensor_copy(carry[:, :, 4:12], segs(X2)[:, :, :, 3]))
                    one(tt(X2, X2, z(ZQ_A, 2), ALU.mult))
                    for a in range(2):
                        r = slice(a * HD, a * HD + HD)
                        ins = v.tensor_copy(qspad[r, :, a, :], X2[r, :, SEQ:])
                    sig.up(ins, "Aqs")

                    for pre in ("A", "B"):
                        if pre == "B":
                            for i in range(4):
                                f = (ZQ_B, ZK_B)[i // 2] + i % 2
                                drain(v, ("swap", i), lambda ps, c: tt(rows[0][:, c], ps, const("sin")[:, c], ALU.mult))
                                one(tt(z(f), z(f), const("cos"), ALU.mult))
                                ins = tt(z(f), z(f), rows[0], ALU.add)
                                if i < 3:
                                    one(ins)
                            sig.up(ins, "rot")
                        for T in range(5):
                            t0, n = TILES[T]
                            if pre == "A":
                                ps = bk.take(v, ("Agc", T))
                                bk.give(v.tensor_copy(gcol[:n, :], ps[:n, 0:36]), ("Agc", T))
                                bk.given(v, ("Agc", T))
                                weight = gcol[:n, 32:36]
                            else:
                                weight = const("zeta" if T < 4 else "zeta_s")[:n]
                            ps = bk.take(v, (pre + "tr", T)).rearrange("p (h c) -> p h c", h=8)
                            tt(kw[:n].rearrange("p q (a c) -> p (q a) c", a=2), ps[:n, 0:4, :],
                               weight.unsqueeze(2).broadcast_to([n, H, HD]), ALU.mult)
                            bk.give(v.tensor_copy(vt[:n].rearrange("p q (a c) -> p (q a) c", a=2), ps[:n, 4:8, :]), (pre + "tr", T))
                            if pre == "A":
                                ps = bk.take(v, ("AG", T)).rearrange("p (h t) -> p h t", h=H)
                                mask = const("causal" if T < 4 else "causal_s")[:n, :n]
                                for h in range(H):
                                    ins = stt(Em[:n, h, :n], ps[:n, h, :n], gcol[:n, h:h + 1], mask, ALU.add, ALU.min)
                                bk.give(ins, ("AG", T))
                                v.wait_ge(sig["AE"], T + 1)
                                factor = Em[:n, :, :n]
                            else:
                                factor = (const("decay", H, P) if T < 4 else const("decay_s", H, NS))[:n]
                            ps = bk.take(v, (pre + "sc", T)).rearrange("p (h t) -> p h t", h=H)
                            bk.give(tt(Wm[:n, :, :n], ps[:n, :, :n], factor, ALU.mult), (pre + "sc", T))
                            ps = bk.take(v, (pre + "nd", T)).rearrange("p (w q t) -> p w q t", w=2, q=2)
                            if pre == "A":
                                one(stt(rden[:, :, :n], ps[:, 1, :, :n], -1.0, X4[:, :, t0:t0 + n], ALU.mult, ALU.max))
                                one(tt(rden[:, :, :n], ps[:, 1, :, :n], rden[:, :, :n], ALU.max))
                                one(v.reciprocal(rden[:, :, :n], rden[:, :, :n]))
                                ins = tt(z(ZQ_A, 2)[:, :, t0:t0 + n], ps[:, 0, :, :n], rden[:, :, :n], ALU.mult)
                            else:
                                ins = v.tensor_copy(z(ZQ_B, 2)[:, :, t0:t0 + n], ps[:, 0, :, :n])
                            bk.give(ins, (pre + "nd", T))
                            if T < 4:
                                ps = bk.take(v, (pre + "st", T))
                                state = Cb if pre == "A" else Rb
                                for pr in range(2):
                                    if pre == "A":
                                        stt(ncol[:, pr:pr + 1], ncol[:, pr:pr + 1], carry[:, pr, T:T + 1],
                                            ps[:, 256 + pr:257 + pr], ALU.mult, ALU.add)
                                    for a in range(2):
                                        r = slice(a * HD, a * HD + HD)
                                        c = carry[r, pr, T:T + 1] if pre == "A" else const("g_chunk")[r, pr:pr + 1]
                                        ins = stt(state[r, pr, r], state[r, pr, r], c, ps[r, pr * P + a * HD:pr * P + a * HD + HD],
                                                  ALU.mult, ALU.add)
                                bk.give(ins, (pre + "st", T))
                                bk.given(v, (pre + "st", T))
                                if pre == "A":
                                    for pr in range(2):
                                        ins = ts(nb_[:, pr, :], const("sum64"), ncol[:, pr:pr + 1], None, ALU.mult)
                                    if T == 3:
                                        v.tensor_copy(oc2[:, 18:20], ncol)
                                    sig.up(ins, "Astate") if T < 3 else sig.up(v.memset(sm[:, 83:84], 0.0), "Astate")
                                else:
                                    sig.up(v.memset(sm[:, 83:84], 0.0), "Bstate")
                            else:
                                own = const("own")[:n].unsqueeze(2).broadcast_to([n, NB, HD])
                                for h in range(H):
                                    if h == 2:
                                        v.wait_ge(sig[pre + "vxread"], 1)
                                    if h == 3:
                                        bk.take(v, (pre + "sts", 0))
                                    sig.up(tt(vx2[:n, h % 2], vt[:n, h // 2, (h % 2) * HD:(h % 2) * HD + HD].unsqueeze(1)
                                              .broadcast_to([n, NB, HD]), own, ALU.mult), pre + "vx")
                                for pr in range(2):
                                    if pre == "A":
                                        one(tt(Cs[:, pr], Cs[:, pr], carry[:, pr, 4:12].unsqueeze(2).broadcast_to([P, NB, HD]), ALU.mult))
                                    ps = bk.take(v, (pre + "sts", pr)).rearrange("p (b c) -> p b c", b=NB)
                                    if pre == "A":
                                        ins = tt(Cs[:, pr], Cs[:, pr], ps, ALU.add)
                                    else:
                                        ins = stt(Rs[:, pr], Rs[:, pr], const("g_chunk_s")[:, pr:pr + 1], ps, ALU.mult, ALU.add)
                                    bk.give(ins, (pre + "sts", pr))
                                if pre == "A":
                                    ns = oc2[:, 20:36].rearrange("p (b q) -> p q b", b=NB)
                                    one(tt(ns, n0c, carry[:, :, 4:12], ALU.mult))
                                    ps = bk.take(v, ("Ans",))[:, 0:16].rearrange("p (q b) -> p q b", q=2)
                                    bk.give(tt(ns, ns, ps, ALU.add), ("Ans",))
                                    bk.given(v, ("Ans",))
                                    sig.up(v.memset(sm[:, 84:85], 0.0), "oc2")
                                bk.given(v, (pre + "nd", T))
                                sig.up(v.memset(sm[:, 85:86], 0.0), pre + "h")
                        q0 = ZQ_A if pre == "A" else ZQ_B
                        g0 = ZO_A if pre == "A" else ZG_B
                        sq = X2 if pre == "A" else X4
                        center(pre, z(q0, 2))
                        v.wait_ge(sig[pre + "rs"], 1)
                        one(tt(z(q0, 2), z(q0, 2), sq, ALU.mult))
                        for i in range(2):
                            ins = stt(z(g0 + i), z(q0 + i), prm(("mlstm_g" if pre == "A" else "ret_g"), i), z(g0 + i), ALU.mult, ALU.mult)
                        sig.up(ins, "y" + pre)
                    bk.take(v, ("orow2",))
                    bk.give(v.tensor_copy(orow2[:36, :], psum[:36, 6, :P]), ("orow2",))

                @block.scalar
                def _(s):
                    act = s.activation
                    for pr in range(2):
                        ps = bk.take(s, ("SsT", pr))
                        bk.give(act(SsT[:, pr].rearrange("p b v -> p (b v)"), ps, ACT.Copy), ("SsT", pr))
                    s.wait_ge(sig["lam"], 1)
                    after(s, act(lamc[:, 0, :], lamc[:, 0, :], ACT.Exp, scale=-1.0), "s")
                    sig.up(act(lamc[:, 0, :], lamc[:, 0, :], ACT.Ln, bias=1.0), "lamln")

                    def z_tiles(n):
                        f0 = SLABS_IN[n][1]
                        for f in range(f0, f0 + 4):
                            for half, c in HALVES:
                                z_half(f, half, c)

                    def z_half(f, half, c):
                        fn = ACT.Sigmoid if f in (6, 7) else ACT.Silu if f in (14, 15) else ACT.Copy
                        scale = QSCALE if f in (2, 3, 10, 11) else 1.0
                        ps = bk.take(s, ("z", f, half))
                        bk.give(act(z(f)[:, c], ps[:, 0:c.stop - c.start], fn, scale=scale), ("z", f, half))

                    def spare_tiles(point):
                        while spare_read[0] < HALF_DONE[point]:
                            n, f, half, _ = SPARE[KC * spare_read[0]]
                            z_half(f, half, HALVES[half][1])
                            spare_read[0] += 1

                    spare_read = [0]

                    def both(key, dst, fn, **kw_):
                        drain(s, key, lambda ps, c: act(dst[:, c], ps, fn, **kw_))

                    z_tiles(0)
                    z_wait(s, 19)
                    sig.up(act(T28, z(ZG_C, 2), ACT.Square), "gg2")
                    z_tiles(1)
                    for g in range(2):
                        for f in range(2):
                            both(("rg", g, f), (X2, X4)[g][:, f, :], ACT.Sigmoid, bias=prm(("rg_b_a", "rg_b_x")[g], f))
                    s.wait_ge(sig["gg3"], 1)
                    sig.up(act(T28, T28, ACT.Sigmoid), "gg4")
                    s.wait_ge(sig["lamc"], 1)
                    for f in range(2):
                        act(X5[:, f, :], X2[:, f, :], ACT.Exp, scale=lamc[:, 2, f:f + 1])
                    for f in range(2):
                        sig.up(act(X2[:, f, :], X2[:, f, :], ACT.Tanh, scale=lamc[:, 1, f:f + 1]), "ga")
                    z_tiles(2)
                    s.wait_ge(sig["t1"], 1)
                    after(s, act(X1, X1, ACT.Ln), "s")
                    sig.up(act(X1, X1, ACT.Exp, scale=0.5), "sq1")
                    z_tiles(3)
                    s.wait_ge(sig["zs"], 2)
                    sig.up(act(z(26)[0:64, :], z(26)[0:64, :], ACT.Tanh), "act_d")
                    sig.up(act(z(27), z(27), ACT.Sigmoid), "act_d")
                    for i in range(4):
                        if i == 0:
                            spare_tiles("wa")
                        both(("wa", i), z(28 + i), ACT.Sigmoid, bias=prm(("rwkv_w0", "rwkv_a0")[i // 2], i % 2))
                    for i in range(2):
                        both(("g2", i), z(26 + i), ACT.Copy)
                    s.wait_ge(sig["kk1"], 1)
                    sig.up(act(X5, X4, ACT.Square), "kk2")
                    s.wait_ge(sig["S"], 1)
                    sig.up(act(X2, X2, ACT.Exp, scale=-RW_C), "expd")
                    sig.up(act(T28, X1, ACT.Exp, scale=-RW_C), "expd")
                    s.wait_ge(sig["expd"], 2)
                    sig.up(act(X1, X1, ACT.Exp, scale=RW_C), "expd")
                    spare_tiles("gates")
                    s.wait_ge(sig["ss"], 1)
                    after(s, act(X5, X5, ACT.Ln, scale=1048576.0), "s")
                    sig.up(act(X5, X5, ACT.Exp, scale=-0.5, bias=const("eps")[:, 2:3]), "rn")
                    spare_tiles("bonus")
                    spare_tiles("rwkv")

                    for T in range(5):
                        t0, n = TILES[T]
                        for i in range(2):
                            ps = bk.take(s, ("dtok", T, i))
                            bk.give(act(Dtok[:n, 2 * i:2 * i + 2].rearrange("p a q c -> p (a q c)"), ps[:n, :], ACT.Copy), ("dtok", T, i))
                        levels = (1, 2, 4, 8, 16, 32) if T < 4 else (1, 2)
                        spare_tiles(("dsc", T))
                        for m in levels[1:]:
                            spare_tiles(("om", T, m))
                            ps = bk.take(s, ("X", T, m)).rearrange("p (h t) -> p h t", h=H)
                            bk.give(act(Xm[:n, :, :n], ps[:n, :, :n], ACT.Copy), ("X", T, m))
                        spare_tiles(("inv", T))
                        if T < 4:
                            ps = bk.take(s, ("WK", T))
                            bk.give(act(WKT.rearrange("p a b -> p (a b)"), ps[:, 0:256], ACT.Copy), ("WK", T))
                            ps = bk.take(s, ("UV", T))
                            bk.give(act(UV.rearrange("p a b -> p (a b)"), ps[:, 0:256], ACT.Copy), ("UV", T))
                            spare_tiles(("UV", T))
                            for cc in range(2):
                                cn = 2 * T + cc
                                if cn:
                                    spare_tiles(("state", cn))
                                    bk.given(s, ("st", cn - 1))
                                for pr in range(2):
                                    ins = act(STe[:, pr, :], ST[:, pr, :], ACT.Copy, scale=epc[:, pr, cn:cn + 1])
                                sig.up(ins, "STe")
                                ps = bk.take(s, ("o", cn))[:, 0:128].rearrange("p (q t) -> p q t", q=2)
                                bk.give(act(X1[:, :, t0 + 64 * cc:t0 + 64 * cc + 64], ps, ACT.Copy), ("o", cn))
                        else:
                            spare_tiles(("inv", T))
                            ps = bk.take(s, ("KS",))
                            bk.give(act(Xm[:, 0, 0:64], ps[:, 0:64], ACT.Copy), ("KS",))
                            ps = bk.take(s, ("os",))[:, 0:64].rearrange("p (q t) -> p q t", q=2)
                            spare_tiles(("SAs",))
                            bk.give(act(X1[:, :, SEQ:], ps, ACT.Copy), ("os",))
                            bk.given(s, ("os",))
                            sig.up(s.copy(sm[:, 86:87], const("eps")[:, 0:1]), "Dh")
                            spare_tiles(("Sss",))
                            for pr in range(2):
                                ps = bk.take(s, ("SsB", pr)).rearrange("p (b c) -> p b c", b=4)
                                bk.give(act(Sraw[:, :, 2 * pr:2 * pr + 2, :].rearrange("p b a c -> p b (a c)"), ps, ACT.Copy), ("SsB", pr))
                            ps = bk.take(s, ("STb",))[:, 0:256].rearrange("p (q v) -> p q v", q=2)
                            for a in range(2):
                                r = slice(a * HD, a * HD + HD)
                                ins = act(CV[r, 0:2, :], ps[r, :, r], ACT.Copy)
                            bk.give(ins, ("STb",))

                    def norm(pre, ht, sq, eps):
                        s.wait_ge(sig[pre + "cen"], 1)
                        sig.up(act(sq, ht, ACT.Square), pre + "sq")
                        for i in range(2):
                            both((pre + "var", i), sq[:, i, :], ACT.Ln, bias=const("eps")[:, eps:eps + 1])
                        sig.up(act(sq, sq, ACT.Exp, scale=-0.5), pre + "rs")

                    spare_tiles("Dnorm")
                    norm("D", X1, T28, 1)
                    s.wait_ge(sig["absf"], 1)
                    after(s, act(rows[2][32:36, :], rows[2][32:36, :], ACT.Exp, scale=-1.0), "s")
                    sig.up(act(rows[2][32:36, :], rows[2][32:36, :], ACT.Ln, bias=1.0), "lnf")
                    s.wait_ge(sig["mrows"], 1)
                    act(rows[3][0:4, :], rows[3][0:4, :], ACT.Exp)
                    act(rows[2][0:4, :], rows[2][0:4, :], ACT.Exp, scale=-1.0)
                    sig.up(act(rows[5][32:36, :], rows[5][32:36, :], ACT.Exp), "rowsA")
                    spare_tiles("rowsA")
                    for q in range(2):
                        for pr in range(2):
                            both(("bcA", q, pr), (X2, X4)[q][:, pr, :], ACT.Copy)
                    for T in range(5):
                        n = TILES[T][1]
                        bk.given(s, ("AG", T))
                        sig.up(act(Em[:n, :, :n], Em[:n, :, :n], ACT.Exp), "AE")
                        if T < 4:
                            spare_tiles(("Asc", T))
                            spare_tiles(("Ast", T))
                    norm("A", z(ZQ_A, 2), X2, 0)
                    spare_tiles("rotary")
                    spare_tiles("Bv")
                    norm("B", z(ZQ_B, 2), X4, 0)

                @block.gpsimd
                def _(g):
                    def done(ins, name="g"):
                        after(g, ins, name)

                    done(g.memset(wgate, 0.0))
                    done(g.memset(wax, 0.0))
                    done(g.memset(wwa, 0.0), "wzero")
                    done(g.memset(dpad, 0.0))
                    for gr in range(2):
                        if gr == 0:
                            z_wait(g, 23)
                            g.wait_ge(sig["yC"], 1)
                            g.wait_ge(sig["rows"], 16 * N_ROW_DMAS)
                            bk.given(g, ("prow",))
                        else:
                            z_wait(g, 27)
                            g.wait_ge(sig["zs"], 1)
                        a, d = z(20 + 4 * gr, 4), z(28, 4)
                        done(g.tensor_tensor(d[:, :, 1:SEQ], a[:, :, 0:SEQ - 1], a[:, :, 1:SEQ], ALU.subtract))
                        done(g.tensor_scalar(d[:, :, 0:1], a[:, :, 0:1], -1.0, None, ALU.mult))
                        for f in range(4):
                            av, dv = segs(z(20 + 4 * gr + f)), segs(z(28 + f))
                            done(g.tensor_tensor(dv[:, :, 1:TS], av[:, :, 0:TS - 1], av[:, :, 1:TS], ALU.subtract))
                        ins = g.tensor_tensor(segs(d)[:, :, :, 0], sh0[:, 4 * gr:4 * gr + 4, :], segs(a)[:, :, :, 0], ALU.subtract)
                        done(ins, "delta")
                    for T in range(5):
                        t0, n = TILES[T]
                        if T == 0:
                            g.wait_ge(sig["dfeat"], 1)
                        else:
                            bk.given(g, ("dsc", T - 1, 1, 1))
                            bk.given(g, ("dsc", T - 1, 1, 0))
                        for a in range(2):
                            r = slice(a * HD, a * HD + HD)
                            done(g.tensor_copy(dpad[r, :, a, 0, :n], X2[r, :, t0:t0 + n]))
                            done(g.tensor_copy(dpad[r, :, a, 1, :n], z(ZR_D, 2)[r, :, t0:t0 + n]), "dpad")
                        bk.given(g, ("dsc", T, 0, 1))
                        bk.given(g, ("dsc", T, 0, 0))
                        levels = (1, 2, 4, 8, 16, 32) if T < 4 else (1, 2)
                        for li, m in enumerate(levels):
                            if li >= 2:
                                bk.given(g, ("X", T, levels[li - 2]))
                            if li == 0 and T:
                                bk.given(g, ("st", 2 * T - 1))
                            k = (OM0[T] + li) % 2
                            done(g.tensor_tensor(OmT[:n, k].rearrange("p (q a) t -> p q a t", q=2)[:, :, :, :n], BM[:n, :, :, 0, :n],
                                                   const(f"level{m}")[:n, :n].unsqueeze(1).unsqueeze(1).broadcast_to([n, 2, 2, n]),
                                                   ALU.mult), "om")
                    bk.given(g, ("os",))
                    bk.given(g, ("sts", 1))
                    bk.given(g, ("dsc", 4, 1, 1))
                    done(g.memset(qpad, 0.0))
                    for pre, q0 in (("A", ZQ_A), ("B", ZQ_B)):
                        if pre == "B":
                            g.wait_ge(sig["rot"], 1)
                        for T in range(5):
                            t0, n = TILES[T]
                            if T or pre == "B":
                                bk.given(g, (pre + "sc", T - 1) if T else ("Asc", 4))
                            for a in range(2):
                                r = slice(a * HD, a * HD + HD)
                                done(g.tensor_copy(qpad[r, :, a, :n], z(q0, 2)[r, :, t0:t0 + n]), pre + "pad")
                            if pre == "B":
                                if T < 4:
                                    if T:
                                        bk.given(g, ("Bnd", T - 1))
                                    done(g.tensor_tensor(qx, z(q0, 2)[:, :, t0:t0 + n], const("xi", 2, P), ALU.mult), "Bqx")
                                else:
                                    for a in range(2):
                                        r = slice(a * HD, a * HD + HD)
                                        done(g.tensor_tensor(qspad[r, :, a, :], z(q0, 2)[r, :, SEQ:], const("xi_s", 2, NS)[r], ALU.mult), "Bqs")

                @block.sync
                def _(sp):
                    def lay(name):
                        return A[name][bass.ds(l, 1)]

                    for name, (r0, k) in ROWS.items():
                        a = lay(name)
                        if name == "state_rwkv_shift" or name == "state_rglru_h":
                            a = a.rearrange("a b (f p) -> (a b f) p", p=P)
                        elif name == "conv_w":
                            a = a.rearrange("a i (f p) -> (a i f) p", p=P)
                        elif name == "rwkv_r_k":
                            a = a.rearrange("a (f h) d -> (a f) (h d)", h=2)
                        else:
                            a = a.rearrange("a (f p) -> (a f) p", p=P)
                        sp.dma_start(prow[r0:r0 + k, :], a).then_inc(sig["rows"], 16)
                    sp.dma_start(prow2[0:48, :], lay("state_rglru_conv").rearrange("a b i (f p) -> (a b i f) p", p=P)).then_inc(sig["rows"], 16)
                    sp.dma_start(prow2[48:64, :], lay("state_mlstm_n").rearrange("a b (q h) d -> (a b q) (h d)", h=2)).then_inc(sig["rows"], 16)
                    for b in range(NB):
                        src = A["state_rwkv_S"][bass.ds(l, 1), b].rearrange("a h v k -> v (a h) k")
                        sp.dma_start(Sraw[(b % 2) * HD:(b % 2) * HD + HD, b // 2], src).then_inc(sig["Sraw"], 16)

                    def slab(n, src):
                        if n >= 2:
                            slab_read(sp, n - 2)
                        sp.dma_start(wring[:, n % 2], src).then_inc(sig[f"slab{n % 2}"], 16)

                    def in_slab(n):
                        c0 = SLABS_IN[n][0]
                        slab(n, A["w_in"][bass.ds(l, 1), :, c0:c0 + W512].rearrange("a (c p) n -> p (a c) n", p=P))

                    in_slab(0)
                    in_slab(1)
                    sp.wait_ge(sig["wzero"], 1)
                    w = sig["small_w"]
                    gsrc = A["w_in"][bass.ds(l, 1), :, GATE_COL:GATE_COL + 8].rearrange("a (c p) n -> p (a c) n", p=P)
                    sp.dma_start(wgate[:, :, 0:4], gsrc[:, :, 0:4]).then_inc(w, 16)
                    sp.dma_start(wgate[:, :, 32:36], gsrc[:, :, 4:8]).then_inc(w, 16)
                    for i, name in enumerate(("rg_w_a", "rg_w_x")):
                        for a in range(2):
                            r = slice(a * HD, a * HD + HD)
                            src = A[name][bass.ds(l, 1)].rearrange("z (q a) i j -> a i (z q) j", a=2)[a]
                            sp.dma_start(wax[r, i, :, r], src).then_inc(w, 16)
                    for i, name in enumerate(("rwkv_w2", "rwkv_a2")):
                        sp.dma_start(wwa[i * 64:i * 64 + 64, 2 * i:2 * i + 2, :].rearrange("p f c -> p (f c)"),
                                     A[name][bass.ds(l, 1)].rearrange("a k n -> (a k) n")).then_inc(w, 16)
                    sp.dma_start(wg2.rearrange("p f c -> p (f c)"), A["rwkv_g2"][bass.ds(l, 1)].rearrange("a k n -> (a k) n")).then_inc(w, 16)
                    sp.dma_start(bif[0:4, 0:1], A["mlstm_b_i"][bass.ds(l, 1)].rearrange("a h -> h a"), allow_slow_non_contiguous=True).then_inc(w, 16)
                    sp.dma_start(bif[32:36, 1:2], A["mlstm_b_f"][bass.ds(l, 1)].rearrange("a h -> h a"), allow_slow_non_contiguous=True).then_inc(w, 16)
                    sp.dma_start(m0[0:4, :], A["state_mlstm_m"][bass.ds(l, 1)].rearrange("a b h -> h (a b)"),
                                 allow_slow_non_contiguous=True).then_inc(sig["m0"], 16)
                    for n in range(2, 7):
                        in_slab(n)

                    def put(name, src, view, waits):
                        waits()
                        sp.dma_start(view(O[name][bass.ds(l, 1)]), src, allow_slow_non_contiguous=name in ("p_m", "s_m")).then_inc(sig["out1"], 16)
                        N_OUT1.append(1)

                    bk.given(sp, ("orow1",))
                    put("p_shift", orow1[0:8, :], lambda o: o.rearrange("a b (f p) -> (a b f) p", p=P), lambda: None)
                    put("s_shift", orow1[8:72, :], lambda o: o.rearrange("a b (f p) -> (a b f) p", p=P), lambda: None)
                    put("p_conv", orow1[72:78, :], lambda o: o.rearrange("a b i (f p) -> (a b i f) p", p=P), lambda: None)
                    put("s_conv", orow1[78:126, :], lambda o: o.rearrange("a b i (f p) -> (a b i f) p", p=P), lambda: None)
                    bk.given(sp, ("SsB", 1))
                    bk.given(sp, ("STb",))
                    for b in range(NB):
                        sp.dma_start(O["s_S"][bass.ds(l, 1), b].rearrange("a h v k -> v (a h) k"),
                                     Sraw[(b % 2) * HD:(b % 2) * HD + HD, b // 2]).then_inc(sig["Sout"], 16)
                    for a in range(2):
                        sp.dma_start(O["p_S"][bass.ds(l, 1), 0].rearrange("z (q a) v k -> a v (z q) k", a=2)[a],
                                     CV[a * HD:a * HD + HD, 0:2, :]).then_inc(sig["Sout"], 16)
                    sp.wait_ge(sig["yD"], 1)
                    sp.wait_ge(sig["Sout"], 16 * (NB + 2))
                    for name, dst, sem in (("state_mlstm_C", Cs, "As"), ("state_ret", Rs, "Bs")):
                        for pr in range(2):
                            src = A[name][bass.ds(l, 1), :, 2 * pr:2 * pr + 2].rearrange("a b h k v -> (h k) (a b) v")
                            sp.dma_start(dst[:, pr], src).then_inc(sig[sem], 16)
                    out_slab(sp, 7)
                    sp.wait_ge(sig["mrows"], 1)
                    put("p_m", mcar[0:4, 3:4], lambda o: o.rearrange("a b h -> h (a b)"), lambda: None)
                    put("s_m", m0[0:4, :], lambda o: o.rearrange("a b h -> h (a b)"), lambda: None)
                    for pre, st, ss, pn, sn in (("A", Cb, Cs, "p_C", "s_C"), ("B", Rb, Rs, "p_R", "s_R")):
                        sp.wait_ge(sig[pre + "state"], 4)
                        if pre == "B":
                            out_slab(sp, 8)
                        for a in range(2):
                            r = slice(a * HD, a * HD + HD)
                            put(pn, st[r, :, r], lambda o: o[:, 0].rearrange("z (q a) k v -> a k (z q) v", a=2)[a], lambda: None)
                        for pr in range(2):
                            bk.given(sp, (pre + "sts", pr))
                            put(sn, ss[:, pr], lambda o: o[:, :, 2 * pr:2 * pr + 2].rearrange("a b h k v -> (h k) (a b) v"), lambda: None)
                    bk.given(sp, ("orow2",))
                    put("p_h", orow2[0:2, :], lambda o: o.rearrange("a b (f p) -> (a b f) p", p=P), lambda: None)
                    put("s_h", orow2[2:18, :], lambda o: o.rearrange("a b (f p) -> (a b f) p", p=P), lambda: None)
                    put("p_n", orow2[18:20, :], lambda o: o.rearrange("a b (q h) d -> (a b q) (h d)", h=2), lambda: None)
                    put("s_n", orow2[20:36, :], lambda o: o.rearrange("a b (q h) d -> (a b q) (h d)", h=2), lambda: None)
                    sp.wait_ge(sig["out1"], 16 * len(N_OUT1))


            qT = z(0, 8)
            aT = z(8, 8)
            KpT = cols(big, 16 * NT, KC, NMEM)
            Vp = cols(big, 16 * NT + 2048, 2, D)
            Kr = cols(big, 16 * NT + 4096, 2, 2, D)
            Vr = cols(tmp, 2048, 2, 2, D)
            kpt = cols(tmp, 6144, 2, D)
            KbT = [KpT, cols(tmp, 6144, KC, NMEM)]
            memT = cols(tmp, 8192, KC, NMEM)
            Pm = cols(tmp, 8192, H, NMEM)
            pT = cols(tmp, 9216, H, 2, P)
            sTs = cols(tmp, 8192, 2, P)
            Ps = cols(tmp, 8448, NMEM)
            pTs = cols(tmp, 8704, 2, P)
            mx = cols(tmp, 10240, 4)
            sums = cols(tmp, 10244, 4)
            inv = cols(tmp, 10248, 4)
            mems = Kr[:, 0]
            Y = [z(f) for f in (6, 7, 14, 15, 18, 19, 20, 21)]


            def project_tensor(pe, pre, left, slabs, i):
                w = [slab_pe(pe, n) for n in slabs]
                for T in range(5):
                    t0, n = TILES[T]
                    for half in range(2):
                        ps = bk.begin(pe, (pre, T, half), 2 * (T % 2) + half)
                        for k in range(KC):
                            ins = pe.matmul(ps[:n, :], left[k][:, t0:t0 + n], w[half][:, k, :], start=(k == 0), stop=(k == KC - 1))
                        bk.filled(ins, (pre, T, half))
                    if T >= 2:
                        turn_x_tensor(pe, bk, sig, i, T - 2, (4, 5))


            def residual(v, key, T, half):
                n = TILES[T][1]
                x = xk[:n, T, half * W512:half * W512 + W512]
                ps = bk.take(v, key)
                bk.give(v.scalar_tensor_tensor(x, x, ALPHA, ps[:n, :], ALU.mult, ALU.add), key)
                bk.given(v, key)


            with nc.Block() as block:

                @block.tensor
                def _(pe):
                    project_tensor(pe, "wout", Y, (7, 8), 0)
                    pe.wait_ge(sig["mem"], 16)
                    for nt in range(2):
                        for g in range(2):
                            ps = bk.begin(pe, ("memT", nt, g), 6 + g).rearrange("p (c t) -> p c t", c=4)
                            for c in range(4):
                                k = 4 * g + c
                                ins = pe.transpose(ps[:, c, :], mems[:, nt, k * P:(k + 1) * P], ident)
                            bk.filled(ins, ("memT", nt, g))
                    for nt in range(2):
                        for g in range(2):
                            bk.given(pe, ("memT", nt, g))
                    for s_ in range(4):
                        w = slab_pe(pe, 9 + s_)
                        for nt in range(2):
                            ps = bk.begin(pe, ("kv", s_, nt), 6 + nt)
                            for k in range(KC):
                                ins = pe.matmul(ps, memT[:, k, nt * P:(nt + 1) * P], w[:, k, :], start=(k == 0), stop=(k == KC - 1))
                            bk.filled(ins, ("kv", s_, nt))
                        if s_ < 2:
                            turn_x_tensor(pe, bk, sig, 0, 3 + s_, (4, 5))
                        if s_ == 2:
                            for nt in range(2):
                                bk.given(pe, ("kv", 1, nt))
                            for nt in range(2):
                                for g in range(2):
                                    ps = bk.begin(pe, ("KpT", nt, g), 4 + g).rearrange("p (c t) -> p c t", c=4)
                                    for c in range(4):
                                        k = 4 * g + c
                                        ins = pe.transpose(ps[:, c, :], kpt[:, nt, k * P:(k + 1) * P], ident)
                                    bk.filled(ins, ("KpT", nt, g))
                    for g in range(2):
                        bk.given(pe, ("xT", 0, 4, g))
                    for n in (13, 14):
                        w = slab_pe(pe, n)
                        for i in range(4):
                            f = 4 * (n - 13) + i
                            x_product(pe, ("q", f), f % 2, [w[:, k, i * P:(i + 1) * P] for k in range(KC)])
                    for nt in range(2):
                        bk.given(pe, ("kv", 3, nt))
                        bk.given(pe, ("KpT", 1, nt))
                    for f in (6, 7):
                        bk.given(pe, ("q", f, 0))
                        bk.given(pe, ("q", f, 1))

                    def scores(T):
                        t0, n = TILES[T]
                        for hp in range(2):
                            ps = bk.begin(pe, ("s", T, hp), 4 + hp).rearrange("p (a n) -> p a n", a=2)
                            for a in range(2):
                                for c in range(2):
                                    k = 2 * (2 * hp + a) + c
                                    ins = pe.matmul(ps[:, a, :], qT[:, k, t0:t0 + n], KpT[:, k, :], start=(c == 0), stop=(c == 1))
                            bk.filled(ins, ("s", T, hp))

                    scores(0)
                    for T in range(4):
                        t0, n = TILES[T]
                        if T < 3:
                            scores(T + 1)
                        pe.wait_ge(sig["P"], T + 1)
                        for hp in range(2):
                            ps = bk.begin(pe, ("pT", T, hp), 6 + hp).rearrange("p (a n t) -> p a n t", a=2, n=2)
                            for a in range(2):
                                for nt in range(2):
                                    ins = pe.transpose(ps[:, a, nt, :], Pm[:, 2 * hp + a, nt * P:(nt + 1) * P], ident)
                            bk.filled(ins, ("pT", T, hp))
                        for hp in range(2):
                            bk.given(pe, ("pT", T, hp))
                            ps = bk.begin(pe, ("pv", T, hp), hp).rearrange("p (c t) -> p c t", c=4)
                            for c in range(4):
                                h, col = 2 * hp + c // 2, (4 * hp + c) * P
                                for nt in range(2):
                                    ins = pe.matmul(ps[:, c, :], Vp[:, nt, col:col + P], pT[:, h, nt, :], start=(nt == 0), stop=(nt == 1))
                            bk.filled(ins, ("pv", T, hp))
                    sT_ps = bk.begin(pe, ("sT",), 2)[:, 0:256].rearrange("p (n h b t) -> p n h b t", n=2, h=H, b=NB)

                    def turn_keys(b):
                        pe.wait_ge(sig[f"K{b % 2}"], 16 * (b // 2 + 1))
                        for nt in range(2):
                            for g in range(2):
                                key = ("KbT", b, nt, g)
                                ps = bk.begin(pe, key, 4 + 2 * nt + g).rearrange("p (c t) -> p c t", c=4)
                                for c in range(4):
                                    k = 4 * g + c
                                    ins = pe.transpose(ps[:, c, :], Kr[:, b % 2, nt, k * P:(k + 1) * P], ident)
                                bk.filled(ins, key)

                    turn_keys(0)
                    for b in range(NB):
                        if b < NB - 1:
                            turn_keys(b + 1)
                        for nt in range(2):
                            for g in range(2):
                                bk.given(pe, ("KbT", b, nt, g))
                        for h in range(H):
                            for nt in range(2):
                                for c in range(2):
                                    k = 2 * h + c
                                    ins = pe.matmul(sT_ps[:, nt, h, b, :], KbT[b % 2][:, k, nt * P:(nt + 1) * P],
                                                    qT[:, k, SEQ + TS * b:SEQ + TS * b + TS], start=(c == 0), stop=(c == 1))
                        if b == NB - 1:
                            bk.filled(ins, ("sT",))
                        else:
                            sig.up(ins, "KbTread")
                    bk.given(pe, ("sT",))
                    ps = bk.begin(pe, ("ss",), 3)
                    for nt in range(2):
                        ins = pe.transpose(ps[:, nt * P:(nt + 1) * P], sTs[:, nt, :], ident)
                    bk.filled(ins, ("ss",))
                    pe.wait_ge(sig["P"], 5)
                    ps = bk.begin(pe, ("pTs",), 4)
                    for nt in range(2):
                        ins = pe.transpose(ps[:, nt * P:(nt + 1) * P], Ps[:, nt * P:(nt + 1) * P], ident)
                    bk.filled(ins, ("pTs",))
                    bk.given(pe, ("pTs",))
                    ps = bk.begin(pe, ("pvs",), 5)[:, 0:256].rearrange("p (c b t) -> p c b t", c=KC, b=NB)
                    for b in range(NB):
                        pe.wait_ge(sig[f"V{b % 2}"], 16 * (b // 2 + 1))
                        for c in range(KC):
                            for nt in range(2):
                                col = (c // 2) * NS + TS * b
                                ins = pe.matmul(ps[:, c, b, :], Vr[:, b % 2, nt, c * P:(c + 1) * P], pTs[:, nt, col:col + TS],
                                                start=(nt == 0), stop=(nt == 1))
                        if b < NB - 1:
                            sig.up(ins, "Vread")
                    bk.filled(ins, ("pvs",))
                    for hp in range(2):
                        bk.given(pe, ("pv", 3, hp))
                    bk.given(pe, ("pvs",))
                    project_tensor(pe, "wo", [aT[:, c, :] for c in range(KC)], (15, 16), 1)
                    turn_x_tensor(pe, bk, sig, 1, 3, (4, 5))
                    turn_x_tensor(pe, bk, sig, 1, 4, (4, 5))

                @block.vector
                def _(v):
                    v.wait_ge(sig["xres"], 32)
                    for T in range(5):
                        for half in range(2):
                            residual(v, ("wout", T, half), T, half)
                        ln_vector(v, sig, 0, T)
                    for T in range(4):
                        for hp in range(2):
                            ps = bk.take(v, ("s", T, hp)).rearrange("p (a n) -> p a n", a=2)
                            if T and hp == 0:
                                v.wait_ge(sig["P"], T)
                            sig.up(v.tensor_reduce(mx[:, 2 * hp:2 * hp + 2], ps, AX.X, ALU.max, negate=True), "max")
                        v.wait_ge(sig["exp"], H * (T + 1))
                        after(v, v.reciprocal(inv, sums), "v")
                        sig.up(v.tensor_tensor(Pm, Pm, inv.unsqueeze(2).broadcast_to([P, H, NMEM]), ALU.mult), "P")
                        for hp in range(2):
                            ps = bk.take(v, ("pT", T, hp))
                            bk.give(v.tensor_copy(pT[:, 2 * hp:2 * hp + 2].rearrange("p a n t -> p (a n t)"), ps), ("pT", T, hp))
                    for b in range(NB):
                        if b >= 2:
                            v.wait_ge(sig["KbTread"], b - 1)
                        for g in range(2):
                            ps = bk.take(v, ("KbT", b, 0, g)).rearrange("p (c t) -> p c t", c=4)
                            bk.give(v.tensor_copy(KbT[b % 2][:, 4 * g:4 * g + 4, 0:P], ps), ("KbT", b, 0, g))
                    ps = bk.take(v, ("sT",))
                    bk.give(v.tensor_copy(sTs.rearrange("p n t -> p (n t)"), ps[:, 0:256]), ("sT",))
                    ps = bk.take(v, ("ss",))
                    sig.up(v.tensor_reduce(mx[:, 0:1], ps[:, 0:256], AX.X, ALU.max, negate=True), "max")
                    v.wait_ge(sig["exp"], 17)
                    after(v, v.reciprocal(inv[:, 0:1], sums[:, 0:1]), "v")
                    sig.up(v.tensor_scalar(Ps, Ps, inv[:, 0:1], None, ALU.mult), "P")
                    ps = bk.take(v, ("pTs",))
                    bk.give(v.tensor_copy(pTs.rearrange("p n t -> p (n t)"), ps[:, 0:256]), ("pTs",))
                    for T in range(5):
                        for half in range(2):
                            residual(v, ("wo", T, half), T, half)
                        ln_vector(v, sig, 1, T)

                @block.scalar
                def _(s):
                    act = s.activation
                    for T in range(3):
                        ln_scalar(s, sig, 0, T)

                    for T in (3, 4):
                        ln_scalar(s, sig, 0, T)
                        turn_x_scalar(s, bk, sig, 0, T - 3)
                    turn_x_scalar(s, bk, sig, 0, 2)
                    for nt in range(2):
                        for g in range(2):
                            ps = bk.take(s, ("memT", nt, g)).rearrange("p (c t) -> p c t", c=4)
                            bk.give(act(memT[:, 4 * g:4 * g + 4, nt * P:(nt + 1) * P], ps, ACT.Copy), ("memT", nt, g))
                    for s_ in range(4):
                        dst = kpt if s_ < 2 else Vp
                        for nt in range(2):
                            ps = bk.take(s, ("kv", s_, nt))
                            bk.give(act(dst[:, nt, (s_ % 2) * W512:(s_ % 2) * W512 + W512], ps, ACT.Copy), ("kv", s_, nt))
                        if s_ < 2:
                            turn_x_scalar(s, bk, sig, 0, 3 + s_)
                        if s_ == 2:
                            for nt in range(2):
                                for g in range(2):
                                    ps = bk.take(s, ("KpT", nt, g)).rearrange("p (c t) -> p c t", c=4)
                                    bk.give(act(KpT[:, 4 * g:4 * g + 4, nt * P:(nt + 1) * P], ps, ACT.Copy), ("KpT", nt, g))
                    for f in range(KC):
                        for part, c in HALVES:
                            ps = bk.take(s, ("q", f, part))
                            bk.give(act(qT[:, f, c], ps[:, 0:c.stop - c.start], ACT.Copy, scale=XSCALE), ("q", f, part))
                    for T in range(4):
                        t0, n = TILES[T]
                        if T:
                            for hp in range(2):
                                bk.take(s, ("pT", T - 1, hp))
                        for hp in range(2):
                            s.wait_ge(sig["max"], 2 * T + hp + 1)
                            ps = bk.take(s, ("s", T, hp)).rearrange("p (a n) -> p a n", a=2)
                            for a in range(2):
                                h = 2 * hp + a
                                ins = act(Pm[:, h, :], ps[:, a, :], ACT.Exp, bias=mx[:, h:h + 1], accum_out=sums[:, h:h + 1])
                                if a == 0:
                                    sig.up(ins, "exp")
                            bk.give(ins, ("s", T, hp))
                            bk.given(s, ("s", T, hp))
                            sig.up(s.copy(sm[:, 86:87], const("eps")[:, 0:1]), "exp")
                        for hp in range(2):
                            ps = bk.take(s, ("pv", T, hp)).rearrange("p (c t) -> p c t", c=4)
                            bk.give(act(aT[:, 4 * hp:4 * hp + 4, t0:t0 + n], ps, ACT.Copy), ("pv", T, hp))
                    for b in range(NB):
                        if b >= 2:
                            s.wait_ge(sig["KbTread"], b - 1)
                        for g in range(2):
                            ps = bk.take(s, ("KbT", b, 1, g)).rearrange("p (c t) -> p c t", c=4)
                            bk.give(act(KbT[b % 2][:, 4 * g:4 * g + 4, P:2 * P], ps, ACT.Copy), ("KbT", b, 1, g))
                    s.wait_ge(sig["max"], 9)
                    ps = bk.take(s, ("ss",))
                    bk.give(act(Ps, ps[:, 0:256], ACT.Exp, bias=mx[:, 0:1], accum_out=sums[:, 0:1]), ("ss",))
                    bk.given(s, ("ss",))
                    sig.up(s.copy(sm[:, 86:87], const("eps")[:, 0:1]), "exp")
                    ps = bk.take(s, ("pvs",))[:, 0:256].rearrange("p (c t) -> p c t", c=KC)
                    bk.give(act(aT[:, :, SEQ:], ps, ACT.Copy), ("pvs",))
                    for T in range(3):
                        ln_scalar(s, sig, 1, T)
                    for T in (3, 4):
                        ln_scalar(s, sig, 1, T)
                        turn_x_scalar(s, bk, sig, 1, T - 3)
                    for T in (2, 3, 4):
                        turn_x_scalar(s, bk, sig, 1, T)

                @block.gpsimd
                def _(g):
                    for i in range(2):
                        for T in range(5):
                            ln_pool(g, sig, i, T)

                @block.sync
                def _(sp):
                    sp.dma_start(xk[:, 0:4, :], yp).then_inc(sig["xres"], 16)
                    sp.dma_start(xk[:NS, 4, :], ys).then_inc(sig["xres"], 16)
                    ln_params(sp, sig, A["ln1_g"][bass.ds(l, 1)].rearrange("a n -> (a n)"), A["ln1_b"][bass.ds(l, 1)].rearrange("a n -> (a n)"))
                    sp.dma_start(mems, A["mem_prompt"].rearrange("a (t p) d -> p (a t) d", p=P)).then_inc(sig["mem"], 16)
                    out_slab(sp, 9)
                    out_slab(sp, 10)

                    def kv_load(name, dst, b, s_):
                        sp.dma_start(dst[:, b % 2], A[name][bass.ds(l, 1), b].rearrange("a (t p) h d -> p (a t) (h d)", p=P)).then_inc(sig[f"{s_}{b % 2}"], 16)

                    kv_load("cache_mem_v", Vr, 0, "V")
                    kv_load("cache_mem_v", Vr, 1, "V")
                    out_slab(sp, 11)
                    out_slab(sp, 12)
                    for nt in range(2):
                        for g in range(2):
                            bk.take(sp, ("memT", nt, g))
                    kv_load("cache_mem_k", Kr, 0, "K")
                    kv_load("cache_mem_k", Kr, 1, "K")
                    sp.wait_ge(sig["ln_done"], 5)
                    ln_params(sp, sig, A["ln2_g"][bass.ds(l, 1)].rearrange("a n -> (a n)"), A["ln2_b"][bass.ds(l, 1)].rearrange("a n -> (a n)"))
                    for nt in range(2):
                        bk.given(sp, ("kv", 1, nt))
                    sp.dma_start(O["p_mem_k"][bass.ds(l, 1)].rearrange("a b (t p) h d -> p (a b t) (h d)", p=P), kpt).then_inc(sig["memout"], 16)
                    out_slab(sp, 13)
                    out_slab(sp, 14)
                    for nt in range(2):
                        bk.given(sp, ("kv", 3, nt))
                    sp.dma_start(O["p_mem_v"][bass.ds(l, 1)].rearrange("a b (t p) h d -> p (a b t) (h d)", p=P), Vp).then_inc(sig["memout"], 16)
                    out_slab(sp, 15)
                    out_slab(sp, 16)
                    for b in range(2, NB):
                        for nt in range(2):
                            for g in range(2):
                                bk.take(sp, ("KbT", b - 2, nt, g))
                        kv_load("cache_mem_k", Kr, b, "K")
                    for b in range(2, NB):
                        sp.wait_ge(sig["Vread"], b - 1)
                        kv_load("cache_mem_v", Vr, b, "V")
                    sp.wait_ge(sig["memout"], 32)
                    out_slab(sp, 17)
                    out_slab(sp, 18)

            hT = cols(big, 0, FC, NT)
            with nc.Block() as block:

                @block.tensor
                def _(pe):
                    for g in range(2):
                        bk.given(pe, ("xT", 1, 4, g))
                    for n in range(8):
                        w = slab_pe(pe, 17 + n)
                        for i in range(4):
                            f = 4 * n + i
                            x_product(pe, ("up", f), f % 2, [w[:, k, i * P:(i + 1) * P] for k in range(KC)])
                    for half in range(2):
                        for ks in range(4):
                            w = slab_pe(pe, 25 + 4 * half + ks)
                            if half == 0:
                                pe.wait_ge(sig["h"], 8 * (ks + 1))
                            for T in range(5):
                                t0, n = TILES[T]
                                key = ("down", half, T)
                                if ks == 0:
                                    bk.begin(pe, key, T if half == 0 else (5 + T) % 8)
                                ps = psum[:, bk.turn[key][0], :]
                                for k in range(KC):
                                    ins = pe.matmul(ps[:n, :], hT[:, ks * KC + k, t0:t0 + n], w[:, k, :],
                                                    start=(ks == 0 and k == 0), stop=(ks == 3 and k == KC - 1))
                                if ks == 3:
                                    bk.filled(ins, key)
                                    if half == 1 and T >= 2:
                                        turn_x_tensor(pe, bk, sig, 2, T - 2, (2, 3))
                                elif T == 4:
                                    sig.up(ins, "downread")
                    turn_x_tensor(pe, bk, sig, 2, 3, (2, 3))
                    turn_x_tensor(pe, bk, sig, 2, 4, (2, 3))

                @block.vector
                def _(v):
                    for T in range(5):
                        residual(v, ("down", 0, T), T, 0)
                    for T in range(5):
                        residual(v, ("down", 1, T), T, 1)
                        ln_vector(v, sig, 2, T)

                @block.scalar
                def _(s):
                    for f in range(FC):
                        for part, c in HALVES:
                            ps = bk.take(s, ("up", f, part))
                            bk.give(s.activation(hT[:, f, c], ps[:, 0:c.stop - c.start], ACT.Relu), ("up", f, part))
                            bk.given(s, ("up", f, part))
                        sig.up(s.activation(hT[:, f, :], hT[:, f, :], ACT.Square), "h")
                    for T in range(3):
                        ln_scalar(s, sig, 2, T)
                    for T in (3, 4):
                        ln_scalar(s, sig, 2, T)
                        turn_x_scalar(s, bk, sig, 2, T - 3)
                    for T in (2, 3, 4):
                        turn_x_scalar(s, bk, sig, 2, T)

                @block.gpsimd
                def _(g):
                    for T in range(5):
                        ln_pool(g, sig, 2, T)

                @block.sync
                def _(sp):
                    ln_params(sp, sig, A["ln3_g"][bass.ds(l, 1)].rearrange("a n -> (a n)"), A["ln3_b"][bass.ds(l, 1)].rearrange("a n -> (a n)"))
                    for n in range(19, 33):
                        out_slab(sp, n)
                    sp.wait_ge(sig["ln_done"], 15)
                    sp.dma_start(yp, xk[:, 0:4, :]).then_inc(sig["y"], 16)
                    sp.dma_start(ys, xk[:NS, 4, :]).then_inc(sig["y"], 16)
                    sp.wait_ge(sig["y"], 32)

            nc.multi_engine_barrier(engines, sems_to_clear=sig.numbers())


_OUTS = [("y_prompt", (1, SEQ, D)), ("y_sample", (NB, TS, D)),
         ("p_C", (DEPTH, 1, H, HD, HD)), ("p_n", (DEPTH, 1, H, HD)), ("p_m", (DEPTH, 1, H)),
         ("p_R", (DEPTH, 1, H, HD, HD)), ("p_h", (DEPTH, 1, 256)), ("p_conv", (DEPTH, 1, 3, 256)),
         ("p_S", (DEPTH, 1, H, HD, HD)), ("p_shift", (DEPTH, 1, D)),
         ("p_mem_k", (DEPTH, 1, NMEM, H, 256)), ("p_mem_v", (DEPTH, 1, NMEM, H, 256)),
         ("s_C", (DEPTH, NB, H, HD, HD)), ("s_n", (DEPTH, NB, H, HD)), ("s_m", (DEPTH, NB, H)),
         ("s_R", (DEPTH, NB, H, HD, HD)), ("s_h", (DEPTH, NB, 256)), ("s_conv", (DEPTH, NB, 3, 256)),
         ("s_S", (DEPTH, NB, H, HD, HD)), ("s_shift", (DEPTH, NB, D))]


def kernel(**inputs):
    import numpy as np
    import concourse.bacc as bacc
    from concourse.bass_utils import run_bass_kernel_spmd

    nc = bacc.Bacc("TRN2", target_bir_lowering=False, num_devices=1)
    arrays, ins, outs = {}, {}, {}
    for name, a in inputs.items():
        a = np.ascontiguousarray(a)
        arrays["in_" + name] = a
        ins[name] = nc.dram_tensor("in_" + name, a.shape, F32, kind="ExternalInput").ap()
    table, where = constants()
    arrays["in_table"] = table
    t = nc.dram_tensor("in_table", table.shape, F32, kind="ExternalInput").ap()
    for name, shape in _OUTS:
        outs[name] = nc.dram_tensor("out_" + name, shape, F32, kind="ExternalOutput").ap()
    build(nc, ins, outs, t, where)
    r = run_bass_kernel_spmd(nc, [arrays], core_ids=[0])
    return tuple(r.results[0]["out_" + name] for name, _ in _OUTS)
```

```python
from contextlib import ExitStack

import concourse.bass as bass
from concourse import mybir

F32 = mybir.dt.float32
ALU = mybir.AluOpType
ACT = mybir.ActivationFunctionType
AX = mybir.AxisListType

P = 128
D = 1024
KC = D // P
DEPTH = 2
SEQ = 512
NB = 8
TS = 4
NS = NB * TS
NT = SEQ + NS
H = 4
HD = 64
FF = 4 * D
FC = FF // P
NMEM = 256
W512 = 512
W256 = 256
N_IN = 3592
ALPHA = (2.0 * DEPTH) ** 0.25
LN_EPS = 1e-5
HEAD_EPS = 1e-6
RW_EPS = 64e-5
QSCALE = HD ** -0.5
XSCALE = 256 ** -0.5
RW_C = 0.6065306597126334
NEG = -1.0e30
TMP = 11712
TILES = [(0, 128), (128, 128), (256, 128), (384, 128), (SEQ, NS)]

ZQ_A, ZK_A, ZV_A, ZO_A = 0, 2, 4, 6
ZQ_B, ZK_B, ZV_B, ZG_B = 8, 10, 12, 14
ZX_C, ZG_C = 16, 18
ZR_D, ZK_D, ZV_D, ZWA_D, ZG_D = 20, 22, 24, 26, 27
SLABS_IN = [(2056, 16), (2568, 20), (3080, 24), (0, 0), (512, 4), (1032, 8), (1544, 12)]
GATE_COL = 1024

ROWS = {}
for _n, _k in (("mlstm_g", 2), ("ret_g", 2), ("conv_w", 8), ("conv_b", 2), ("rg_b_a", 2), ("rg_b_x", 2),
               ("rg_lam", 2), ("rwkv_mu", 8), ("rwkv_w0", 2), ("rwkv_a0", 2), ("rwkv_k_k", 2), ("rwkv_k_a", 2),
               ("rwkv_r_k", 2), ("rwkv_lnx_g", 2), ("rwkv_lnx_b", 2), ("state_rglru_h", 16),
               ("state_rwkv_shift", 64)):
    ROWS[_n] = (sum(k for _, k in ROWS.values()), _k)
N_ROWS = sum(k for _, k in ROWS.values())


def constants():
    import numpy as np
    p = np.arange(P)
    c = {}
    c["ident"] = np.eye(P)
    c["eps"] = np.tile(np.array([HEAD_EPS, RW_EPS, 10.0 * np.log(2.0), LN_EPS]), (P, 1))
    same64 = (p[:, None] // 64 == p[None, :] // 64)
    c["sum64"] = same64
    c["mean64"] = same64 / 64.0
    swap = np.zeros((P, P))
    for m in range(P):
        d = m % 64
        swap[m + 32 if d < 32 else m - 32, m] = -1.0 if d < 32 else 1.0
    c["swap"] = swap
    inv = (10000.0 ** (-np.arange(32, dtype=np.float32) / 32)).astype(np.float32)
    pos = np.concatenate([np.arange(SEQ), 4096 + np.tile(np.arange(TS), NB)]).astype(np.float32)
    ang = (pos[None, :] * inv[p % 32][:, None]).astype(np.float32)
    c["cos"] = np.cos(ang)
    c["sin"] = np.sin(ang)
    j, t = p[:, None], p[None, :]
    js, ts = j[:NS], t[:, :NS]
    seq_same = (js // TS == ts // TS)
    c["causal"] = np.where(j <= t, 0.0, NEG)
    cs = np.full((P, NS), NEG)
    cs[:NS] = np.where(seq_same & (js <= ts), 0.0, NEG)
    c["causal_s"] = cs
    lg = np.log(1.0 - 2.0 ** (-5.0 - np.arange(H, dtype=np.float32))).astype(np.float64)
    dm = np.where((j <= t)[:, None, :], np.exp(np.maximum(t - j, 0)[:, None, :] * lg[None, :, None]), 0.0)
    c["decay"] = dm.reshape(P, H * P)
    ds = np.zeros((P, H, NS))
    ds[:NS] = np.where((seq_same & (js <= ts))[:, None, :],
                       np.exp(np.maximum(ts - js, 0)[:, None, :] * lg[None, :, None]), 0.0)
    c["decay_s"] = ds.reshape(P, H * NS)
    idx = np.concatenate([np.arange(SEQ) % P, np.tile(np.arange(TS), NB)])
    hp = 2 * np.arange(2)[None, :] + (p // 64)[:, None]
    c["xi"] = np.exp((idx + 1.0)[None, None, :] * lg[hp][:, :, None])[:, :, :P]
    c["xi_s"] = np.exp((idx + 1.0)[None, None, :] * lg[hp][:, :, None])[:, :, SEQ:]
    c["zeta"] = np.exp((P - 1.0 - p)[:, None] * lg[None, :])
    c["zeta_s"] = np.exp((TS - 1.0 - p % TS)[:, None] * lg[None, :])
    c["g_chunk"] = np.exp(P * lg[hp])
    c["g_chunk_s"] = np.exp(TS * lg[hp])
    same = (j // 64 == t // 64)
    c["delta"] = np.stack([same & (j < t), same & (j <= t)], 1)
    dsm = np.zeros((P, 2, NS))
    dsm[:NS] = np.stack([seq_same & (js < ts), seq_same & (js <= ts)], 1)
    c["delta_s"] = dsm
    for m in (1, 2, 4, 8, 16, 32):
        c[f"level{m}"] = (j // (2 * m) == t // (2 * m)) & (j % (2 * m) < m) & (t % (2 * m) >= m)
    c["own"] = (p[:, None] // TS == np.arange(NB)[None, :])
    sp = np.zeros((P, 2, P))
    sg = np.zeros((P, H, P))
    for h in range(H):
        for pr in range(2):
            sp[h, pr] = (h == 2 * pr + p // 64)
        sg[h, h] = 1.0
    c["sel_pair"] = sp
    c["sel_head"] = sg
    r128 = np.ones(NT)
    r128[0:SEQ:P] = 0
    r128[SEQ::TS] = 0
    c["keep_a"] = np.tile(r128, (P, 1))
    md = np.zeros(NT)
    md[SEQ::TS] = NEG
    c["drop_a"] = np.tile(md, (P, 1))
    r64 = np.ones(NT)
    r64[0:SEQ:64] = 0
    r64[SEQ::TS] = 0
    c["keep_d"] = np.tile(r64, (P, 1))
    c["ones"] = np.ones((P, 64))
    table, at, n = [], {}, 0
    for k, a in c.items():
        a = np.asarray(a, np.float32).reshape(P, -1)
        at[k] = (n, a.shape[1])
        table.append(a)
        n += a.shape[1]
    return np.ascontiguousarray(np.concatenate(table, 1)), at


class Signals:

    def __init__(self, nc, ctx, prefix):
        self.nc, self.ctx, self.prefix = nc, ctx, prefix
        self.sems, self.count = {}, {}

    def __getitem__(self, name):
        if name not in self.sems:
            self.sems[name] = self.ctx.enter_context(self.nc.semaphore(self.prefix + name))
            self.count[name] = 0
        return self.sems[name]

    def up(self, ins, name, by=1):
        ins.then_inc(self[name], by)
        self.count[name] += by
        return self.count[name]

    def numbers(self):
        n = [s.num for s in self.sems.values()]
        return range(min(n), max(n) + 1)


class Banks:

    def __init__(self, sig, psum):
        self.sig, self.psum = sig, psum
        self.uses = [0] * 8
        self.turn = {}
        for b in range(8):
            sig[f"full{b}"], sig[f"free{b}"]

    def begin(self, pe, key, b):
        assert key not in self.turn, key
        if self.uses[b]:
            pe.wait_ge(self.sig[f"free{b}"], self.uses[b])
        self.uses[b] += 1
        self.turn[key] = (b, self.uses[b])
        return self.psum[:, b, :]

    def filled(self, ins, key):
        ins.then_inc(self.sig[f"full{self.turn[key][0]}"], 1)

    def take(self, eng, key):
        b, n = self.turn[key]
        eng.wait_ge(self.sig[f"full{b}"], n)
        return self.psum[:, b, :]

    def give(self, ins, key):
        ins.then_inc(self.sig[f"free{self.turn[key][0]}"], 1)

    def given(self, eng, key):
        b, n = self.turn[key]
        eng.wait_ge(self.sig[f"free{b}"], n)


def build(nc, A, O, table, where):
    with ExitStack() as ctx:
        def sb(name, cols):
            return ctx.enter_context(nc.sbuf_tensor(name, [P, cols], F32))

        con = sb("con", table.shape[1])
        big = sb("big", 32 * NT)
        xT = sb("xT", KC * NT)
        xtok = sb("xtok", 5 * D)
        ring = sb("ring", 2 * KC * W512)
        tmp = sb("tmp", TMP)
        sm = sb("sm", 96)
        psum = ctx.enter_context(nc.psum_tensor("psum", [P, 8, 512], F32))

        def const(name, *shape):
            a, n = where[name]
            v = con[:, a:a + n]
            if len(shape) == 2:
                v = v.rearrange("p (a b) -> p a b", a=shape[0])
            return v

        def cols(t, at, *shape):
            n = 1
            for s in shape:
                n *= s
            v = t[:, at:at + n]
            if len(shape) == 2:
                v = v.rearrange("p (a b) -> p a b", a=shape[0])
            if len(shape) == 3:
                v = v.rearrange("p (a b c) -> p a b c", a=shape[0], b=shape[1])
            if len(shape) == 4:
                v = v.rearrange("p (a b c d) -> p a b c d", a=shape[0], b=shape[1], c=shape[2])
            return v

        def z(f, n=1):
            v = big[:, f * NT:(f + n) * NT]
            return v if n == 1 else v.rearrange("p (n t) -> p n t", n=n)

        def bc(ap, shape):
            return ap.broadcast_to(shape)

        xTv = cols(xT, 0, KC, NT)
        xk = cols(xtok, 0, 5, D)
        wring = cols(ring, 0, 2, KC, W512)
        stats = cols(sm, 0, 5, 2, 6)
        mv = cols(sm, 60, 5, 2)
        rstd = cols(sm, 70, 5)
        ident = const("ident")
        lnp = cols(tmp, 0, 2, D)
        yp = O["y_prompt"].rearrange("a (t p) d -> p (a t) d", p=P)
        ys = O["y_sample"].rearrange("b t d -> (b t) d")

        def ln_vector(v, sig, i, T):
            n = TILES[T][1]
            x = xk[:n, T, :]
            for half in range(2):
                ins = v.bn_stats(stats[:n, T, half, :], x[:, half * 512:half * 512 + 512])
            v.wait_ge(sig["v"], sig.up(ins, "v"))
            v.wait_ge(sig["ln_var"], sig.up(v.bn_aggr(mv[:n, T, :], stats[:n, T, :, :].rearrange("p a b -> p (a b)")), "ln_var"))
            if T == 0:
                v.wait_ge(sig["ln_param"], 32 * (i + 1))
            v.wait_ge(sig["v"], sig.up(v.scalar_tensor_tensor(x, x, mv[:n, T, 0:1], lnp[:n, 0, :], ALU.subtract, ALU.mult), "v"))
            v.wait_ge(sig["ln_rstd"], 5 * i + T + 1)
            sig.up(v.scalar_tensor_tensor(x, x, rstd[:n, T:T + 1], lnp[:n, 1, :], ALU.mult, ALU.add), "ln_done")

        def ln_scalar(s, sig, i, T):
            n = TILES[T][1]
            s.wait_ge(sig["ln_var"], 5 * i + T + 1)
            r = rstd[:n, T:T + 1]
            s.wait_ge(sig["s"], sig.up(s.activation(r, mv[:n, T, 1:2], ACT.Ln, bias=const("eps")[:n, 3:4]), "s"))
            sig.up(s.activation(r, r, ACT.Exp, scale=-0.5), "ln_rstd")

        def turn_x_tensor(pe, bk, sig, i, T, banks):
            t0, n = TILES[T]
            pe.wait_ge(sig["ln_done"], 5 * i + T + 1)
            for g in range(2):
                ps = bk.begin(pe, ("xT", i, T, g), banks[g]).rearrange("p (c t) -> p c t", c=4)
                for c in range(4):
                    ins = pe.transpose(ps[:, c, :n], xk[:n, T, (4 * g + c) * P:(4 * g + c + 1) * P], ident[:n, :n])
                bk.filled(ins, ("xT", i, T, g))

        def turn_x_scalar(s, bk, sig, i, T):
            t0, n = TILES[T]
            for g in range(2):
                ps = bk.take(s, ("xT", i, T, g)).rearrange("p (c t) -> p c t", c=4)
                bk.give(s.activation(xTv[:, 4 * g:4 * g + 4, t0:t0 + n], ps[:, :, :n], ACT.Copy), ("xT", i, T, g))

        def ln_params(sp, sig, g, b):
            sig.up(sp.dma_start(lnp[:, 0, :], g.partition_broadcast(P)), "ln_param", 16)
            sig.up(sp.dma_start(lnp[:, 1, :], b.partition_broadcast(P)), "ln_param", 16)

        def first_slab(sp, n, layer, sem):
            c0 = SLABS_IN[n][0]
            sp.dma_start(wring[:, n], A["w_in"][bass.ds(layer, 1), :, c0:c0 + W512]
                         .rearrange("a (c p) n -> p (a c) n", p=P)).then_inc(sem, 16)

        s0 = Signals(nc, ctx, "in_")
        b0 = Banks(s0, psum)
        with nc.Block() as block:
            @block.tensor
            def _(pe):
                pe.wait_ge(s0["ident"], 16)
                for T in range(5):
                    turn_x_tensor(pe, b0, s0, 0, T, (2 * (T % 2), 2 * (T % 2) + 1))

            @block.scalar
            def _(s):
                s.wait_ge(s0["ident"], 16)
                for T in range(5):
                    ln_scalar(s, s0, 0, T)
                    if T:
                        turn_x_scalar(s, b0, s0, 0, T - 1)
                turn_x_scalar(s, b0, s0, 0, 4)

            @block.vector
            def _(v):
                for T in range(5):
                    v.wait_ge(s0[f"x{T}"], 16)
                    ln_vector(v, s0, 0, T)

            @block.sync
            def _(sp):
                xp = A["x_prompt"].rearrange("a (t p) d -> p (a t) d", p=P)
                n_first = where["eps"][0] + where["eps"][1]
                sp.dma_start(xk[:, 0, :], xp[:, 0, :]).then_inc(s0["x0"], 16)
                sp.dma_start(con[:, :n_first], table[:, :n_first]).then_inc(s0["ident"], 16)
                ln_params(sp, s0, A["ln_in_g"], A["ln_in_b"])
                for T in range(1, 4):
                    sp.dma_start(xk[:, T, :], xp[:, T, :]).then_inc(s0[f"x{T}"], 16)
                sp.dma_start(xk[:NS, 4, :], A["x_sample"].rearrange("b t d -> (b t) d")).then_inc(s0["x4"], 16)
                sp.dma_start(con[:, n_first:], table[:, n_first:]).then_inc(s0["con"], 16)
                for n in range(2):
                    first_slab(sp, n, 0, s0["w"])
                sp.wait_ge(s0["con"], 16)
                sp.wait_ge(s0["w"], 32)

        engines = list(nc.engines.keys())
        nc.multi_engine_barrier(engines, sems_to_clear=s0.numbers())

        sig = Signals(nc, ctx, "")
        bk = Banks(sig, psum)
        with nc.Fori(0, DEPTH) as l:
            N_ROW_DMAS = len(ROWS) + 2
            N_SMALL_W = 11
            N_OUT1 = []
            def slab_read(sp, n):
                if n < 7:
                    bk.take(sp, ("z", SLABS_IN[n][1] + 3, 1))
                elif n < 9:
                    bk.take(sp, ("wout", 4, n - 7))
                elif n < 13:
                    bk.take(sp, ("kv", n - 9, 1))
                elif n < 15:
                    bk.take(sp, ("q", 4 * (n - 13) + 3, 1))
                elif n < 17:
                    bk.take(sp, ("wo", 4, n - 15))
                elif n < 25:
                    bk.take(sp, ("up", 4 * (n - 17) + 3, 1))
                elif n % 2 == 0:
                    bk.take(sp, ("down", (n - 25) // 2, 1, 1))
                else:
                    sp.wait_ge(sig["downread"], (n - 25) // 2 + 1)


            def out_slab(sp, n):
                if n < 9:
                    name, r, c = "w_out", 0, n - 7
                elif n < 13:
                    name, r, c = ("xa_wk", "xa_wv")[(n - 9) // 2], 0, (n - 9) % 2
                elif n < 15:
                    name, r, c = "xa_wq", 0, n - 13
                elif n < 17:
                    name, r, c = "xa_wo", 0, n - 15
                elif n < 25:
                    name, r, c = "w_up", 0, n - 17
                slab_read(sp, n - 2)
                if n >= 25:
                    q, r = (n - 25) // 2, (n - 25) % 2
                    sp.dma_start(cols(ring, (n % 2) * KC * W512, 2 * KC, W256),
                                 A["w_down"][bass.ds(l, 1), r * 2 * D:(r + 1) * 2 * D, q * W256:(q + 1) * W256]
                                 .rearrange("a (c p) n -> p (a c) n", p=P)).then_inc(sig[f"slab{n % 2}"], 16)
                    return
                sp.dma_start(wring[:, n % 2], A[name][bass.ds(l, 1), r * D:(r + 1) * D, c * W512:(c + 1) * W512]
                             .rearrange("a (c p) n -> p (a c) n", p=P)).then_inc(sig[f"slab{n % 2}"], 16)



            row = {k: slice(a, a + n) for k, (a, n) in ROWS.items()}
            placed = {"tmp": 0}


            def region(t, n):
                placed[t] += n
                return placed[t] - n


            prow = cols(tmp, region("tmp", 128), 128)
            prow2 = cols(tmp, region("tmp", 128), 128)
            pc = cols(tmp, region("tmp", N_ROWS), N_ROWS)
            pc2 = cols(tmp, region("tmp", 64), 64)
            oc1 = cols(tmp, region("tmp", 126), 126)
            oc2 = cols(tmp, region("tmp", 36), 36)
            orow1, orow2 = prow, prow2
            graw = cols(tmp, region("tmp", NT), NT)
            wgate = cols(tmp, region("tmp", 512), KC, 64)
            wax = cols(tmp, region("tmp", 512), 2, 2, P)
            wwa = cols(tmp, region("tmp", 512), 4, P)
            wg2 = cols(tmp, region("tmp", 256), 2, P)
            bif = cols(tmp, region("tmp", 2), 2)
            m0 = cols(tmp, region("tmp", 8), NB)
            lamc = cols(tmp, region("tmp", 6), 3, 2)
            omka = cols(tmp, region("tmp", 2), 2)
            mcar = cols(tmp, region("tmp", 4), 4)
            carry = cols(tmp, region("tmp", 24), 2, 12)
            epc = cols(tmp, region("tmp", 32), 2, 16)
            SsT = cols(tmp, region("tmp", 1024), 2, NB, HD)
            X1 = cols(tmp, region("tmp", 2 * NT), 2, NT)
            X2 = cols(tmp, region("tmp", 2 * NT), 2, NT)
            X4 = cols(tmp, region("tmp", 2 * NT), 2, NT)
            X5 = cols(tmp, region("tmp", 2 * NT), 2, NT)
            dbase = region("tmp", 3072)
            Xm = cols(tmp, dbase, H, P)
            Dm = cols(tmp, dbase + 512, H, P)
            DmT = cols(tmp, dbase + 1024, H, P)
            WKT = cols(tmp, dbase + 1536, 2, P)
            CV = cols(tmp, dbase + 1792, H, HD)
            UV = cols(tmp, dbase + 2048, H, HD)
            SAn = cols(tmp, dbase + 2304, H, HD)
            ST = cols(tmp, dbase + 2560, 2, P)
            STe = cols(tmp, dbase + 2816, 2, P)
            assert placed["tmp"] <= TMP, placed
            dpad = cols(xtok, 0, 2, 2, 2, P)
            BM = cols(xtok, 1024, 2, 2, 2, P)
            KM = cols(xtok, 2048, 2, 2, 2, P)
            Dtok = cols(xtok, 3072, 4, 2, P)
            OmT = cols(xtok, 4096, 2, H, P)
            d_first = cols(xtok, 2048, 4, NT)
            kkr = cols(xtok, 2048, 2, NT)
            kks = cols(xtok, 2048 + 2 * NT, 2, NT)
            Sraw = cols(xtok, 1024, 4, H, HD)
            rows = [cols(xtok, 544 * i, NT) for i in range(6)]
            qpad = cols(xtok, 3264, 2, 2, P)
            Em = cols(xtok, 3776, H, P)
            Wm = cols(xtok, 4288, H, P)
            kw = cols(tmp, dbase, 2, P)
            vt = cols(tmp, dbase + 256, 2, P)
            Cb = cols(tmp, dbase + 512, 2, P)
            nb_ = cols(tmp, dbase + 768, 2, P)
            Rb = cols(tmp, dbase + 1024, 2, P)
            Cs = cols(tmp, dbase + 1280, 2, NB, HD)
            gcol = cols(tmp, dbase + 2304, 36)
            ncol = cols(tmp, dbase + 2340, 2)
            qspad = cols(tmp, dbase + 2344, 2, 2, NS)
            rden = cols(tmp, dbase + 2480, 2, P)
            qx = cols(tmp, dbase + 2736, 2, P)
            vx2 = cols(big, 22 * NT + 1536, 2, NB, HD)
            qpad_b = cols(big, 22 * NT, 2, 2, P)
            Wm_b = cols(big, 22 * NT + 512, H, P)
            kw_b = cols(big, 22 * NT + 1024, 2, P)
            vt_b = cols(big, 22 * NT + 1280, 2, P)
            qspad_b = cols(big, 22 * NT + 2560, 2, 2, NS)
            vx2_b = cols(big, 16 * NT, 2, NB, HD)
            Rs = cols(big, 28 * NT, 2, NB, HD)
            n0x = cols(big, 28 * NT + 1024, 2, NB, HD)
            OM0 = [0, 6, 12, 18, 24]
            T28 = z(28, 2)
            T30 = z(30, 2)


            HALVES = ((0, slice(0, NT // 2)), (1, slice(NT // 2, NT)))


            def segs(v):
                if len(v.shape) == 2:
                    return v[:, SEQ:].rearrange("p (b t) -> p b t", b=NB)
                return v[:, :, SEQ:].rearrange("p n (b t) -> p n b t", b=NB)


            def prm(name, i):
                return pc[:, ROWS[name][0] + i:ROWS[name][0] + i + 1]


            conv0 = pc2[:, 0:48].rearrange("p (b i f) -> p f b i", b=NB, i=3)
            n0c = pc2[:, 48:64].rearrange("p (b q) -> p q b", b=NB)
            h0c = pc[:, row["state_rglru_h"]].rearrange("p (b f) -> p f b", b=NB)
            sh0 = pc[:, row["state_rwkv_shift"]].rearrange("p (b f) -> p f b", b=NB)
            ZPOS = {}
            for _, f0 in SLABS_IN:
                for f in range(f0, f0 + 4):
                    ZPOS[f] = len(ZPOS)


            def z_wait(eng, *fs):
                f = max(fs, key=ZPOS.get)
                bk.given(eng, ("z", f, 0))
                bk.given(eng, ("z", f, 1))


            def slab_pe(pe, n):
                if n >= 2:
                    pe.wait_ge(sig[f"slab{n % 2}"], 16 * (n // 2))
                return wring[:, n % 2, :, :]


            def after(eng, ins, name):
                eng.wait_ge(sig[name], sig.up(ins, name))


            def product(pe, key, bank, rhs, lhsT_list):
                n = len(lhsT_list)
                m = lhsT_list[0].shape[1]
                for part, c in HALVES:
                    b, w = bank + 2 * part, c.stop - c.start
                    ps = bk.begin(pe, key + (part,), b)
                    for k in range(n):
                        ins = pe.matmul(ps[:m, :w], lhsT_list[k], rhs(k)[:, c], start=(k == 0), stop=(k == n - 1))
                    bk.filled(ins, key + (part,))


            def x_product(pe, key, bank, lhsT_list):
                product(pe, key, bank, lambda k: xTv[:, k, :], lhsT_list)


            def drain(eng, key, fn):
                for part, c in HALVES:
                    ps = bk.take(eng, key + (part,))
                    ins = fn(ps[:, :c.stop - c.start], c)
                    bk.give(ins, key + (part,))
                    bk.given(eng, key + (part,))


            SPARE = [(n, SLABS_IN[n][1] + i, half, k) for n in (4, 5, 6) for i in range(4) for half in range(2) for k in range(KC)]
            HALF_DONE = {}
            FILL_BONUS = 2 * KC
            FILL_OM, FILL_X, FILL_ST, FILL_SA = 2, 2, 2, 1


            def spare_products(pe, point, count, banks):
                at = HALF_DONE.get("at", 0)
                for n, f, half, k in SPARE[at:at + count]:
                    if k == 0 and half == 0 and f == SLABS_IN[n][1]:
                        slab_pe(pe, n)
                    c = HALVES[half][1]
                    if k == 0:
                        bk.begin(pe, ("z", f, half), banks[half])
                    ps = psum[:, bk.turn[("z", f, half)][0], :c.stop - c.start]
                    i = f - SLABS_IN[n][1]
                    ins = pe.matmul(ps, wring[:, n % 2, k, i * P:(i + 1) * P], xTv[:, k, c], start=(k == 0), stop=(k == KC - 1))
                    if k == KC - 1:
                        bk.filled(ins, ("z", f, half))
                HALF_DONE["at"] = min(at + count, len(SPARE))
                HALF_DONE[point] = HALF_DONE["at"] // KC


            def finish_half(pe, point, banks, upto=0):
                at = HALF_DONE["at"]
                spare_products(pe, point, max(-at % KC, KC * upto - at), banks)


            with nc.Block() as block:

                @block.tensor
                def _(pe):
                    def gemm(n, tiles=range(4)):
                        c0, f0 = SLABS_IN[n]
                        w = slab_pe(pe, n)
                        for i in tiles:
                            x_product(pe, ("z", f0 + i), (f0 + i) % 2, [w[:, k, i * P:(i + 1) * P] for k in range(KC)])

                    gemm(0)
                    pe.wait_ge(sig["rows"], 16 * N_ROW_DMAS)
                    ps = bk.begin(pe, ("prow",), 4)
                    bk.filled(pe.transpose(ps[:, :N_ROWS], prow[:N_ROWS, :], ident[:N_ROWS, :N_ROWS]), ("prow",))
                    ps = bk.begin(pe, ("prow2",), 5)
                    bk.filled(pe.transpose(ps[:, :64], prow2[:64, :], ident[:64, :64]), ("prow2",))
                    pe.wait_ge(sig["Sraw"], 16 * NB)
                    for pr in range(2):
                        ps = bk.begin(pe, ("SsT", pr), 6 + pr).rearrange("p (b c) -> p b c", b=4)
                        for b4 in range(4):
                            ins = pe.transpose(ps[:, b4, :], Sraw[:, b4, 2 * pr:2 * pr + 2, :].rearrange("p a b -> p (a b)"), ident)
                        bk.filled(ins, ("SsT", pr))

                    gemm(1)
                    pe.wait_ge(sig["small_w"], 16 * N_SMALL_W)
                    pe.wait_ge(sig["xc"], 1)
                    for g in range(2):
                        for f in range(2):
                            product(pe, ("rg", g, f), f, lambda k: X1[:, f, :], [wax[:, g, f, :]])
                    gemm(2)
                    gemm(3, (0, 1))
                    x_product(pe, ("gates",), 0, [wgate[:, k, 0:36] for k in range(KC)])
                    pe.wait_ge(sig["kk2"], 1)
                    for i in range(2):
                        product(pe, ("kk", i), i, lambda k: kks[:, i, :], [const("sum64")])
                    gemm(3, (2,))
                    pe.wait_ge(sig["act_d"], 2)
                    for i in range(4):
                        product(pe, ("wa", i), i % 2, lambda k: z(26)[:, :], [wwa[:, i, :]])
                    for i in range(2):
                        product(pe, ("g2", i), i % 2, lambda k: z(27)[:, :], [wg2[:, i, :]])
                    gemm(3, (3,))
                    spare_products(pe, "bonus", FILL_BONUS, (0, 1))
                    finish_half(pe, "bonus", (0, 1))
                    pe.wait_ge(sig["rk"], 1)
                    for i in range(2):
                        product(pe, ("bonus", i), i, lambda k: X5[:, i, :], [const("sum64")])
                    pe.wait_ge(sig["oc1"], 2)
                    ps = bk.begin(pe, ("orow1",), 6)
                    bk.filled(pe.transpose(ps[:126, :P], oc1[:, :], ident), ("orow1",))

                    for T in range(5):
                        t0, n = TILES[T]
                        pe.wait_ge(sig["dfeat"], 1)
                        for i, pair in enumerate(((X2, X4), (z(ZK_D, 2), z(ZV_D, 2)))):
                            ps = bk.begin(pe, ("dtok", T, i), 4 + i).rearrange("p (a c) -> p a c", a=4)
                            for j in range(2):
                                for pr in range(2):
                                    ins = pe.transpose(ps[:n, 2 * j + pr, :], pair[j][:, pr, t0:t0 + n], ident)
                            bk.filled(ins, ("dtok", T, i))
                        spare_products(pe, ("dpad", T), 2, (0, 1))
                        pe.wait_ge(sig["dpad"], 2 * (T + 1))
                        for i, (left, b) in enumerate(((X4, 6), (z(ZK_D, 2), 6))):
                            if i:
                                spare_products(pe, ("dsc", T), 4, (0, 1))
                            for pr in range(2):
                                ps = bk.begin(pe, ("dsc", T, i, pr), b + pr).rearrange("p (a s t) -> p a s t", a=2, s=2)
                                bk.filled(pe.matmul(ps[:n, :, :, :n], left[:, pr, t0:t0 + n], dpad[:, pr, :, :, :n],
                                                    start=True, stop=True), ("dsc", T, i, pr))
                        levels = (1, 2, 4, 8, 16, 32) if T < 4 else (1, 2)
                        for li, m in enumerate(levels):
                            last = m == levels[-1]
                            spare_products(pe, ("om", T, m), FILL_OM, (0, 1))
                            pe.wait_ge(sig["om"], OM0[T] + li + 1)
                            ps = bk.begin(pe, ("X", T, m), 2).rearrange("p (h t) -> p h t", h=H)
                            om = OmT[:, (OM0[T] + li) % 2]
                            if m > 1:
                                bk.given(pe, ("X", T, 1) if m == 2 else ("DT", T, m // 2))
                            for h in range(H):
                                ins = pe.matmul(ps[:n, h, :n], om[:n, h, :n], (ident if m == 1 else Dm[:, h, :])[:n, :n],
                                                start=True, stop=True)
                            bk.filled(ins, ("X", T, m))
                            if m == 1:
                                continue
                            spare_products(pe, ("X", T, m), FILL_X, (0, 1))
                            bk.given(pe, ("X", T, m))
                            if not last:
                                ps = bk.begin(pe, ("D", T, m), 3).rearrange("p (h t) -> p h t", h=H)
                                for h in range(H):
                                    ins = pe.matmul(ps[:n, h, :n], DmT[:n, h, :n], Xm[:n, h, :n], start=True, stop=True)
                                bk.filled(ins, ("D", T, m))
                            ps = bk.begin(pe, ("DT", T, m), 4).rearrange("p (h t) -> p h t", h=H)
                            for h in range(H):
                                ins = pe.matmul(ps[:n, h, :n], Xm[:n, h, :n], DmT[:n, h, :n], start=True, stop=True)
                            bk.filled(ins, ("DT", T, m))
                        bk.given(pe, ("dtok", T, 1))
                        bk.given(pe, ("dsc", T, 1, 1))
                        ps = bk.begin(pe, ("CV", T), 6)[:, 0:256].rearrange("p (h v) -> p h v", h=H)
                        for h in range(H):
                            ins = pe.matmul(ps[:n, h, :], KM[:n, h // 2, h % 2, 0, :n],
                                            Dtok[:n, 3, h // 2, (h % 2) * HD:(h % 2) * HD + HD], start=True, stop=True)
                        bk.filled(ins, ("CV", T))
                        spare_products(pe, ("inv", T), 1, (0, 1))
                        bk.given(pe, ("DT", T, levels[-1]))
                        if T < 4:
                            ps = bk.begin(pe, ("WK", T), 5)[:, 0:256].rearrange("p (q t) -> p q t", q=2)
                            for h in range(H):
                                par = (h % 2) * HD
                                ins = pe.matmul(ps[par:par + HD, h // 2, :], Dtok[:, 0, h // 2, par:par + HD], DmT[:, h, :],
                                                start=True, stop=True)
                            bk.filled(ins, ("WK", T))
                            bk.given(pe, ("CV", T))
                            ps = bk.begin(pe, ("UV", T), 7)[:, 0:256].rearrange("p (h v) -> p h v", h=H)
                            for h in range(H):
                                ins = pe.matmul(ps[:, h, :], DmT[:, h, :], CV[:, h, :], start=True, stop=True)
                            bk.filled(ins, ("UV", T))
                            spare_products(pe, ("UV", T), 1, (0, 1))
                            bk.given(pe, ("WK", T))
                            bk.given(pe, ("UV", T))
                            for cc in range(2):
                                c0 = cc * 64
                                cn = 2 * T + cc
                                if cn:
                                    spare_products(pe, ("state", cn), FILL_ST, (0, 1))
                                    bk.given(pe, ("st", cn - 1))
                                else:
                                    pe.wait_ge(sig["zeroed"], 1)
                                ps = bk.begin(pe, ("SA", cn), 2)[:, 0:256].rearrange("p (q v) -> p q v", q=2)
                                for pr in range(2):
                                    ins = pe.matmul(ps[c0:c0 + 64, pr, :], WKT[:, pr, c0:c0 + 64], ST[:, pr, :],
                                                    start=True, stop=True)
                                bk.filled(ins, ("SA", cn))
                                spare_products(pe, ("SA", cn), FILL_SA, (0, 1))
                                bk.given(pe, ("SA", cn))
                                ps2 = bk.begin(pe, ("o", cn), 3)[:, 0:128].rearrange("p (q t) -> p q t", q=2)
                                for pr in range(2):
                                    pe.matmul(ps2[:, pr, :], ST[:, pr, :], z(ZR_D + pr)[:, t0 + c0:t0 + c0 + 64],
                                              start=True, stop=False, skip_group_check=True)
                                    for a in range(2):
                                        h = 2 * pr + a
                                        o = ps2[a * HD:a * HD + HD, pr, :]
                                        pe.matmul(o, Dtok[:, 3, pr, a * HD:a * HD + HD], KM[:, pr, a, 1, c0:c0 + 64],
                                                  start=False, stop=False, skip_group_check=True)
                                        ins2 = pe.matmul(o, SAn[:, h, :], BM[:, pr, a, 1, c0:c0 + 64],
                                                         start=False, stop=True, skip_group_check=True)
                                bk.filled(ins2, ("o", cn))
                                ps = bk.begin(pe, ("st", cn), 4)[:, 0:256].rearrange("p (q v) -> p q v", q=2)
                                for pr in range(2):
                                    san = SAn[c0:c0 + 64, 2 * pr:2 * pr + 2, :].rearrange("p a b -> p (a b)")
                                    pe.matmul(ps[:, pr, :], Dtok[c0:c0 + 64, 1, pr, :], san, start=True, stop=False)
                                    ins = pe.matmul(ps[:, pr, :], Dtok[c0:c0 + 64, 2, pr, :], Dtok[c0:c0 + 64, 3, pr, :],
                                                    start=False, stop=True)
                                bk.filled(ins, ("st", cn))
                        else:
                            ps = bk.begin(pe, ("KS",), 2)[:, 0:64].rearrange("p (q t) -> p q t", q=2)
                            for pr in range(2):
                                for a in range(2):
                                    for b in range(NB):
                                        ins = pe.matmul(ps[a * HD:a * HD + HD, pr, TS * b:TS * b + TS], SsT[:, pr, b, :],
                                                        dpad[:, pr, a, 0, TS * b:TS * b + TS], start=True, stop=True)
                            bk.filled(ins, ("KS",))
                            spare_products(pe, ("KS",), 2, (0, 1))
                            bk.given(pe, ("KS",))
                            ps = bk.begin(pe, ("KSt",), 3)[:, 0:256].rearrange("p (q v) -> p q v", q=2)
                            for pr in range(2):
                                ins = pe.transpose(ps[:NS, pr, :], Xm[:, 0, pr * NS:pr * NS + NS], ident)
                            bk.filled(ins, ("KSt",))
                            spare_products(pe, ("KSt",), 2, (0, 1))
                            bk.given(pe, ("KSt",))
                            ps = bk.begin(pe, ("SAs",), 7)[:, 0:256].rearrange("p (h v) -> p h v", h=H)
                            for h in range(H):
                                ins = pe.matmul(ps[:n, h, :], DmT[:n, h, :n], CV[:n, h, :], start=True, stop=True)
                            bk.filled(ins, ("SAs",))
                            spare_products(pe, ("SAs",), 2, (0, 1))
                            bk.given(pe, ("SAs",))
                            ps = bk.begin(pe, ("os",), 3)[:, 0:64].rearrange("p (q t) -> p q t", q=2)
                            for pr in range(2):
                                for a in range(2):
                                    o = ps[a * HD:a * HD + HD, pr, :]
                                    pe.matmul(o, Dtok[:NS, 3, pr, a * HD:a * HD + HD], KM[:NS, pr, a, 1, :NS],
                                              start=True, stop=False, skip_group_check=True)
                                    pe.matmul(o, SAn[:NS, 2 * pr + a, :], BM[:NS, pr, a, 1, :NS],
                                              start=False, stop=False, skip_group_check=True)
                                    for b in range(NB):
                                        ins = pe.matmul(o[:, TS * b:TS * b + TS], SsT[:, pr, b, :],
                                                        dpad[:, pr, a, 1, TS * b:TS * b + TS],
                                                        start=False, stop=(b == NB - 1), skip_group_check=True)
                            bk.filled(ins, ("os",))
                            for pr in range(2):
                                ps = bk.begin(pe, ("sts", pr), 4 + pr)
                                for a in range(2):
                                    h = 2 * pr + a
                                    spare_products(pe, ("SX", h), 3, (0, 1))
                                    pe.wait_ge(sig["SX"], h + 1)
                                    pe.matmul(ps[a * HD:a * HD + HD, :], Dtok[:NS, 1, pr, a * HD:a * HD + HD],
                                              OmT[:NS, h % 2].rearrange("p a b -> p (a b)"), start=True, stop=False)
                                    ins = pe.matmul(ps[a * HD:a * HD + HD, :], Dtok[:NS, 2, pr, a * HD:a * HD + HD],
                                                    (Xm, Dm)[h % 2][:NS].rearrange("p a b -> p (a b)"), start=False, stop=True)
                                    if a == 0:
                                        sig.up(ins, "SXread")
                                bk.filled(ins, ("sts", pr))
                            spare_products(pe, ("Sss",), 3, (0, 1))
                            pe.wait_ge(sig["Sss"], 2)
                            for pr in range(2):
                                ps = bk.begin(pe, ("SsB", pr), 6 + pr).rearrange("p (b c) -> p b c", b=4)
                                for b4 in range(4):
                                    ins = pe.transpose(ps[:, b4, :], SsT[:, pr, 2 * b4:2 * b4 + 2, :].rearrange("p a b -> p (a b)"),
                                                       ident)
                                bk.filled(ins, ("SsB", pr))
                            bk.given(pe, ("st", 7))
                            ps = bk.begin(pe, ("STb",), 2)[:, 0:256].rearrange("p (q v) -> p q v", q=2)
                            for pr in range(2):
                                ins = pe.transpose(ps[:, pr, :], ST[:, pr, :], ident)
                            bk.filled(ins, ("STb",))

                    finish_half(pe, "Dnorm", (0, 1), 24)

                    def head_means(pre, ht, bank):
                        pe.wait_ge(sig[pre + "h"], 1)
                        for i in range(2):
                            product(pe, (pre + "mu", i), bank + i, lambda k: ht[:, i, :], [const("mean64")])

                    def head_variances(pre, sq, bank):
                        pe.wait_ge(sig[pre + "sq"], 1)
                        for i in range(2):
                            product(pe, (pre + "var", i), bank + i, lambda k: sq[:, i, :], [const("mean64")])

                    head_means("D", X1, 0)
                    z_wait(pe, 15)
                    for i in range(4):
                        f = (ZQ_B, ZK_B)[i // 2] + i % 2
                        product(pe, ("swap", i), 4 + i % 2, lambda k: z(f)[:, :], [const("swap")])
                    head_variances("D", T28, 0)

                    pe.wait_ge(sig["rowsA"], 1)
                    for q, r in enumerate((3, 2)):
                        for pr in range(2):
                            product(pe, ("bcA", q, pr), pr, lambda k: rows[r][:4, :], [const("sel_pair", 2, P)[:4, pr, :]])

                    def keys_values(pre, T, bank):
                        t0, n = TILES[T]
                        zk, zv = (ZK_A, ZV_A) if pre == "A" else (ZK_B, ZV_B)
                        ps = bk.begin(pe, (pre + "tr", T), bank).rearrange("p (a c) -> p a c", a=4)
                        for j, f in enumerate((zk, zk + 1, zv, zv + 1)):
                            ins = pe.transpose(ps[:n, j, :], z(f)[:, t0:t0 + n], ident)
                        bk.filled(ins, (pre + "tr", T))

                    def gate_tiles(T):
                        t0, n = TILES[T]
                        ps = bk.begin(pe, ("Agc", T), 5)[:, 0:36]
                        bk.filled(pe.transpose(ps[:n, :], rows[5][0:36, t0:t0 + n], ident[:36, :36]), ("Agc", T))
                        if T == 0:
                            pe.wait_ge(sig["negG"], 1)
                        ps = bk.begin(pe, ("AG", T), 6).rearrange("p (h t) -> p h t", h=H)
                        for h in range(H):
                            ins = pe.matmul(ps[:n, h, :n], const("sel_head", H, P)[:4, h, :n], rows[1][:4, t0:t0 + n],
                                            start=True, stop=True)
                        bk.filled(ins, ("AG", T))

                    def key_scores(pre, T, bank):
                        t0, n = TILES[T]
                        zk, pad = (ZK_A, qpad) if pre == "A" else (ZK_B, qpad_b)
                        pe.wait_ge(sig[pre + "pad"], 2 * (T + 1))
                        ps = bk.begin(pe, (pre + "sc", T), bank).rearrange("p (q a t) -> p q a t", q=2, a=2)
                        for pr in range(2):
                            ins = pe.matmul(ps[:n, pr, :, :n], z(zk + pr)[:, t0:t0 + n], pad[:, pr, :, :n], start=True, stop=True)
                        bk.filled(ins, (pre + "sc", T))

                    def outputs(pre, T, bank):
                        t0, n = TILES[T]
                        w_, k_, v_ = (Wm, kw, vt) if pre == "A" else (Wm_b, kw_b, vt_b)
                        q_, x_ = (qspad, vx2) if pre == "A" else (qspad_b, vx2_b)
                        bk.given(pe, (pre + "sc", T))
                        bk.given(pe, (pre + "tr", T))
                        if T:
                            pe.wait_ge(sig[pre + "state"], T)
                        else:
                            pe.wait_ge(sig["Azero"], 1)
                        if pre == "B" and T < 4:
                            pe.wait_ge(sig["Bqx"], T + 1)
                        if T == 4:
                            pe.wait_ge(sig[pre + "s"], 16 * 2)
                            pe.wait_ge(sig[pre + "qs"], 1 if pre == "A" else 2)
                        nd = bk.begin(pe, (pre + "nd", T), bank).rearrange("p (w q t) -> p w q t", w=2, q=2)
                        for w in range(2 if pre == "A" else 1):
                            for pr in range(2):
                                o = nd[:, w, pr, :n]
                                for a in range(2):
                                    left = (v_[:n, pr, a * HD:a * HD + HD], const("ones")[:n, :])[w]
                                    pe.matmul(o[a * HD:a * HD + HD, :], left, w_[:n, 2 * pr + a, :n],
                                              start=True, stop=False, skip_group_check=True)
                                if T < 4:
                                    state = ((Cb, nb_)[w] if pre == "A" else Rb)[:, pr, :]
                                    right = X2[:, pr, t0:t0 + n] if pre == "A" else qx[:, pr, :]
                                    ins = pe.matmul(o, state, right, start=False, stop=True, skip_group_check=True)
                                else:
                                    for a in range(2):
                                        for b in range(NB):
                                            state = (Cs if pre == "A" else Rs)[:, pr, b, :]
                                            if w:
                                                state = n0x[:, pr, b, :]
                                            ins = pe.matmul(o[a * HD:a * HD + HD, TS * b:TS * b + TS], state,
                                                            q_[:, pr, a, TS * b:TS * b + TS],
                                                            start=False, stop=(b == NB - 1), skip_group_check=True)
                        bk.filled(ins, (pre + "nd", T))
                        if T < 4:
                            ps = bk.begin(pe, (pre + "st", T), bank + 1)
                            for pr in range(2):
                                ins = pe.matmul(ps[:, pr * P:(pr + 1) * P], k_[:, pr, :], v_[:, pr, :], start=True, stop=True)
                                if pre == "A":
                                    ins = pe.matmul(ps[:, 256 + pr:257 + pr], k_[:, pr, :], const("ones")[:, 0:1],
                                                    start=True, stop=True)
                            bk.filled(ins, (pre + "st", T))
                        else:
                            for pr in range(2):
                                ps = bk.begin(pe, (pre + "sts", pr), (1, 4)[pr] if pre == "A" else (3, 5)[pr])
                                for a in range(2):
                                    h = 2 * pr + a
                                    pe.wait_ge(sig[pre + "vx"], h + 1)
                                    ins = pe.matmul(ps[a * HD:a * HD + HD, :], k_[:NS, pr, a * HD:a * HD + HD],
                                                    x_[:NS, h % 2, :, :].rearrange("p a b -> p (a b)"), start=True, stop=True)
                                    if a == 0:
                                        sig.up(ins, pre + "vxread")
                                bk.filled(ins, (pre + "sts", pr))
                            if pre == "A":
                                ps = bk.begin(pe, ("Ans",), 6)[:, 0:16].rearrange("p (q b) -> p q b", q=2)
                                for pr in range(2):
                                    ins = pe.matmul(ps[:, pr, :], k_[:NS, pr, :], const("own")[:NS, :], start=True, stop=True)
                                bk.filled(ins, ("Ans",))

                    pe.wait_ge(sig["rot"], 1)
                    for T in range(5):
                        keys_values("A", T, 4)
                        gate_tiles(T)
                        key_scores("A", T, 7)
                        keys_values("B", T, 5)
                        key_scores("B", T, 6)
                        outputs("B", T, 2)
                        outputs("A", T, 0)
                    pe.wait_ge(sig["oc2"], 1)
                    ps = bk.begin(pe, ("orow2",), 3)
                    bk.filled(pe.transpose(ps[:36, :P], oc2[:, :], ident), ("orow2",))
                    head_means("A", z(ZQ_A, 2), 0)
                    head_means("B", z(ZQ_B, 2), 4)
                    head_variances("A", X2, 0)
                    head_variances("B", X4, 4)


                @block.vector
                def _(v):
                    def one(ins):
                        after(v, ins, "v")

                    tt, stt, ts = v.tensor_tensor, v.scalar_tensor_tensor, v.tensor_scalar
                    bk.take(v, ("prow",))
                    bk.give(v.tensor_copy(pc[:, :], psum[:, 4, :N_ROWS]), ("prow",))
                    bk.take(v, ("prow2",))
                    bk.give(v.tensor_copy(pc2[:, :], psum[:, 5, :64]), ("prow2",))
                    bk.given(v, ("prow",))
                    bk.given(v, ("prow2",))
                    v.memset(SAn[:, :, :], 0.0)
                    sig.up(v.memset(ST[:, :, :], 0.0), "zeroed")
                    lam = pc[:, row["rg_lam"]]
                    sig.up(stt(lamc[:, 0, :], lam, -1.0, lam, ALU.mult, ALU.max), "lam")
                    one(ts(lamc[:, 1, :], lam, -1.0, 0.0, ALU.mult, ALU.max))
                    v.wait_ge(sig["lamln"], 1)
                    one(tt(lamc[:, 1, :], lamc[:, 1, :], lamc[:, 0, :], ALU.add))
                    ts(lamc[:, 2, :], lamc[:, 1, :], -8.0, None, ALU.mult)
                    sig.up(ts(lamc[:, 1, :], lamc[:, 1, :], 8.0, None, ALU.mult), "lamc")
                    one(ts(omka[:, :], pc[:, row["rwkv_k_a"]], -1.0, 1.0, ALU.mult, ALU.add))

                    def graw_rows(ps, c):
                        ts(graw[0:4, c], ps[0:4], bif[0:4, 0:1], None, ALU.add)
                        return ts(graw[32:36, c], ps[32:36], bif[32:36, 1:2], None, ALU.add)
                    def token_shift(g):
                        f0 = 20 + 4 * g
                        z_wait(v, f0 + 3)
                        v.tensor_copy(oc1[:, 4 * g:4 * g + 4], z(f0, 4)[:, :, SEQ - 1])
                        ins = v.tensor_copy(oc1[:, 8:72].rearrange("p (b f) -> p f b", b=NB)[:, 4 * g:4 * g + 4],
                                            segs(z(f0, 4))[:, :, :, 3])
                        v.wait_ge(sig["oc1"], sig.up(ins, "oc1"))
                        v.wait_ge(sig["delta"], g + 1)
                        d = (d_first, z(28, 4))[g]
                        for i in range(4):
                            ins = stt(z(f0 + i), d[:, i, :], prm("rwkv_mu", 4 * g + i), z(f0 + i), ALU.mult, ALU.add)
                        sig.up(ins, "zs")

                    z_wait(v, 19)
                    v.tensor_copy(oc1[:, 72:78].rearrange("p (i f) -> p f i", i=3), z(ZX_C, 2)[:, :, SEQ - 3:SEQ])
                    for f in range(2):
                        v.tensor_copy(oc1[:, 78:126].rearrange("p (b i f) -> p f b i", b=NB, i=3)[:, f], segs(z(ZX_C + f))[:, :, 1:4])
                    for f in range(2):
                        ins = ts(X1[:, f, :], z(ZX_C + f), prm("conv_w", 6 + f), prm("conv_b", f), ALU.mult, ALU.add)
                    for i in range(3):
                        sh = 3 - i
                        one(ins)
                        for f in range(2):
                            w = prm("conv_w", 2 * i + f)
                            x, y = z(ZX_C + f), X1[:, f, :]
                            stt(y[:, sh:SEQ], x[:, 0:SEQ - sh], w, y[:, sh:SEQ], ALU.mult, ALU.add)
                            xs, ysg = segs(x), segs(y)
                            stt(ysg[:, :, sh:TS], xs[:, :, 0:TS - sh], w, ysg[:, :, sh:TS], ALU.mult, ALU.add)
                            ins = stt(ysg[:, :, 0:sh], conv0[:, f, :, i:3], w, ysg[:, :, 0:sh], ALU.mult, ALU.add)
                            if i == 2 and f == 1:
                                sig.up(ins, "xc")
                    v.wait_ge(sig["xc"], 1)
                    v.wait_ge(sig["gg2"], 1)
                    one(ts(T28, T28, 0.07135481282, 1.5957691216, ALU.mult, ALU.add))
                    sig.up(tt(T28, T28, z(ZG_C, 2), ALU.mult), "gg3")
                    for g in range(2):
                        for f in range(2):
                            bk.given(v, ("rg", g, f, 1))
                            bk.given(v, ("rg", g, f, 0))
                    one(tt(X4, X4, X1, ALU.mult))
                    v.wait_ge(sig["ga"], 2)
                    one(tt(X1, X5, X5, ALU.mult))
                    one(stt(X1, X1, 1.0, X2, ALU.add, ALU.mult))
                    sig.up(ts(X1, X1, 1.0e-19, None, ALU.max), "t1")
                    token_shift(0)
                    v.wait_ge(sig["zs"], 1)
                    for i in range(2):
                        ins = ts(kkr[:, i, :], z(ZK_D + i), prm("rwkv_k_k", i), None, ALU.mult)
                    sig.up(ins, "kk1")
                    v.wait_ge(sig["sq1"], 1)
                    one(tt(X4, X4, X1, ALU.mult))
                    one(tt(carry[:, :, 0:8], segs(X5)[:, :, :, 0], h0c, ALU.mult))
                    one(tt(segs(X4)[:, :, :, 0], segs(X4)[:, :, :, 0], carry[:, :, 0:8], ALU.add))
                    one(v.memset(segs(X5)[:, :, :, 0], 0.0))
                    for f in range(2):
                        v.tensor_tensor_scan(X2[:, f, 0:SEQ], X5[:, f, 0:SEQ], X4[:, f, 0:SEQ], 0.0, ALU.mult, ALU.add)
                        ins = v.tensor_tensor_scan(X2[:, f, SEQ:], X5[:, f, SEQ:], X4[:, f, SEQ:], 0.0, ALU.mult, ALU.add)
                    one(ins)
                    v.wait_ge(sig["gg4"], 1)
                    one(tt(T28, T28, z(ZG_C, 2), ALU.mult))
                    v.tensor_copy(oc2[:, 0:2], X2[:, :, SEQ - 1])
                    v.tensor_copy(oc2[:, 2:18].rearrange("p (b f) -> p f b", b=NB), segs(X2)[:, :, :, 3])
                    sig.up(tt(z(ZG_C, 2), X2, T28, ALU.mult), "yC")

                    v.wait_ge(sig["small_w"], 16 * N_SMALL_W)
                    drain(v, ("gates",), graw_rows)
                    for i in range(2):
                        drain(v, ("kk", i), lambda ps, c: ts(kks[:, i, c], ps, 1.0e-24, None, ALU.max))
                    sig.up(v.memset(sm[:, 81:82], 0.0), "ss")
                    token_shift(1)
                    v.wait_ge(sig["zs"], 2)
                    bk.given(v, ("wa", 1, 0))
                    bk.given(v, ("wa", 1, 1))
                    for i in range(2):
                        ins = v.tensor_tensor_scan(X1[:, i, :], const("keep_d"), T28[:, i, :], 0.0, ALU.mult, ALU.add)
                    one(ins)
                    sig.up(tt(X2, X1, T28, ALU.subtract), "S")
                    v.wait_ge(sig["expd"], 3)
                    v.tensor_copy(epc[:, :, 0:8], T28[:, :, 63:SEQ:64])
                    v.tensor_copy(epc[:, :, 8:16], segs(T28)[:, :, :, 3])
                    v.wait_ge(sig["rn"], 1)
                    one(tt(X4, kkr, kks, ALU.mult))
                    tt(X2, X4, X2, ALU.mult)
                    bk.given(v, ("wa", 3, 0))
                    bk.given(v, ("wa", 3, 1))
                    one(tt(X4, X4, T30, ALU.mult))
                    tt(X4, X4, X1, ALU.mult)
                    for i in range(2):
                        ins = ts(T30[:, i, :], T30[:, i, :], prm("rwkv_k_a", i), omka[:, i:i + 1], ALU.mult, ALU.add)
                    one(ins)
                    one(tt(z(ZK_D, 2), z(ZK_D, 2), T30, ALU.mult))
                    for i in range(2):
                        ins = stt(X5[:, i, :], z(ZR_D + i), prm("rwkv_r_k", i), z(ZK_D + i), ALU.mult, ALU.mult)
                    sig.up(ins, "rk")
                    v.wait_ge(sig["rk"], 1)
                    tt(z(ZR_D, 2), z(ZR_D, 2), T28, ALU.mult)
                    sig.up(tt(z(ZK_D, 2), z(ZK_D, 2), X1, ALU.mult), "dfeat")
                    for i in range(2):
                        drain(v, ("bonus", i), lambda ps, c: tt(X5[:, i, c], ps, z(ZV_D + i)[:, c], ALU.mult))
                    bk.take(v, ("orow1",))
                    bk.give(v.tensor_copy(orow1[:126, :], psum[:126, 6, :P]), ("orow1",))

                    for T in range(5):
                        t0, n = TILES[T]
                        mask = const("delta", 2, P) if T < 4 else const("delta_s", 2, NS)
                        for i, dst in enumerate((BM, KM)):
                            for pr in range(2):
                                ps = bk.take(v, ("dsc", T, i, pr)).rearrange("p (a s t) -> p a s t", a=2, s=2)
                                bk.give(tt(dst[:n, pr, :, :, :n], ps[:n, :, :, :n],
                                           mask[:n].unsqueeze(1).broadcast_to([n, 2, 2, n]), ALU.mult), ("dsc", T, i, pr))
                                bk.given(v, ("dsc", T, i, pr))
                        levels = (1, 2, 4, 8, 16, 32) if T < 4 else (1, 2)
                        idb = ident[:n, :n].unsqueeze(1).broadcast_to([n, H, n])
                        for li, m in enumerate(levels):
                            if m == 1:
                                v.wait_ge(sig["om"], OM0[T] + 1)
                                tt(DmT[:n, :, :n], idb, OmT[:n, OM0[T] % 2, :, :n], ALU.subtract)
                                ps = bk.take(v, ("X", T, 1)).rearrange("p (h t) -> p h t", h=H)
                                bk.give(tt(Dm[:n, :, :n], idb, ps[:n, :, :n], ALU.subtract), ("X", T, 1))
                                bk.given(v, ("X", T, 1))
                                continue
                            if m != levels[-1]:
                                ps = bk.take(v, ("D", T, m)).rearrange("p (h t) -> p h t", h=H)
                                bk.give(tt(Dm[:n, :, :n], Dm[:n, :, :n], ps[:n, :, :n], ALU.subtract), ("D", T, m))
                            ps = bk.take(v, ("DT", T, m)).rearrange("p (h t) -> p h t", h=H)
                            bk.give(tt(DmT[:n, :, :n], DmT[:n, :, :n], ps[:n, :, :n], ALU.subtract), ("DT", T, m))
                            bk.given(v, ("DT", T, m))
                        ps = bk.take(v, ("CV", T))
                        bk.give(v.tensor_copy(CV[:n].rearrange("p a b -> p (a b)"), ps[:n, 0:256]), ("CV", T))
                        if T < 4:
                            bk.given(v, ("UV", T))
                            for cc in range(2):
                                c0, cn = 64 * cc, 2 * T + cc
                                ps = bk.take(v, ("SA", cn))
                                bk.give(stt(SAn[c0:c0 + 64].rearrange("p a b -> p (a b)"), ps[c0:c0 + 64, 0:256], -1.0,
                                            UV[c0:c0 + 64].rearrange("p a b -> p (a b)"), ALU.mult, ALU.subtract), ("SA", cn))
                                ps = bk.take(v, ("st", cn))[:, 0:256].rearrange("p (q v) -> p q v", q=2)
                                v.wait_ge(sig["STe"], cn + 1)
                                for pr in range(2):
                                    for a in range(2):
                                        r = slice(a * HD, a * HD + HD)
                                        ins = stt(ST[r, pr, r], ps[r, pr, r], epc[r, pr, cn:cn + 1], STe[r, pr, r], ALU.mult, ALU.add)
                                bk.give(ins, ("st", cn))
                        else:
                            bk.given(v, ("CV", T))
                            ps = bk.take(v, ("KSt",))
                            cv = CV[:n].rearrange("p a b -> p (a b)")
                            bk.give(tt(cv, cv, ps[:n, 0:256], ALU.add), ("KSt",))
                            ps = bk.take(v, ("SAs",))
                            bk.give(ts(SAn[:n].rearrange("p a b -> p (a b)"), ps[:n, 0:256], -1.0, None, ALU.mult), ("SAs",))
                            bk.given(v, ("SAs",))
                            own = const("own")[:n].unsqueeze(2).broadcast_to([n, NB, HD])
                            bk.take(v, ("os",))
                            for h in range(H):
                                if h == 2:
                                    v.wait_ge(sig["SXread"], 1)
                                if h == 3:
                                    bk.take(v, ("sts", 0))
                                tt(OmT[:n, h % 2].rearrange("p a b -> p (a b)").rearrange("p (b v) -> p b v", b=NB),
                                   SAn[:n, h, :].unsqueeze(1).broadcast_to([n, NB, HD]), own, ALU.mult)
                                sig.up(tt((Xm, Dm)[h % 2][:n].rearrange("p a b -> p (a b)").rearrange("p (b v) -> p b v", b=NB),
                                          Dtok[:n, 3, h // 2, (h % 2) * HD:(h % 2) * HD + HD].unsqueeze(1).broadcast_to([n, NB, HD]),
                                          own, ALU.mult), "SX")
                            for pr in range(2):
                                ps = bk.take(v, ("sts", pr)).rearrange("p (b v) -> p b v", b=NB)
                                bk.give(tt(SsT[:, pr], ps, SsT[:, pr], ALU.add), ("sts", pr))
                                bk.given(v, ("sts", pr))
                                sig.up(tt(SsT[:, pr], SsT[:, pr], epc[:, pr, 8:16].unsqueeze(2).broadcast_to([P, NB, HD]), ALU.mult), "Sss")

                    def center(pre, ht):
                        for i in range(2):
                            drain(v, (pre + "mu", i), lambda ps, c: tt(ht[:, i, c], ht[:, i, c], ps, ALU.subtract))
                        sig.up(v.memset(sm[:, 82:83], 0.0), pre + "cen")

                    center("D", X1)
                    for i in range(4):
                        f = (ZQ_B, ZK_B)[i // 2] + i % 2
                        drain(v, ("swap", i), lambda ps, c: tt(rows[0][:, c], ps, const("sin")[:, c], ALU.mult))
                        one(tt(z(f), z(f), const("cos"), ALU.mult))
                        ins = tt(z(f), z(f), rows[0], ALU.add)
                        if i < 3:
                            one(ins)
                    sig.up(ins, "rot")
                    v.wait_ge(sig["rot"], 1)

                    v.wait_ge(sig["Sout"], 16 * (NB + 2))
                    bk.given(v, ("SsB", 1))
                    bk.given(v, ("STb",))
                    one(v.memset(rows[5][0:36, :], 0.0))
                    sig.up(stt(rows[2][32:36, :], graw[32:36, :], -1.0, graw[32:36, :], ALU.mult, ALU.max), "absf")
                    v.wait_ge(sig["Drs"], 1)
                    one(tt(X1, X1, T28, ALU.mult))
                    for i in range(2):
                        ins = ts(X1[:, i, :], X1[:, i, :], prm("rwkv_lnx_g", i), prm("rwkv_lnx_b", i), ALU.mult, ALU.add)
                    one(ins)
                    one(tt(X1, X1, X5, ALU.add))
                    sig.up(tt(z(ZR_D, 2), X1, z(26, 2), ALU.mult), "yD")

                    v.wait_ge(sig["yD"], 1)
                    v.memset(Cb, 0.0)
                    v.memset(ncol, 0.0)
                    v.memset(nb_, 0.0)
                    v.memset(qspad, 0.0)
                    v.memset(qspad_b, 0.0)
                    sig.up(v.memset(Rb, 0.0), "Azero")
                    v.wait_ge(sig["Azero"], 1)
                    v.wait_ge(sig["lnf"], 1)
                    one(stt(rows[3][0:4, :], graw[32:36, :], 0.0, rows[2][32:36, :], ALU.min, ALU.subtract))
                    one(v.tensor_tensor_scan(rows[4][0:4, :], const("keep_a")[0:4], rows[3][0:4, :], 0.0, ALU.mult, ALU.add))
                    one(tt(rows[5][0:4, :], graw[0:4, :], rows[4][0:4, :], ALU.subtract))
                    one(v.tensor_copy(rows[0][0:4, :], rows[5][0:4, :]))
                    v.wait_ge(sig["m0"], 16)
                    one(tt(segs(rows[0])[0:4, :, 0], segs(rows[0])[0:4, :, 0], m0[0:4, :], ALU.max))
                    G, b_, g_ = rows[1][0:4], rows[4][0:4], rows[5][0:4]
                    for T in range(4):
                        c = slice(T * P, T * P + P)
                        one(v.tensor_tensor_scan(G[:, c], const("drop_a")[0:4, c], rows[0][0:4, c],
                                                 mcar[0:4, T - 1:T] if T else 0.0, ALU.add, ALU.max))
                        e = T * P + P - 1
                        one(tt(mcar[0:4, T:T + 1], b_[:, e:e + 1], G[:, e:e + 1], ALU.add))
                        ts(rows[3][0:4, c], G[:, c], -1.0, mcar[0:4, T - 1:T] if T else 0.0, ALU.mult, ALU.add)
                        ts(rows[5][32:36, c], g_[:, c], G[:, e:e + 1], None, ALU.subtract)
                    one(v.tensor_tensor_scan(G[:, SEQ:], const("drop_a")[0:4, SEQ:], rows[0][0:4, SEQ:], 0.0, ALU.add, ALU.max))
                    Gs = segs(G)
                    tt(segs(rows[3][0:4]), m0[0:4, :].unsqueeze(2).broadcast_to([4, NB, TS]), Gs, ALU.subtract)
                    tt(segs(rows[5][32:36]), segs(g_), Gs[:, :, 3:4].broadcast_to([4, NB, TS]), ALU.subtract)
                    one(tt(rows[2][0:4, :], b_, G, ALU.add))
                    sig.up(v.tensor_copy(m0[0:4, :], segs(rows[2][0:4])[:, :, 3]), "mrows")
                    sig.up(ts(G, G, -1.0, None, ALU.mult), "negG")
                    for pr in range(2):
                        v.tensor_copy(n0x[:, pr], n0c[:, pr, :].unsqueeze(2).broadcast_to([P, NB, HD]))
                    for q in range(2):
                        for pr in range(2):
                            bk.given(v, ("bcA", q, pr, 0))
                            bk.given(v, ("bcA", q, pr, 1))
                    v.tensor_copy(carry[:, :, 0:4], X2[:, :, P - 1:SEQ:P])
                    one(v.tensor_copy(carry[:, :, 4:12], segs(X2)[:, :, :, 3]))
                    one(tt(X2, X2, z(ZQ_A, 2), ALU.mult))
                    for a in range(2):
                        r = slice(a * HD, a * HD + HD)
                        ins = v.tensor_copy(qspad[r, :, a, :], X2[r, :, SEQ:])
                    sig.up(ins, "Aqs")

                    def keys_values(pre, T):
                        n = TILES[T][1]
                        if pre == "A":
                            ps = bk.take(v, ("Agc", T))
                            bk.give(v.tensor_copy(gcol[:n, :], ps[:n, 0:36]), ("Agc", T))
                            bk.given(v, ("Agc", T))
                            weight, k_, v_ = gcol[:n, 32:36], kw, vt
                        else:
                            weight, k_, v_ = const("zeta" if T < 4 else "zeta_s")[:n], kw_b, vt_b
                        ps = bk.take(v, (pre + "tr", T)).rearrange("p (h c) -> p h c", h=8)
                        tt(k_[:n].rearrange("p q (a c) -> p (q a) c", a=2), ps[:n, 0:4, :],
                           weight.unsqueeze(2).broadcast_to([n, H, HD]), ALU.mult)
                        bk.give(v.tensor_copy(v_[:n].rearrange("p q (a c) -> p (q a) c", a=2), ps[:n, 4:8, :]), (pre + "tr", T))

                    def exponents(T):
                        n = TILES[T][1]
                        ps = bk.take(v, ("AG", T)).rearrange("p (h t) -> p h t", h=H)
                        mask = const("causal" if T < 4 else "causal_s")[:n, :n]
                        for h in range(H):
                            ins = stt(Em[:n, h, :n], ps[:n, h, :n], gcol[:n, h:h + 1], mask, ALU.add, ALU.min)
                        bk.give(ins, ("AG", T))

                    def weights(pre, T):
                        n = TILES[T][1]
                        if pre == "A":
                            v.wait_ge(sig["AE"], T + 1)
                            factor, w_ = Em[:n, :, :n], Wm
                        else:
                            factor, w_ = (const("decay", H, P) if T < 4 else const("decay_s", H, NS))[:n], Wm_b
                        ps = bk.take(v, (pre + "sc", T)).rearrange("p (h t) -> p h t", h=H)
                        bk.give(tt(w_[:n, :, :n], ps[:n, :, :n], factor, ALU.mult), (pre + "sc", T))

                    def normalise(T):
                        t0, n = TILES[T]
                        ps = bk.take(v, ("And", T)).rearrange("p (w q t) -> p w q t", w=2, q=2)
                        one(stt(rden[:, :, :n], ps[:, 1, :, :n], -1.0, X4[:, :, t0:t0 + n], ALU.mult, ALU.max))
                        one(tt(rden[:, :, :n], ps[:, 1, :, :n], rden[:, :, :n], ALU.max))
                        one(v.reciprocal(rden[:, :, :n], rden[:, :, :n]))
                        bk.give(tt(z(ZQ_A, 2)[:, :, t0:t0 + n], ps[:, 0, :, :n], rden[:, :, :n], ALU.mult), ("And", T))

                    def prompt_state(pre, T):
                        ps = bk.take(v, (pre + "st", T))
                        state = Cb if pre == "A" else Rb
                        for pr in range(2):
                            if pre == "A":
                                stt(ncol[:, pr:pr + 1], ncol[:, pr:pr + 1], carry[:, pr, T:T + 1],
                                    ps[:, 256 + pr:257 + pr], ALU.mult, ALU.add)
                            for a in range(2):
                                r = slice(a * HD, a * HD + HD)
                                c = carry[r, pr, T:T + 1] if pre == "A" else const("g_chunk")[r, pr:pr + 1]
                                ins = stt(state[r, pr, r], state[r, pr, r], c, ps[r, pr * P + a * HD:pr * P + a * HD + HD],
                                          ALU.mult, ALU.add)
                        bk.give(ins, (pre + "st", T))
                        bk.given(v, (pre + "st", T))
                        if pre == "A":
                            for pr in range(2):
                                ins = ts(nb_[:, pr, :], const("sum64"), ncol[:, pr:pr + 1], None, ALU.mult)
                            if T == 3:
                                v.tensor_copy(oc2[:, 18:20], ncol)
                        if pre == "A" and T < 3:
                            sig.up(ins, "Astate")
                        else:
                            sig.up(v.memset(sm[:, 83:84], 0.0), pre + "state")

                    def decode_states(pre):
                        n, T = NS, 4
                        v_, x_ = (vt, vx2) if pre == "A" else (vt_b, vx2_b)
                        own = const("own")[:n].unsqueeze(2).broadcast_to([n, NB, HD])
                        bk.given(v, (pre + "tr", T))
                        for h in range(H):
                            if h == 2:
                                v.wait_ge(sig[pre + "vxread"], 1)
                            if h == 3:
                                bk.take(v, (pre + "sts", 0))
                            sig.up(tt(x_[:n, h % 2], v_[:n, h // 2, (h % 2) * HD:(h % 2) * HD + HD].unsqueeze(1)
                                      .broadcast_to([n, NB, HD]), own, ALU.mult), pre + "vx")
                        for pr in range(2):
                            bk.take(v, (pre + "nd", T))
                            if pre == "A":
                                one(tt(Cs[:, pr], Cs[:, pr], carry[:, pr, 4:12].unsqueeze(2).broadcast_to([P, NB, HD]), ALU.mult))
                            ps = bk.take(v, (pre + "sts", pr)).rearrange("p (b c) -> p b c", b=NB)
                            if pre == "A":
                                ins = tt(Cs[:, pr], Cs[:, pr], ps, ALU.add)
                            else:
                                ins = stt(Rs[:, pr], Rs[:, pr], const("g_chunk_s")[:, pr:pr + 1], ps, ALU.mult, ALU.add)
                            bk.give(ins, (pre + "sts", pr))
                        if pre == "A":
                            ns = oc2[:, 20:36].rearrange("p (b q) -> p q b", b=NB)
                            one(tt(ns, n0c, carry[:, :, 4:12], ALU.mult))
                            ps = bk.take(v, ("Ans",))[:, 0:16].rearrange("p (q b) -> p q b", q=2)
                            bk.give(tt(ns, ns, ps, ALU.add), ("Ans",))
                            bk.given(v, ("Ans",))
                            sig.up(v.memset(sm[:, 84:85], 0.0), "oc2")
                        bk.given(v, (pre + "nd", T))
                        sig.up(v.memset(sm[:, 85:86], 0.0), pre + "h")

                    for T in range(5):
                        keys_values("A", T)
                        exponents(T)
                        keys_values("B", T)
                        weights("B", T)
                        weights("A", T)
                        if T < 4:
                            prompt_state("B", T)
                            normalise(T)
                            prompt_state("A", T)
                        else:
                            decode_states("B")
                            normalise(T)
                            decode_states("A")
                    ps = bk.take(v, ("orow2",))
                    bk.give(v.tensor_copy(orow2[:36, :], ps[:36, :P]), ("orow2",))
                    center("A", z(ZQ_A, 2))
                    center("B", z(ZQ_B, 2))
                    for pre, q0, g0, sq, gain in (("A", ZQ_A, ZO_A, X2, "mlstm_g"), ("B", ZQ_B, ZG_B, X4, "ret_g")):
                        v.wait_ge(sig[pre + "rs"], 1)
                        one(tt(z(q0, 2), z(q0, 2), sq, ALU.mult))
                        for i in range(2):
                            ins = stt(z(g0 + i), z(q0 + i), prm(gain, i), z(g0 + i), ALU.mult, ALU.mult)
                        sig.up(ins, "y" + pre)

                @block.scalar
                def _(s):
                    act = s.activation
                    def lam_decay():
                        s.wait_ge(sig["lam"], 1)
                        after(s, act(lamc[:, 0, :], lamc[:, 0, :], ACT.Exp, scale=-1.0), "s")

                        sig.up(act(lamc[:, 0, :], lamc[:, 0, :], ACT.Ln, bias=1.0), "lamln")

                    def z_tiles(n, tiles=range(4)):
                        for i in tiles:
                            for half, c in HALVES:
                                z_half(SLABS_IN[n][1] + i, half, c)

                    def z_half(f, half, c):
                        fn = ACT.Sigmoid if f in (6, 7) else ACT.Silu if f in (14, 15) else ACT.Copy
                        scale = QSCALE if f in (2, 3, 10, 11) else 1.0
                        ps = bk.take(s, ("z", f, half))
                        bk.give(act(z(f)[:, c], ps[:, 0:c.stop - c.start], fn, scale=scale), ("z", f, half))

                    def spare_tiles(point):
                        while spare_read[0] < HALF_DONE[point]:
                            n, f, half, _ = SPARE[KC * spare_read[0]]
                            z_half(f, half, HALVES[half][1])
                            spare_read[0] += 1

                    spare_read = [0]

                    def both(key, dst, fn, **kw_):
                        drain(s, key, lambda ps, c: act(dst[:, c], ps, fn, **kw_))

                    z_tiles(0)
                    for pr in range(2):
                        ps = bk.take(s, ("SsT", pr))
                        bk.give(act(SsT[:, pr].rearrange("p b v -> p (b v)"), ps, ACT.Copy), ("SsT", pr))
                    lam_decay()
                    z_wait(s, 19)
                    sig.up(act(T28, z(ZG_C, 2), ACT.Square), "gg2")
                    z_tiles(1)
                    for g in range(2):
                        for f in range(2):
                            both(("rg", g, f), (X2, X4)[g][:, f, :], ACT.Sigmoid, bias=prm(("rg_b_a", "rg_b_x")[g], f))
                    s.wait_ge(sig["gg3"], 1)
                    sig.up(act(T28, T28, ACT.Sigmoid), "gg4")
                    s.wait_ge(sig["lamc"], 1)
                    for f in range(2):
                        act(X5[:, f, :], X2[:, f, :], ACT.Exp, scale=lamc[:, 2, f:f + 1])
                    for f in range(2):
                        sig.up(act(X2[:, f, :], X2[:, f, :], ACT.Tanh, scale=lamc[:, 1, f:f + 1]), "ga")
                    z_tiles(2)
                    s.wait_ge(sig["t1"], 1)
                    after(s, act(X1, X1, ACT.Ln), "s")
                    sig.up(act(X1, X1, ACT.Exp, scale=0.5), "sq1")
                    s.wait_ge(sig["kk1"], 1)
                    sig.up(act(kks, kkr, ACT.Square), "kk2")
                    z_tiles(3, (0, 1, 2))
                    s.wait_ge(sig["zs"], 2)
                    sig.up(act(z(26)[0:64, :], z(26)[0:64, :], ACT.Tanh), "act_d")
                    sig.up(act(z(27), z(27), ACT.Sigmoid), "act_d")
                    for i in range(4):
                        both(("wa", i), z(28 + i), ACT.Sigmoid, bias=prm(("rwkv_w0", "rwkv_a0")[i // 2], i % 2))
                    for i in range(2):
                        both(("g2", i), z(26 + i), ACT.Copy)
                    s.wait_ge(sig["ss"], 1)
                    after(s, act(kks, kks, ACT.Ln, scale=1048576.0), "s")
                    sig.up(act(kks, kks, ACT.Exp, scale=-0.5, bias=const("eps")[:, 2:3]), "rn")
                    z_tiles(3, (3,))
                    s.wait_ge(sig["S"], 1)
                    sig.up(act(X2, X2, ACT.Exp, scale=-RW_C), "expd")
                    sig.up(act(T28, X1, ACT.Exp, scale=-RW_C), "expd")
                    s.wait_ge(sig["expd"], 2)
                    sig.up(act(X1, X1, ACT.Exp, scale=RW_C), "expd")
                    spare_tiles("bonus")

                    for T in range(5):
                        t0, n = TILES[T]
                        for i in range(2):
                            ps = bk.take(s, ("dtok", T, i))
                            bk.give(act(Dtok[:n, 2 * i:2 * i + 2].rearrange("p a q c -> p (a q c)"), ps[:n, :], ACT.Copy), ("dtok", T, i))
                        levels = (1, 2, 4, 8, 16, 32) if T < 4 else (1, 2)
                        spare_tiles(("dsc", T))
                        for m in levels[1:]:
                            spare_tiles(("om", T, m))
                            ps = bk.take(s, ("X", T, m)).rearrange("p (h t) -> p h t", h=H)
                            bk.give(act(Xm[:n, :, :n], ps[:n, :, :n], ACT.Copy), ("X", T, m))
                        spare_tiles(("inv", T))
                        if T < 4:
                            ps = bk.take(s, ("WK", T))
                            bk.give(act(WKT.rearrange("p a b -> p (a b)"), ps[:, 0:256], ACT.Copy), ("WK", T))
                            ps = bk.take(s, ("UV", T))
                            bk.give(act(UV.rearrange("p a b -> p (a b)"), ps[:, 0:256], ACT.Copy), ("UV", T))
                            spare_tiles(("UV", T))
                            for cc in range(2):
                                cn = 2 * T + cc
                                if cn:
                                    spare_tiles(("state", cn))
                                    bk.given(s, ("st", cn - 1))
                                for pr in range(2):
                                    ins = act(STe[:, pr, :], ST[:, pr, :], ACT.Copy, scale=epc[:, pr, cn:cn + 1])
                                sig.up(ins, "STe")
                                ps = bk.take(s, ("o", cn))[:, 0:128].rearrange("p (q t) -> p q t", q=2)
                                bk.give(act(X1[:, :, t0 + 64 * cc:t0 + 64 * cc + 64], ps, ACT.Copy), ("o", cn))
                        else:
                            spare_tiles(("inv", T))
                            ps = bk.take(s, ("KS",))
                            bk.give(act(Xm[:, 0, 0:64], ps[:, 0:64], ACT.Copy), ("KS",))
                            ps = bk.take(s, ("os",))[:, 0:64].rearrange("p (q t) -> p q t", q=2)
                            spare_tiles(("SAs",))
                            bk.give(act(X1[:, :, SEQ:], ps, ACT.Copy), ("os",))
                            bk.given(s, ("os",))
                            sig.up(s.copy(sm[:, 86:87], const("eps")[:, 0:1]), "Dh")
                            spare_tiles(("Sss",))
                            for pr in range(2):
                                ps = bk.take(s, ("SsB", pr)).rearrange("p (b c) -> p b c", b=4)
                                bk.give(act(Sraw[:, :, 2 * pr:2 * pr + 2, :].rearrange("p b a c -> p b (a c)"), ps, ACT.Copy), ("SsB", pr))
                            ps = bk.take(s, ("STb",))[:, 0:256].rearrange("p (q v) -> p q v", q=2)
                            for a in range(2):
                                r = slice(a * HD, a * HD + HD)
                                ins = act(CV[r, 0:2, :], ps[r, :, r], ACT.Copy)
                            bk.give(ins, ("STb",))

                    def norm(*heads):
                        for pre, ht, sq, eps in heads:
                            s.wait_ge(sig[pre + "cen"], 1)
                            sig.up(act(sq, ht, ACT.Square), pre + "sq")
                        for pre, ht, sq, eps in heads:
                            for i in range(2):
                                both((pre + "var", i), sq[:, i, :], ACT.Ln, bias=const("eps")[:, eps:eps + 1])
                        for pre, ht, sq, eps in heads:
                            sig.up(act(sq, sq, ACT.Exp, scale=-0.5), pre + "rs")

                    spare_tiles("Dnorm")
                    norm(("D", X1, T28, 1))
                    s.wait_ge(sig["absf"], 1)
                    after(s, act(rows[2][32:36, :], rows[2][32:36, :], ACT.Exp, scale=-1.0), "s")
                    sig.up(act(rows[2][32:36, :], rows[2][32:36, :], ACT.Ln, bias=1.0), "lnf")
                    s.wait_ge(sig["mrows"], 1)
                    act(rows[3][0:4, :], rows[3][0:4, :], ACT.Exp)
                    act(rows[2][0:4, :], rows[2][0:4, :], ACT.Exp, scale=-1.0)
                    sig.up(act(rows[5][32:36, :], rows[5][32:36, :], ACT.Exp), "rowsA")
                    for q in range(2):
                        for pr in range(2):
                            both(("bcA", q, pr), (X2, X4)[q][:, pr, :], ACT.Copy)
                    for T in range(5):
                        n = TILES[T][1]
                        bk.given(s, ("AG", T))
                        sig.up(act(Em[:n, :, :n], Em[:n, :, :n], ACT.Exp), "AE")
                        t0 = TILES[T][0]
                        ps = bk.take(s, ("Bnd", T)).rearrange("p (w q t) -> p w q t", w=2, q=2)
                        bk.give(act(z(ZQ_B, 2)[:, :, t0:t0 + n], ps[:, 0, :, :n], ACT.Copy), ("Bnd", T))
                    norm(("A", z(ZQ_A, 2), X2, 0), ("B", z(ZQ_B, 2), X4, 0))

                @block.gpsimd
                def _(g):
                    def done(ins, name="g"):
                        after(g, ins, name)

                    done(g.memset(wgate, 0.0))
                    done(g.memset(wax, 0.0))
                    done(g.memset(wwa, 0.0), "wzero")
                    g.wait_ge(sig["y"], 32)
                    done(g.memset(dpad, 0.0))
                    for gr in range(2):
                        if gr == 0:
                            z_wait(g, 23)
                            g.wait_ge(sig["rows"], 16 * N_ROW_DMAS)
                            bk.given(g, ("prow",))
                        else:
                            z_wait(g, 27)
                            g.wait_ge(sig["yC"], 1)
                        a, d = z(20 + 4 * gr, 4), (d_first, z(28, 4))[gr]
                        done(g.tensor_tensor(d[:, :, 1:SEQ], a[:, :, 0:SEQ - 1], a[:, :, 1:SEQ], ALU.subtract))
                        done(g.tensor_scalar(d[:, :, 0:1], a[:, :, 0:1], -1.0, None, ALU.mult))
                        for f in range(4):
                            av, dv = segs(z(20 + 4 * gr + f)), segs(d[:, f, :])
                            done(g.tensor_tensor(dv[:, :, 1:TS], av[:, :, 0:TS - 1], av[:, :, 1:TS], ALU.subtract))
                        ins = g.tensor_tensor(segs(d)[:, :, :, 0], sh0[:, 4 * gr:4 * gr + 4, :], segs(a)[:, :, :, 0], ALU.subtract)
                        done(ins, "delta")
                    for T in range(5):
                        t0, n = TILES[T]
                        if T == 0:
                            g.wait_ge(sig["dfeat"], 1)
                        else:
                            bk.given(g, ("dsc", T - 1, 1, 1))
                            bk.given(g, ("dsc", T - 1, 1, 0))
                        for a in range(2):
                            r = slice(a * HD, a * HD + HD)
                            done(g.tensor_copy(dpad[r, :, a, 0, :n], X2[r, :, t0:t0 + n]))
                            done(g.tensor_copy(dpad[r, :, a, 1, :n], z(ZR_D, 2)[r, :, t0:t0 + n]), "dpad")
                        bk.given(g, ("dsc", T, 0, 1))
                        bk.given(g, ("dsc", T, 0, 0))
                        levels = (1, 2, 4, 8, 16, 32) if T < 4 else (1, 2)
                        for li, m in enumerate(levels):
                            if li >= 2:
                                bk.given(g, ("X", T, levels[li - 2]))
                            if li == 0 and T:
                                bk.given(g, ("st", 2 * T - 1))
                            k = (OM0[T] + li) % 2
                            done(g.tensor_tensor(OmT[:n, k].rearrange("p (q a) t -> p q a t", q=2)[:, :, :, :n], BM[:n, :, :, 0, :n],
                                                   const(f"level{m}")[:n, :n].unsqueeze(1).unsqueeze(1).broadcast_to([n, 2, 2, n]),
                                                   ALU.mult), "om")
                    bk.given(g, ("os",))
                    bk.given(g, ("sts", 1))
                    bk.given(g, ("dsc", 4, 1, 1))
                    done(g.memset(qpad, 0.0))
                    done(g.memset(qpad_b, 0.0))
                    for T in range(5):
                        t0, n = TILES[T]
                        for pre, q0, pad in (("A", ZQ_A, qpad), ("B", ZQ_B, qpad_b)):
                            if pre == "B" and T == 0:
                                g.wait_ge(sig["rot"], 1)
                            if T:
                                bk.given(g, (pre + "sc", T - 1))
                            for a in range(2):
                                r = slice(a * HD, a * HD + HD)
                                done(g.tensor_copy(pad[r, :, a, :n], z(q0, 2)[r, :, t0:t0 + n]), pre + "pad")
                        if T < 4:
                            if T:
                                bk.given(g, ("Bnd", T - 1))
                            done(g.tensor_tensor(qx, z(ZQ_B, 2)[:, :, t0:t0 + n], const("xi", 2, P), ALU.mult), "Bqx")
                        else:
                            g.wait_ge(sig["Azero"], 1)
                            for a in range(2):
                                r = slice(a * HD, a * HD + HD)
                                done(g.tensor_tensor(qspad_b[r, :, a, :], z(ZQ_B, 2)[r, :, SEQ:], const("xi_s", 2, NS)[r], ALU.mult), "Bqs")

                @block.sync
                def _(sp):
                    def lay(name):
                        return A[name][bass.ds(l, 1)]

                    def slab(n, src):
                        slab_read(sp, n - 2)
                        sp.dma_start(wring[:, n % 2], src).then_inc(sig[f"slab{n % 2}"], 16)

                    def in_slab(n):
                        c0 = SLABS_IN[n][0]
                        slab(n, A["w_in"][bass.ds(l, 1), :, c0:c0 + W512].rearrange("a (c p) n -> p (a c) n", p=P))

                    sp.dma_start(yp, xk[:, 0:4, :]).then_inc(sig["y"], 16)
                    sp.dma_start(ys, xk[:NS, 4, :]).then_inc(sig["y"], 16)
                    for name, (r0, k) in ROWS.items():
                        a = lay(name)
                        if name == "state_rwkv_shift" or name == "state_rglru_h":
                            a = a.rearrange("a b (f p) -> (a b f) p", p=P)
                        elif name == "conv_w":
                            a = a.rearrange("a i (f p) -> (a i f) p", p=P)
                        elif name == "rwkv_r_k":
                            a = a.rearrange("a (f h) d -> (a f) (h d)", h=2)
                        else:
                            a = a.rearrange("a (f p) -> (a f) p", p=P)
                        sp.dma_start(prow[r0:r0 + k, :], a).then_inc(sig["rows"], 16)
                    sp.dma_start(prow2[0:48, :], lay("state_rglru_conv").rearrange("a b i (f p) -> (a b i f) p", p=P)).then_inc(sig["rows"], 16)
                    sp.dma_start(prow2[48:64, :], lay("state_mlstm_n").rearrange("a b (q h) d -> (a b q) (h d)", h=2)).then_inc(sig["rows"], 16)
                    sp.wait_ge(sig["y"], 32)
                    for b in range(NB):
                        src = A["state_rwkv_S"][bass.ds(l, 1), b].rearrange("a h v k -> v (a h) k")
                        sp.dma_start(Sraw[(b % 2) * HD:(b % 2) * HD + HD, b // 2], src).then_inc(sig["Sraw"], 16)

                    sp.wait_ge(sig["wzero"], 1)
                    w = sig["small_w"]
                    gsrc = A["w_in"][bass.ds(l, 1), :, GATE_COL:GATE_COL + 8].rearrange("a (c p) n -> p (a c) n", p=P)
                    sp.dma_start(wgate[:, :, 0:4], gsrc[:, :, 0:4]).then_inc(w, 16)
                    sp.dma_start(wgate[:, :, 32:36], gsrc[:, :, 4:8]).then_inc(w, 16)
                    for i, name in enumerate(("rg_w_a", "rg_w_x")):
                        for a in range(2):
                            r = slice(a * HD, a * HD + HD)
                            src = A[name][bass.ds(l, 1)].rearrange("z (q a) i j -> a i (z q) j", a=2)[a]
                            sp.dma_start(wax[r, i, :, r], src).then_inc(w, 16)
                    for i, name in enumerate(("rwkv_w2", "rwkv_a2")):
                        sp.dma_start(wwa[i * 64:i * 64 + 64, 2 * i:2 * i + 2, :].rearrange("p f c -> p (f c)"),
                                     A[name][bass.ds(l, 1)].rearrange("a k n -> (a k) n")).then_inc(w, 16)
                    sp.dma_start(wg2.rearrange("p f c -> p (f c)"), A["rwkv_g2"][bass.ds(l, 1)].rearrange("a k n -> (a k) n")).then_inc(w, 16)
                    sp.dma_start(bif[0:4, 0:1], A["mlstm_b_i"][bass.ds(l, 1)].rearrange("a h -> h a"), allow_slow_non_contiguous=True).then_inc(w, 16)
                    sp.dma_start(bif[32:36, 1:2], A["mlstm_b_f"][bass.ds(l, 1)].rearrange("a h -> h a"), allow_slow_non_contiguous=True).then_inc(w, 16)
                    sp.dma_start(m0[0:4, :], A["state_mlstm_m"][bass.ds(l, 1)].rearrange("a b h -> h (a b)"),
                                 allow_slow_non_contiguous=True).then_inc(sig["m0"], 16)
                    for n in range(2, 7):
                        in_slab(n)

                    def put(name, src, view, waits):
                        waits()
                        sp.dma_start(view(O[name][bass.ds(l, 1)]), src, allow_slow_non_contiguous=name in ("p_m", "s_m")).then_inc(sig["out1"], 16)
                        N_OUT1.append(1)

                    bk.given(sp, ("orow1",))
                    put("p_shift", orow1[0:8, :], lambda o: o.rearrange("a b (f p) -> (a b f) p", p=P), lambda: None)
                    put("s_shift", orow1[8:72, :], lambda o: o.rearrange("a b (f p) -> (a b f) p", p=P), lambda: None)
                    put("p_conv", orow1[72:78, :], lambda o: o.rearrange("a b i (f p) -> (a b i f) p", p=P), lambda: None)
                    put("s_conv", orow1[78:126, :], lambda o: o.rearrange("a b i (f p) -> (a b i f) p", p=P), lambda: None)
                    bk.given(sp, ("SsB", 1))
                    bk.given(sp, ("STb",))
                    for b in range(NB):
                        sp.dma_start(O["s_S"][bass.ds(l, 1), b].rearrange("a h v k -> v (a h) k"),
                                     Sraw[(b % 2) * HD:(b % 2) * HD + HD, b // 2]).then_inc(sig["Sout"], 16)
                    for a in range(2):
                        sp.dma_start(O["p_S"][bass.ds(l, 1), 0].rearrange("z (q a) v k -> a v (z q) k", a=2)[a],
                                     CV[a * HD:a * HD + HD, 0:2, :]).then_inc(sig["Sout"], 16)
                    sp.wait_ge(sig["yD"], 1)
                    sp.wait_ge(sig["Sout"], 16 * (NB + 2))
                    for name, dst, sem in (("state_mlstm_C", Cs, "As"), ("state_ret", Rs, "Bs")):
                        for pr in range(2):
                            src = A[name][bass.ds(l, 1), :, 2 * pr:2 * pr + 2].rearrange("a b h k v -> (h k) (a b) v")
                            sp.dma_start(dst[:, pr], src).then_inc(sig[sem], 16)
                    out_slab(sp, 7)
                    sp.wait_ge(sig["mrows"], 1)
                    put("p_m", mcar[0:4, 3:4], lambda o: o.rearrange("a b h -> h (a b)"), lambda: None)
                    put("s_m", m0[0:4, :], lambda o: o.rearrange("a b h -> h (a b)"), lambda: None)
                    for pre, st, ss, pn, sn in (("A", Cb, Cs, "p_C", "s_C"), ("B", Rb, Rs, "p_R", "s_R")):
                        sp.wait_ge(sig[pre + "state"], 4)
                        if pre == "B":
                            out_slab(sp, 8)
                        for a in range(2):
                            r = slice(a * HD, a * HD + HD)
                            put(pn, st[r, :, r], lambda o: o[:, 0].rearrange("z (q a) k v -> a k (z q) v", a=2)[a], lambda: None)
                        for pr in range(2):
                            bk.given(sp, (pre + "sts", pr))
                            put(sn, ss[:, pr], lambda o: o[:, :, 2 * pr:2 * pr + 2].rearrange("a b h k v -> (h k) (a b) v"), lambda: None)
                    bk.given(sp, ("orow2",))
                    put("p_h", orow2[0:2, :], lambda o: o.rearrange("a b (f p) -> (a b f) p", p=P), lambda: None)
                    put("s_h", orow2[2:18, :], lambda o: o.rearrange("a b (f p) -> (a b f) p", p=P), lambda: None)
                    put("p_n", orow2[18:20, :], lambda o: o.rearrange("a b (q h) d -> (a b q) (h d)", h=2), lambda: None)
                    put("s_n", orow2[20:36, :], lambda o: o.rearrange("a b (q h) d -> (a b q) (h d)", h=2), lambda: None)



            qT = z(0, 8)
            aT = z(8, 8)
            KpT = cols(big, 16 * NT, KC, NMEM)
            Vp = cols(big, 16 * NT + 2048, 2, D)
            Kr = cols(big, 16 * NT + 4096, 2, 2, D)
            Vr = cols(tmp, 2048, 2, 2, D)
            kpt = cols(tmp, 6144, 2, D)
            KbT = [KpT, cols(tmp, 6144, KC, NMEM)]
            memT = cols(tmp, 8192, KC, NMEM)
            Pm = cols(tmp, 8192, H, NMEM)
            pT = cols(tmp, 9216, H, 2, P)
            Ps = cols(tmp, 8448, NMEM)
            pTs = cols(tmp, 8704, 2, P)
            mx = cols(tmp, 10240, 4)
            sums = cols(tmp, 10244, 4)
            inv = cols(tmp, 10248, 4)
            mems = Kr[:, 0]
            qOwn = cols(xT, 0, NB, KC, NS)
            pOwn = cols(xT, 2048, NB, 2, P)
            V_SLOTS = [Vr[:, 0], Vr[:, 1], Kr[:, 0], Kr[:, 1]]
            pvs = cols(tmp, 10260, 2, W512)
            Y = [z(f) for f in (6, 7, 14, 15, 18, 19, 20, 21)]


            def project_tensor(pe, pre, left, slabs, i):
                w = [slab_pe(pe, n) for n in slabs]
                for T in range(5):
                    t0, n = TILES[T]
                    for half in range(2):
                        ps = bk.begin(pe, (pre, T, half), 2 * (T % 2) + half)
                        for k in range(KC):
                            ins = pe.matmul(ps[:n, :], left[k][:, t0:t0 + n], w[half][:, k, :], start=(k == 0), stop=(k == KC - 1))
                        bk.filled(ins, (pre, T, half))
                    if T >= 2:
                        turn_x_tensor(pe, bk, sig, i, T - 2, (4, 5))


            def residual(v, key, T, half):
                n = TILES[T][1]
                x = xk[:n, T, half * W512:half * W512 + W512]
                ps = bk.take(v, key)
                bk.give(v.scalar_tensor_tensor(x, x, ALPHA, ps[:n, :], ALU.mult, ALU.add), key)
                bk.given(v, key)


            with nc.Block() as block:

                @block.tensor
                def _(pe):
                    project_tensor(pe, "wout", Y, (7, 8), 0)
                    pe.wait_ge(sig["mem"], 16)
                    for nt in range(2):
                        for g in range(2):
                            ps = bk.begin(pe, ("memT", nt, g), 6 + g).rearrange("p (c t) -> p c t", c=4)
                            for c in range(4):
                                k = 4 * g + c
                                ins = pe.transpose(ps[:, c, :], mems[:, nt, k * P:(k + 1) * P], ident)
                            bk.filled(ins, ("memT", nt, g))
                    for nt in range(2):
                        for g in range(2):
                            bk.given(pe, ("memT", nt, g))
                    for s_ in range(4):
                        w = slab_pe(pe, 9 + s_)
                        for nt in range(2):
                            ps = bk.begin(pe, ("kv", s_, nt), 6 + nt)
                            for k in range(KC):
                                ins = pe.matmul(ps, memT[:, k, nt * P:(nt + 1) * P], w[:, k, :], start=(k == 0), stop=(k == KC - 1))
                            bk.filled(ins, ("kv", s_, nt))
                        if s_ < 2:
                            turn_x_tensor(pe, bk, sig, 0, 3 + s_, (4, 5))
                        if s_ == 2:
                            for nt in range(2):
                                bk.given(pe, ("kv", 1, nt))
                            for nt in range(2):
                                for g in range(2):
                                    ps = bk.begin(pe, ("KpT", nt, g), 4 + g).rearrange("p (c t) -> p c t", c=4)
                                    for c in range(4):
                                        k = 4 * g + c
                                        ins = pe.transpose(ps[:, c, :], kpt[:, nt, k * P:(k + 1) * P], ident)
                                    bk.filled(ins, ("KpT", nt, g))
                    for g in range(2):
                        bk.given(pe, ("xT", 0, 4, g))
                    for n in (13, 14):
                        w = slab_pe(pe, n)
                        for i in range(4):
                            f = 4 * (n - 13) + i
                            x_product(pe, ("q", f), f % 2, [w[:, k, i * P:(i + 1) * P] for k in range(KC)])
                    for nt in range(2):
                        bk.given(pe, ("kv", 3, nt))
                        bk.given(pe, ("KpT", 1, nt))
                    for f in (6, 7):
                        bk.given(pe, ("q", f, 0))
                        bk.given(pe, ("q", f, 1))

                    def scores(T):
                        t0, n = TILES[T]
                        for hp in range(2):
                            ps = bk.begin(pe, ("s", T, hp), 4 + hp).rearrange("p (a n) -> p a n", a=2)
                            for a in range(2):
                                for c in range(2):
                                    k = 2 * (2 * hp + a) + c
                                    ins = pe.matmul(ps[:, a, :], qT[:, k, t0:t0 + n], KpT[:, k, :], start=(c == 0), stop=(c == 1))
                            bk.filled(ins, ("s", T, hp))

                    def turn_keys(b):
                        pe.wait_ge(sig[f"K{b % 2}"], 16 * (b // 2 + 1))
                        for nt in range(2):
                            for g in range(2):
                                key = ("KbT", b, nt, g)
                                ps = bk.begin(pe, key, 4 + 2 * nt + g).rearrange("p (c t) -> p c t", c=4)
                                for c in range(4):
                                    k = 4 * g + c
                                    ins = pe.transpose(ps[:, c, :], Kr[:, b % 2, nt, k * P:(k + 1) * P], ident)
                                bk.filled(ins, key)

                    scores(0)
                    for T in range(4):
                        t0, n = TILES[T]
                        if T < 3:
                            scores(T + 1)
                        else:
                            turn_keys(0)
                        pe.wait_ge(sig["P"], T + 1)
                        for hp in range(2):
                            ps = bk.begin(pe, ("pT", T, hp), 6 + hp).rearrange("p (a n t) -> p a n t", a=2, n=2)
                            for a in range(2):
                                for nt in range(2):
                                    ins = pe.transpose(ps[:, a, nt, :], Pm[:, 2 * hp + a, nt * P:(nt + 1) * P], ident)
                            bk.filled(ins, ("pT", T, hp))
                        for hp in range(2):
                            bk.given(pe, ("pT", T, hp))
                            ps = bk.begin(pe, ("pv", T, hp), hp).rearrange("p (c t) -> p c t", c=4)
                            for c in range(4):
                                h, col = 2 * hp + c // 2, (4 * hp + c) * P
                                for nt in range(2):
                                    ins = pe.matmul(ps[:, c, :], Vp[:, nt, col:col + P], pT[:, h, nt, :], start=(nt == 0), stop=(nt == 1))
                            bk.filled(ins, ("pv", T, hp))
                    ss = bk.begin(pe, ("ss",), 2)
                    pe.wait_ge(sig["qOwn"], NB)
                    for b in range(NB):
                        if b < NB - 1:
                            turn_keys(b + 1)
                        for nt in range(2):
                            for g in range(2):
                                bk.given(pe, ("KbT", b, nt, g))
                        for h in range(H):
                            for c in range(2):
                                ins = pe.matmul(ss[h * NS:h * NS + NS, 0:NMEM], qOwn[:, b, 2 * h + c, :], KbT[b % 2][:, 2 * h + c, :],
                                                start=(b == 0 and c == 0), stop=(b == NB - 1 and c == 1), skip_group_check=True)
                        if b == NB - 1:
                            bk.filled(ins, ("ss",))
                        else:
                            sig.up(ins, "KbTread")
                    pe.wait_ge(sig["P"], 5)
                    ps = bk.begin(pe, ("pTs",), 4)
                    for nt in range(2):
                        ins = pe.transpose(ps[:, nt * P:(nt + 1) * P], Ps[:, nt * P:(nt + 1) * P], ident)
                    bk.filled(ins, ("pTs",))
                    for half in range(2):
                        bk.begin(pe, ("pvs", half), 5 + half)
                    for b in range(NB):
                        pe.wait_ge(sig[f"V{b % 4}"], 16 * (b // 4 + 1))
                        pe.wait_ge(sig["pOwn"], b + 1)
                        for half in range(2):
                            for nt in range(2):
                                ins = pe.matmul(psum[:, 5 + half, :], pOwn[:, b, nt, :], V_SLOTS[b % 4][:, nt, half * W512:half * W512 + W512],
                                                start=(b == 0 and nt == 0), stop=(b == NB - 1 and nt == 1))
                            if b == NB - 1:
                                bk.filled(ins, ("pvs", half))
                        if b < NB - 1:
                            sig.up(ins, "Vread")
                    for hp in range(2):
                        bk.given(pe, ("pv", 3, hp))
                    for half in range(2):
                        bk.given(pe, ("pvs", half))
                        ps = bk.begin(pe, ("pvT", half), 5 + half).rearrange("p (c t) -> p c t", c=4)
                        for c in range(4):
                            ins = pe.transpose(ps[:, c, :], pvs[:, half, c * P:(c + 1) * P], ident)
                        bk.filled(ins, ("pvT", half))
                    for half in range(2):
                        bk.given(pe, ("pvT", half))
                    project_tensor(pe, "wo", [aT[:, c, :] for c in range(KC)], (15, 16), 1)
                    turn_x_tensor(pe, bk, sig, 1, 3, (4, 5))
                    turn_x_tensor(pe, bk, sig, 1, 4, (4, 5))

                @block.vector
                def _(v):
                    v.wait_ge(sig["xres"], 32)
                    for T in range(5):
                        for half in range(2):
                            residual(v, ("wout", T, half), T, half)
                        ln_vector(v, sig, 0, T)
                    def turned_keys(b):
                        if b >= 2:
                            v.wait_ge(sig["KbTread"], b - 1)
                        for g in range(2):
                            ps = bk.take(v, ("KbT", b, 0, g)).rearrange("p (c t) -> p c t", c=4)
                            bk.give(v.tensor_copy(KbT[b % 2][:, 4 * g:4 * g + 4, 0:P], ps), ("KbT", b, 0, g))

                    for T in range(4):
                        for hp in range(2):
                            ps = bk.take(v, ("s", T, hp)).rearrange("p (a n) -> p a n", a=2)
                            if T and hp == 0:
                                v.wait_ge(sig["P"], T)
                            sig.up(v.tensor_reduce(mx[:, 2 * hp:2 * hp + 2], ps, AX.X, ALU.max, negate=True), "max")
                        v.wait_ge(sig["exp"], H * (T + 1))
                        after(v, v.reciprocal(inv, sums), "v")
                        sig.up(v.tensor_tensor(Pm, Pm, inv.unsqueeze(2).broadcast_to([P, H, NMEM]), ALU.mult), "P")
                        if T == 3:
                            turned_keys(0)
                        for hp in range(2):
                            ps = bk.take(v, ("pT", T, hp))
                            bk.give(v.tensor_copy(pT[:, 2 * hp:2 * hp + 2].rearrange("p a n t -> p (a n t)"), ps), ("pT", T, hp))
                    for b in range(1, NB):
                        turned_keys(b)
                    ps = bk.take(v, ("ss",))
                    sig.up(v.tensor_reduce(mx[:, 0:1], ps[:, 0:256], AX.X, ALU.max, negate=True), "max")
                    v.wait_ge(sig["exp"], 17)
                    after(v, v.reciprocal(inv[:, 0:1], sums[:, 0:1]), "v")
                    sig.up(v.tensor_scalar(Ps, Ps, inv[:, 0:1], None, ALU.mult), "P")
                    v.wait_ge(sig["pOwn0"], 1)
                    ps = bk.take(v, ("pTs",))
                    pT_ps = ps[:, 0:256].rearrange("p (n h b t) -> p n h b t", n=2, h=H, b=NB)
                    for b in range(NB):
                        ins = v.tensor_copy(pOwn[:, b].rearrange("p n (h b t) -> p n h b t", h=H, b=NB)[:, :, :, b, :], pT_ps[:, :, :, b, :])
                        if b < NB - 1:
                            sig.up(ins, "pOwn")
                    bk.give(ins, ("pTs",))
                    bk.given(v, ("pTs",))
                    sig.up(v.memset(sm[:, 80:81], 0.0), "pOwn")
                    for T in range(5):
                        for half in range(2):
                            residual(v, ("wo", T, half), T, half)
                        ln_vector(v, sig, 1, T)

                @block.scalar
                def _(s):
                    act = s.activation

                    def turned_keys(b):
                        if b >= 2:
                            s.wait_ge(sig["KbTread"], b - 1)
                        for g in range(2):
                            ps = bk.take(s, ("KbT", b, 1, g)).rearrange("p (c t) -> p c t", c=4)
                            bk.give(act(KbT[b % 2][:, 4 * g:4 * g + 4, P:2 * P], ps, ACT.Copy), ("KbT", b, 1, g))

                    for T in range(5):
                        ln_scalar(s, sig, 0, T)
                        if T >= 2:
                            turn_x_scalar(s, bk, sig, 0, T - 2)
                    for nt in range(2):
                        for g in range(2):
                            ps = bk.take(s, ("memT", nt, g)).rearrange("p (c t) -> p c t", c=4)
                            bk.give(act(memT[:, 4 * g:4 * g + 4, nt * P:(nt + 1) * P], ps, ACT.Copy), ("memT", nt, g))
                    for s_ in range(4):
                        dst = kpt if s_ < 2 else Vp
                        for nt in range(2):
                            ps = bk.take(s, ("kv", s_, nt))
                            bk.give(act(dst[:, nt, (s_ % 2) * W512:(s_ % 2) * W512 + W512], ps, ACT.Copy), ("kv", s_, nt))
                        if s_ < 2:
                            turn_x_scalar(s, bk, sig, 0, 3 + s_)
                        if s_ == 2:
                            for nt in range(2):
                                for g in range(2):
                                    ps = bk.take(s, ("KpT", nt, g)).rearrange("p (c t) -> p c t", c=4)
                                    bk.give(act(KpT[:, 4 * g:4 * g + 4, nt * P:(nt + 1) * P], ps, ACT.Copy), ("KpT", nt, g))
                    for f in range(KC):
                        for part, c in HALVES:
                            ps = bk.take(s, ("q", f, part))
                            bk.give(act(qT[:, f, c], ps[:, 0:c.stop - c.start], ACT.Copy, scale=XSCALE), ("q", f, part))
                    for T in range(4):
                        t0, n = TILES[T]
                        if T:
                            for hp in range(2):
                                bk.take(s, ("pT", T - 1, hp))
                        for hp in range(2):
                            s.wait_ge(sig["max"], 2 * T + hp + 1)
                            ps = bk.take(s, ("s", T, hp)).rearrange("p (a n) -> p a n", a=2)
                            for a in range(2):
                                h = 2 * hp + a
                                ins = act(Pm[:, h, :], ps[:, a, :], ACT.Exp, bias=mx[:, h:h + 1], accum_out=sums[:, h:h + 1])
                                if a == 0:
                                    sig.up(ins, "exp")
                            bk.give(ins, ("s", T, hp))
                            bk.given(s, ("s", T, hp))
                            sig.up(s.copy(sm[:, 86:87], const("eps")[:, 0:1]), "exp")
                        if T == 3:
                            turned_keys(0)
                        for hp in range(2):
                            ps = bk.take(s, ("pv", T, hp)).rearrange("p (c t) -> p c t", c=4)
                            bk.give(act(aT[:, 4 * hp:4 * hp + 4, t0:t0 + n], ps, ACT.Copy), ("pv", T, hp))
                    for b in range(1, NB):
                        turned_keys(b)
                    s.wait_ge(sig["max"], 9)
                    ps = bk.take(s, ("ss",))
                    bk.give(act(Ps, ps[:, 0:256], ACT.Exp, bias=mx[:, 0:1], accum_out=sums[:, 0:1]), ("ss",))
                    bk.given(s, ("ss",))
                    sig.up(s.copy(sm[:, 86:87], const("eps")[:, 0:1]), "exp")
                    for half in range(2):
                        ps = bk.take(s, ("pvs", half))
                        bk.give(act(pvs[:, half, :], ps, ACT.Copy), ("pvs", half))
                    for half in range(2):
                        ps = bk.take(s, ("pvT", half)).rearrange("p (c h t) -> p c h t", c=4, h=H)
                        for a in range(2):
                            h = 2 * half + a
                            ins = act(aT[:, 2 * h:2 * h + 2, SEQ:], ps[:, 2 * a:2 * a + 2, h, :], ACT.Copy)
                        bk.give(ins, ("pvT", half))
                    for T in range(5):
                        ln_scalar(s, sig, 1, T)
                        if T >= 2:
                            turn_x_scalar(s, bk, sig, 1, T - 2)
                    for T in (3, 4):
                        turn_x_scalar(s, bk, sig, 1, T)

                @block.gpsimd
                def _(g):
                    for half in range(2):
                        bk.given(g, ("q", KC - 1, half))
                    after(g, g.memset(qOwn, 0.0), "g")
                    for b in range(NB):
                        ins = g.tensor_copy(qOwn[:, b, :, TS * b:TS * b + TS], qT[:, :, SEQ + TS * b:SEQ + TS * b + TS])
                        after(g, ins, "qOwn")
                    after(g, g.memset(pOwn, 0.0), "pOwn0")

                @block.sync
                def _(sp):
                    sp.dma_start(xk[:, 0:4, :], yp).then_inc(sig["xres"], 16)
                    sp.dma_start(xk[:NS, 4, :], ys).then_inc(sig["xres"], 16)
                    sp.wait_ge(sig["out1"], 16 * len(N_OUT1))
                    ln_params(sp, sig, A["ln1_g"][bass.ds(l, 1)].rearrange("a n -> (a n)"), A["ln1_b"][bass.ds(l, 1)].rearrange("a n -> (a n)"))
                    sp.dma_start(mems, A["mem_prompt"].rearrange("a (t p) d -> p (a t) d", p=P)).then_inc(sig["mem"], 16)
                    out_slab(sp, 9)
                    out_slab(sp, 10)

                    def kv_load(name, dst, b, s_):
                        sp.dma_start(dst[:, b % 2], A[name][bass.ds(l, 1), b].rearrange("a (t p) h d -> p (a t) (h d)", p=P)).then_inc(sig[f"{s_}{b % 2}"], 16)

                    def v_load(b):
                        sp.dma_start(V_SLOTS[b % 4], A["cache_mem_v"][bass.ds(l, 1), b].rearrange("a (t p) h d -> p (a t) (h d)", p=P)
                                     ).then_inc(sig[f"V{b % 4}"], 16)

                    v_load(0)
                    v_load(1)
                    out_slab(sp, 11)
                    out_slab(sp, 12)
                    for nt in range(2):
                        for g in range(2):
                            bk.take(sp, ("memT", nt, g))
                    kv_load("cache_mem_k", Kr, 0, "K")
                    kv_load("cache_mem_k", Kr, 1, "K")
                    sp.wait_ge(sig["ln_done"], 5)
                    ln_params(sp, sig, A["ln2_g"][bass.ds(l, 1)].rearrange("a n -> (a n)"), A["ln2_b"][bass.ds(l, 1)].rearrange("a n -> (a n)"))
                    for nt in range(2):
                        bk.given(sp, ("kv", 1, nt))
                    sp.dma_start(O["p_mem_k"][bass.ds(l, 1)].rearrange("a b (t p) h d -> p (a b t) (h d)", p=P), kpt).then_inc(sig["memout"], 16)
                    out_slab(sp, 13)
                    out_slab(sp, 14)
                    for nt in range(2):
                        bk.given(sp, ("kv", 3, nt))
                    sp.dma_start(O["p_mem_v"][bass.ds(l, 1)].rearrange("a b (t p) h d -> p (a b t) (h d)", p=P), Vp).then_inc(sig["memout"], 16)
                    out_slab(sp, 15)
                    out_slab(sp, 16)
                    for b in range(2, NB):
                        for nt in range(2):
                            for g in range(2):
                                bk.take(sp, ("KbT", b - 2, nt, g))
                        kv_load("cache_mem_k", Kr, b, "K")
                    for b in range(2, NB):
                        if b < 4:
                            for nt in range(2):
                                for g in range(2):
                                    bk.take(sp, ("KbT", NB - 4 + b, nt, g))
                        else:
                            sp.wait_ge(sig["Vread"], b - 3)
                        v_load(b)
                    sp.wait_ge(sig["memout"], 32)
                    out_slab(sp, 17)
                    out_slab(sp, 18)

            hT = cols(big, 0, FC, NT)
            yT = [cols(tmp, 2048 + 2 * NT * i, 2, NT) for i in range(2)]
            with nc.Block() as block:

                @block.tensor
                def _(pe):
                    def turn_down(q, pair):
                        done = HALVES[0 if pair == 0 else 1][0]
                        for i in range(2):
                            for half in range(done + 1):
                                bk.given(pe, ("down", q, i, half))
                        ps = bk.begin(pe, ("dt", q, pair), 4 * (q % 2) + (0, 2, 1)[pair]).rearrange("p (a c) -> p a c", a=2)
                        for T in range(2 * pair, min(2 * pair + 2, 5)):
                            t0, n = TILES[T]
                            for i in range(2):
                                ins = pe.transpose(ps[:n, T % 2, i * P:(i + 1) * P], yT[q % 2][:, i, t0:t0 + n], ident)
                        bk.filled(ins, ("dt", q, pair))

                    for g in range(2):
                        bk.given(pe, ("xT", 1, 4, g))
                    for n in range(8):
                        w = slab_pe(pe, 17 + n)
                        for i in range(4):
                            f = 4 * n + i
                            x_product(pe, ("up", f), f % 2, [w[:, k, i * P:(i + 1) * P] for k in range(KC)])
                    for q in range(4):
                        w = [None, None]
                        halves = [(0, 1)] if q < 3 else [(0,), (1,)]
                        for hs in halves:
                            for i, r in ([(0, 0), (1, 0), (0, 1), (1, 1)] if q < 3 else [(0, 0), (0, 1), (1, 0), (1, 1)]):
                                if w[r] is None:
                                    slab_pe(pe, 25 + 2 * q + r)
                                    w[r] = cols(ring, ((25 + 2 * q + r) % 2) * KC * W512, 2 * KC, W256)
                                    if q == 0:
                                        pe.wait_ge(sig["h"], 2 * KC * (r + 1))
                                for half in hs:
                                    key, c = ("down", q, i, half), HALVES[half][1]
                                    if r == 0:
                                        bk.begin(pe, key, 4 * (q % 2) + 2 * i + half)
                                    ps = psum[:, bk.turn[key][0], :c.stop - c.start]
                                    for k in range(2 * KC):
                                        ins = pe.matmul(ps, w[r][:, k, i * P:(i + 1) * P], hT[:, 2 * KC * r + k, c],
                                                        start=(r == 0 and k == 0), stop=(r == 1 and k == 2 * KC - 1))
                                    if r == 1:
                                        bk.filled(ins, key)
                                if q < 3 and (i, r) == (1, 0):
                                    sig.up(ins, "downread")
                                    if q:
                                        for pair in range(3):
                                            turn_down(q - 1, pair)
                                if q == 3 and hs == (1,) and (i, r) == (1, 0):
                                    sig.up(ins, "downread")
                                if q == 3 and hs == (0,) and (i, r) == (0, 0):
                                    for pair in range(3):
                                        turn_down(2, pair)
                                if q == 3 and hs == (1,) and (i, r) == (0, 1):
                                    turn_down(3, 0)
                    for T in range(2):
                        turn_x_tensor(pe, bk, sig, 2, T, (2, 3))
                    for pair in (1, 2):
                        turn_down(3, pair)
                    for T in (2, 3, 4):
                        turn_x_tensor(pe, bk, sig, 2, T, (2, 3))

                @block.vector
                def _(v):
                    for q in range(4):
                        for T in range(5):
                            n = TILES[T][1]
                            x = xk[:n, T, q * W256:(q + 1) * W256]
                            ps = bk.take(v, ("dt", q, T // 2))
                            ins = v.scalar_tensor_tensor(x, x, ALPHA, ps[:n, (T % 2) * W256:(T % 2) * W256 + W256], ALU.mult, ALU.add)
                            if T % 2 or T == 4:
                                bk.give(ins, ("dt", q, T // 2))
                            if q == 3:
                                if T % 2 or T == 4:
                                    bk.given(v, ("dt", q, T // 2))
                                else:
                                    v.wait_ge(sig["v"], sig.up(ins, "v"))
                                ln_vector(v, sig, 2, T)

                @block.scalar
                def _(s):
                    for f in range(FC):
                        for part, c in HALVES:
                            ps = bk.take(s, ("up", f, part))
                            bk.give(s.activation(hT[:, f, c], ps[:, 0:c.stop - c.start], ACT.Relu), ("up", f, part))
                            bk.given(s, ("up", f, part))
                        sig.up(s.activation(hT[:, f, :], hT[:, f, :], ACT.Square), "h")
                    def down_half(q, i, half):
                        c = HALVES[half][1]
                        if q >= 2 and i == 0 and half == 0:
                            for pair in range(3):
                                bk.take(s, ("dt", q - 2, pair))
                        ps = bk.take(s, ("down", q, i, half))
                        bk.give(s.activation(yT[q % 2][:, i, c], ps[:, :c.stop - c.start], ACT.Copy), ("down", q, i, half))

                    for q in range(3):
                        for i in range(2):
                            for half in range(2):
                                down_half(q, i, half)
                    down_half(3, 0, 0)
                    down_half(3, 1, 0)
                    down_half(3, 0, 1)
                    ln_scalar(s, sig, 2, 0)
                    ln_scalar(s, sig, 2, 1)
                    down_half(3, 1, 1)
                    turn_x_scalar(s, bk, sig, 2, 0)
                    turn_x_scalar(s, bk, sig, 2, 1)
                    ln_scalar(s, sig, 2, 2)
                    ln_scalar(s, sig, 2, 3)
                    turn_x_scalar(s, bk, sig, 2, 2)
                    ln_scalar(s, sig, 2, 4)
                    turn_x_scalar(s, bk, sig, 2, 3)
                    turn_x_scalar(s, bk, sig, 2, 4)

                @block.sync
                def _(sp):
                    ln_params(sp, sig, A["ln3_g"][bass.ds(l, 1)].rearrange("a n -> (a n)"), A["ln3_b"][bass.ds(l, 1)].rearrange("a n -> (a n)"))
                    for n in range(19, 33):
                        out_slab(sp, n)
                    slab_read(sp, 31)
                    first_slab(sp, 1, 1 - l, sig["next"])
                    slab_read(sp, 32)
                    first_slab(sp, 0, 1 - l, sig["next"])
                    sp.wait_ge(sig["next"], 32)


            nc.multi_engine_barrier(engines, sems_to_clear=sig.numbers())

        with nc.Block() as block:
            @block.sync
            def _(sp):
                sp.dma_start(yp, xk[:, 0:4, :]).then_inc(s0["out"], 16)
                sp.dma_start(ys, xk[:NS, 4, :]).then_inc(s0["out"], 16)
                sp.wait_ge(s0["out"], 32)


_OUTS = [("y_prompt", (1, SEQ, D)), ("y_sample", (NB, TS, D)),
         ("p_C", (DEPTH, 1, H, HD, HD)), ("p_n", (DEPTH, 1, H, HD)), ("p_m", (DEPTH, 1, H)),
         ("p_R", (DEPTH, 1, H, HD, HD)), ("p_h", (DEPTH, 1, 256)), ("p_conv", (DEPTH, 1, 3, 256)),
         ("p_S", (DEPTH, 1, H, HD, HD)), ("p_shift", (DEPTH, 1, D)),
         ("p_mem_k", (DEPTH, 1, NMEM, H, 256)), ("p_mem_v", (DEPTH, 1, NMEM, H, 256)),
         ("s_C", (DEPTH, NB, H, HD, HD)), ("s_n", (DEPTH, NB, H, HD)), ("s_m", (DEPTH, NB, H)),
         ("s_R", (DEPTH, NB, H, HD, HD)), ("s_h", (DEPTH, NB, 256)), ("s_conv", (DEPTH, NB, 3, 256)),
         ("s_S", (DEPTH, NB, H, HD, HD)), ("s_shift", (DEPTH, NB, D))]


def kernel(**inputs):
    import numpy as np
    import concourse.bacc as bacc
    from concourse.bass_utils import run_bass_kernel_spmd

    nc = bacc.Bacc("TRN2", target_bir_lowering=False, num_devices=1)
    arrays, ins, outs = {}, {}, {}
    for name, a in inputs.items():
        a = np.ascontiguousarray(a)
        arrays["in_" + name] = a
        ins[name] = nc.dram_tensor("in_" + name, a.shape, F32, kind="ExternalInput").ap()
    table, where = constants()
    arrays["in_table"] = table
    t = nc.dram_tensor("in_table", table.shape, F32, kind="ExternalInput").ap()
    for name, shape in _OUTS:
        outs[name] = nc.dram_tensor("out_" + name, shape, F32, kind="ExternalOutput").ap()
    build(nc, ins, outs, t, where)
    r = run_bass_kernel_spmd(nc, [arrays], core_ids=[0])
    return tuple(r.results[0]["out_" + name] for name, _ in _OUTS)
```
